# Optimizing a Trainium2 kernel written in Bass

```python
import math
import jax, jax.numpy as jnp
from jax import lax
import numpy as np

D_MODEL = 1024
BATCH = 1
SEQ = 1024
DEPTH = 2

RMS_EPS = 1e-5
CONV_WIDTH = 4
MLSTM_HEADS = 4
MLSTM_DH = D_MODEL // (2 * MLSTM_HEADS)
MLSTM_W = MLSTM_HEADS * MLSTM_DH
MLSTM_CHUNK = 64
DIFF_HEADS = 4
DIFF_DH = D_MODEL // (4 * DIFF_HEADS)
DIFF_DV = 2 * DIFF_DH
DIFF_QK_W = DIFF_HEADS * DIFF_DH
DIFF_W = DIFF_HEADS * DIFF_DV
Q_BLOCK = 128
AB_SPLITS = (2 * MLSTM_W, MLSTM_W, MLSTM_W, MLSTM_HEADS, MLSTM_HEADS,
             2 * DIFF_QK_W, 2 * DIFF_QK_W, DIFF_W)
AB_IN = sum(AB_SPLITS)
AB_OUT_IN = MLSTM_W + DIFF_W
SSM_INNER = 2 * D_MODEL
SSM_HEADDIM = 64
SSM_HEADS = SSM_INNER // SSM_HEADDIM
SSM_STATE = 128
SSM_GROUPS = 8
SSM_HPG = SSM_HEADS // SSM_GROUPS
SSM_CONV_CH = SSM_INNER + 2 * SSM_GROUPS * SSM_STATE
SSM_IN = SSM_INNER + SSM_CONV_CH + SSM_HEADS
SSM_CHUNK = 64
D_FF = 4 * D_MODEL

kernel_name = "hybrid_mlstm_diffattn_mamba2"

def _split(a, sizes):
    idx = np.cumsum(np.array(sizes))[:-1].tolist()
    return jnp.split(a, idx, axis=-1)

def rmsnorm(x, g):
    xf = x.astype(jnp.float32)
    y = xf * lax.rsqrt(jnp.mean(xf * xf, axis=-1, keepdims=True) + RMS_EPS)
    return (y * g.astype(jnp.float32)).astype(x.dtype)

def causal_dwconv(x, w, b):
    y = lax.conv_general_dilated(x, w[:, None, :], window_strides=(1,),
                                 padding=[(CONV_WIDTH - 1, 0)],
                                 dimension_numbers=('NWC', 'WIO', 'NWC'),
                                 feature_group_count=x.shape[-1])
    return y + b

def alibi_slopes(n):
    return jnp.exp2(-8.0 * jnp.arange(1, n + 1, dtype=jnp.float32) / n)

def mlstm_chunkwise(q, k, v, i_pre, f_pre):
    bsz, nh, T, dh = q.shape
    L = MLSTM_CHUNK
    nc = T // L
    f32 = jnp.float32
    q = q.astype(f32).reshape(bsz, nh, nc, L, dh)
    k = (k.astype(f32) * dh ** -0.5).reshape(bsz, nh, nc, L, dh)
    v = v.astype(f32).reshape(bsz, nh, nc, L, dh)
    ig = i_pre.astype(f32).reshape(bsz, nh, nc, L)
    lf = jax.nn.log_sigmoid(f_pre.astype(f32)).reshape(bsz, nh, nc, L)
    b = jnp.cumsum(lf, axis=-1)
    b_last = b[..., -1]
    a = b_last[..., None] - b + ig
    m_loc = jnp.max(a, axis=-1)
    w = jnp.exp(a - m_loc[..., None])
    C_loc = jnp.einsum('bhcs,bhcsd,bhcse->bhcde', w, k, v)
    n_loc = jnp.einsum('bhcs,bhcsd->bhcd', w, k)

    def step(carry, inp):
        C, n, m = carry
        Cl, nl, ml, bl = inp
        m_new = jnp.maximum(bl + m, ml)
        sp = jnp.exp(bl + m - m_new)
        sl = jnp.exp(ml - m_new)
        C_new = sp[..., None, None] * C + sl[..., None, None] * Cl
        n_new = sp[..., None] * n + sl[..., None] * nl
        return (C_new, n_new, m_new), (C, n, m)

    init = (jnp.zeros((bsz, nh, dh, dh), f32), jnp.zeros((bsz, nh, dh), f32),
            jnp.zeros((bsz, nh), f32))
    xs = (jnp.moveaxis(C_loc, 2, 0), jnp.moveaxis(n_loc, 2, 0),
          jnp.moveaxis(m_loc, 2, 0), jnp.moveaxis(b_last, 2, 0))
    _, (C0, n0, m0) = lax.scan(step, init, xs)
    C0 = jnp.moveaxis(C0, 0, 2)
    n0 = jnp.moveaxis(n0, 0, 2)
    m0 = jnp.moveaxis(m0, 0, 2)
    causal = jnp.tril(jnp.ones((L, L), dtype=bool))
    logw = jnp.where(causal, b[..., :, None] - b[..., None, :] + ig[..., None, :], -jnp.inf)
    m_inter = b + m0[..., None]
    m_t = jnp.maximum(m_inter, jnp.max(logw, axis=-1))
    wts = jnp.exp(logw - m_t[..., None]) * jnp.einsum('bhctd,bhcsd->bhcts', q, k)
    s_inter = jnp.exp(m_inter - m_t)
    num = (jnp.einsum('bhcts,bhcse->bhcte', wts, v)
           + s_inter[..., None] * jnp.einsum('bhctd,bhcde->bhcte', q, C0))
    den = jnp.sum(wts, axis=-1) + s_inter * jnp.einsum('bhctd,bhcd->bhct', q, n0)
    h = num / jnp.maximum(jnp.abs(den), jnp.exp(-m_t))[..., None]
    return h.reshape(bsz, nh, T, dh)

def diff_attention(q, k, v, lam, slopes):
    _, bsz, nh, T, d = q.shape
    f32 = jnp.float32
    nb = T // Q_BLOCK
    q_blocks = jnp.moveaxis((q.astype(f32) * d ** -0.5).reshape(2, bsz, nh, nb, Q_BLOCK, d), 3, 0)
    kf = k.astype(f32)
    vf = v.astype(f32)
    starts = jnp.arange(nb, dtype=jnp.int32) * Q_BLOCK
    kpos = jnp.arange(T, dtype=jnp.int32)

    def one_block(args):
        qb, start = args
        dist = (start + jnp.arange(Q_BLOCK, dtype=jnp.int32))[:, None] - kpos[None, :]
        s = (jnp.einsum('mbhqd,mbhkd->mbhqk', qb, kf)
             - slopes[:, None, None] * dist.astype(f32))
        s = jnp.where(dist >= 0, s, -jnp.inf)
        p = jax.nn.softmax(s, axis=-1)
        return jnp.einsum('bhqk,bhke->bhqe', p[0] - lam * p[1], vf)

    out = lax.map(one_block, (q_blocks, starts))
    return jnp.moveaxis(out, 0, 2).reshape(bsz, nh, T, v.shape[-1])

def mlstm_diff_mixer(h, w_in, conv_w, conv_b, i_bias, f_bias, mnorm_g,
                     lq1, lk1, lq2, lk2, dnorm_g, w_out, lam_init):
    bsz, T, _ = h.shape
    mqk, mv, mo, mi, mf, dq, dk, dv = _split(h @ w_in, AB_SPLITS)
    mqk = jax.nn.silu(causal_dwconv(mqk, conv_w, conv_b))
    mq, mk = jnp.split(mqk, 2, axis=-1)
    heads = lambda t: t.reshape(bsz, T, MLSTM_HEADS, MLSTM_DH).transpose(0, 2, 1, 3)
    hm = mlstm_chunkwise(heads(mq), heads(mk), heads(mv),
                         (mi + i_bias).transpose(0, 2, 1), (mf + f_bias).transpose(0, 2, 1))
    hm = rmsnorm(hm.transpose(0, 2, 1, 3), mnorm_g.reshape(MLSTM_HEADS, MLSTM_DH))
    hm = (jax.nn.sigmoid(mo.astype(jnp.float32)) * hm.reshape(bsz, T, MLSTM_W)).astype(h.dtype)
    qk_heads = lambda t: t.reshape(bsz, T, DIFF_HEADS, 2, DIFF_DH).transpose(3, 0, 2, 1, 4)
    f32 = jnp.float32
    lam = (jnp.exp(jnp.sum(lq1.astype(f32) * lk1.astype(f32)))
           - jnp.exp(jnp.sum(lq2.astype(f32) * lk2.astype(f32))) + lam_init)
    hd = diff_attention(qk_heads(dq), qk_heads(dk),
                        dv.reshape(bsz, T, DIFF_HEADS, DIFF_DV).transpose(0, 2, 1, 3),
                        lam, alibi_slopes(DIFF_HEADS))
    hd = rmsnorm(hd.transpose(0, 2, 1, 3), dnorm_g.reshape(DIFF_HEADS, DIFF_DV)) * (1.0 - lam_init)
    hd = hd.reshape(bsz, T, DIFF_W).astype(h.dtype)
    return jnp.concatenate([hm, hd], axis=-1) @ w_out

def ssd_chunked(x, dt, A, Bm, Cm):
    bsz, T, G, R, P = x.shape
    N = Bm.shape[-1]
    L = SSM_CHUNK
    nc = T // L
    f32 = jnp.float32
    xdt = (x.astype(f32) * dt[..., None]).reshape(bsz, nc, L, G, R, P)
    a_cs = jnp.cumsum((dt * A).reshape(bsz, nc, L, G, R), axis=2)
    Bc = Bm.astype(f32).reshape(bsz, nc, L, G, N)
    Cc = Cm.astype(f32).reshape(bsz, nc, L, G, N)
    causal = jnp.tril(jnp.ones((L, L), dtype=bool))[:, :, None, None]
    seg = a_cs[:, :, :, None] - a_cs[:, :, None, :]
    decay = jnp.exp(jnp.where(causal, seg, -jnp.inf))
    cb = jnp.einsum('bctgn,bcsgn->bctsg', Cc, Bc)
    y_diag = jnp.einsum('bctsg,bctsgr,bcsgrp->bctgrp', cb, decay, xdt)

    def step(S, inp):
        Bk, Ck, xk, ak = inp
        y_off = jnp.einsum('blgn,bgrpn,blgr->blgrp', Ck, S, jnp.exp(ak))
        S_loc = jnp.einsum('blgn,blgr,blgrp->bgrpn', Bk, jnp.exp(ak[:, -1:] - ak), xk)
        S = jnp.exp(ak[:, -1])[..., None, None] * S + S_loc
        return S, y_off

    S0 = jnp.zeros((bsz, G, R, P, N), f32)
    xs = (jnp.moveaxis(Bc, 1, 0), jnp.moveaxis(Cc, 1, 0),
          jnp.moveaxis(xdt, 1, 0), jnp.moveaxis(a_cs, 1, 0))
    _, y_off = lax.scan(step, S0, xs)
    y = y_diag + jnp.moveaxis(y_off, 0, 1)
    return y.reshape(bsz, T, G, R, P)

def mamba2_mixer(h, w_in, conv_w, conv_b, dt_bias, a_log, d_skip, norm_g, w_out):
    bsz, T, _ = h.shape
    f32 = jnp.float32
    z, xbc, dt = _split(h @ w_in, (SSM_INNER, SSM_CONV_CH, SSM_HEADS))
    xbc = jax.nn.silu(causal_dwconv(xbc, conv_w, conv_b))
    xs, Bm, Cm = _split(xbc, (SSM_INNER, SSM_GROUPS * SSM_STATE, SSM_GROUPS * SSM_STATE))
    xs = xs.reshape(bsz, T, SSM_GROUPS, SSM_HPG, SSM_HEADDIM)
    dt = jax.nn.softplus(dt.astype(f32) + dt_bias.astype(f32)).reshape(bsz, T, SSM_GROUPS, SSM_HPG)
    A = -jnp.exp(a_log.astype(f32)).reshape(SSM_GROUPS, SSM_HPG)
    y = ssd_chunked(xs, dt, A, Bm.reshape(bsz, T, SSM_GROUPS, SSM_STATE),
                    Cm.reshape(bsz, T, SSM_GROUPS, SSM_STATE))
    y = y + d_skip.astype(f32).reshape(SSM_GROUPS, SSM_HPG, 1) * xs.astype(f32)
    y = y.reshape(bsz, T, SSM_INNER) * jax.nn.silu(z.astype(f32))
    y = rmsnorm(y.reshape(bsz, T, SSM_GROUPS, SSM_INNER // SSM_GROUPS),
                norm_g.reshape(SSM_GROUPS, SSM_INNER // SSM_GROUPS))
    return y.reshape(bsz, T, SSM_INNER).astype(h.dtype) @ w_out

def squared_relu_mlp(h, w1, w2):
    return jnp.square(jax.nn.relu(h @ w1)) @ w2

def setup_inputs(seed: int = 0) -> dict:
    key = jax.random.key(seed)
    ks = iter(jax.random.split(key, 40))
    f32 = jnp.float32
    nrm = lambda shape, scale: scale * jax.random.normal(next(ks), shape, f32)
    ne = (DEPTH + 1) // 2
    no = DEPTH // 2
    dt0 = jnp.exp(jax.random.uniform(next(ks), (no, SSM_HEADS), f32,
                                     minval=math.log(1e-3), maxval=math.log(1e-1)))
    return {
        'x': nrm((BATCH, SEQ, D_MODEL), 1.0),
        'norm_mix_g': 1.0 + nrm((DEPTH, D_MODEL), 0.02),
        'norm_mlp_g': 1.0 + nrm((DEPTH, D_MODEL), 0.02),
        'ab_w_in': nrm((ne, D_MODEL, AB_IN), D_MODEL ** -0.5),
        'ab_conv_w': nrm((ne, CONV_WIDTH, 2 * MLSTM_W), CONV_WIDTH ** -0.5),
        'ab_conv_b': nrm((ne, 2 * MLSTM_W), 0.01),
        'ab_i_bias': nrm((ne, MLSTM_HEADS), 0.1),
        'ab_f_bias': jnp.linspace(3.0, 6.0, MLSTM_HEADS, dtype=f32)[None] + nrm((ne, MLSTM_HEADS), 0.1),
        'ab_mnorm_g': 1.0 + nrm((ne, MLSTM_W), 0.02),
        'ab_lam_q1': nrm((ne, DIFF_DH), 0.1),
        'ab_lam_k1': nrm((ne, DIFF_DH), 0.1),
        'ab_lam_q2': nrm((ne, DIFF_DH), 0.1),
        'ab_lam_k2': nrm((ne, DIFF_DH), 0.1),
        'ab_dnorm_g': 1.0 + nrm((ne, DIFF_W), 0.02),
        'ab_w_out': nrm((ne, AB_OUT_IN, D_MODEL), AB_OUT_IN ** -0.5),
        'ssm_w_in': nrm((no, D_MODEL, SSM_IN), D_MODEL ** -0.5),
        'ssm_conv_w': nrm((no, CONV_WIDTH, SSM_CONV_CH), CONV_WIDTH ** -0.5),
        'ssm_conv_b': nrm((no, SSM_CONV_CH), 0.01),
        'ssm_dt_bias': dt0 + jnp.log(-jnp.expm1(-dt0)),
        'ssm_a_log': jnp.log(jax.random.uniform(next(ks), (no, SSM_HEADS), f32, minval=1.0, maxval=16.0)),
        'ssm_d': 1.0 + nrm((no, SSM_HEADS), 0.1),
        'ssm_norm_g': 1.0 + nrm((no, SSM_INNER), 0.02),
        'ssm_w_out': nrm((no, SSM_INNER, D_MODEL), SSM_INNER ** -0.5),
        'mlp_w1': nrm((DEPTH, D_MODEL, D_FF), D_MODEL ** -0.5),
        'mlp_w2': nrm((DEPTH, D_FF, D_MODEL), D_FF ** -0.5),
        'final_g': 1.0 + nrm((D_MODEL,), 0.02),
    }

def reference(x, norm_mix_g, norm_mlp_g, ab_w_in, ab_conv_w, ab_conv_b, ab_i_bias,
              ab_f_bias, ab_mnorm_g, ab_lam_q1, ab_lam_k1, ab_lam_q2, ab_lam_k2,
              ab_dnorm_g, ab_w_out, ssm_w_in, ssm_conv_w, ssm_conv_b, ssm_dt_bias,
              ssm_a_log, ssm_d, ssm_norm_g, ssm_w_out, mlp_w1, mlp_w2, final_g):
    for i in range(DEPTH):
        j = i // 2
        h = rmsnorm(x, norm_mix_g[i])
        if i % 2 == 0:
            lam_init = 0.8 - 0.6 * math.exp(-0.3 * i)
            x = x + mlstm_diff_mixer(h, ab_w_in[j], ab_conv_w[j], ab_conv_b[j], ab_i_bias[j],
                                     ab_f_bias[j], ab_mnorm_g[j], ab_lam_q1[j], ab_lam_k1[j],
                                     ab_lam_q2[j], ab_lam_k2[j], ab_dnorm_g[j], ab_w_out[j],
                                     lam_init)
        else:
            x = x + mamba2_mixer(h, ssm_w_in[j], ssm_conv_w[j], ssm_conv_b[j], ssm_dt_bias[j],
                                 ssm_a_log[j], ssm_d[j], ssm_norm_g[j], ssm_w_out[j])
        x = x + squared_relu_mlp(rmsnorm(x, norm_mlp_g[i]), mlp_w1[i], mlp_w2[i])
    return rmsnorm(x, final_g)


_drawn_inputs = setup_inputs


def setup_inputs(seed=0):
    import zlib

    import numpy as np

    out = dict(_drawn_inputs(seed))
    spreads = {}
    factors = {'ab_conv_b': 8.0,
     'ab_i_bias': 64.0,
     'ab_mnorm_g': 72.888,
     'ab_lam_q1': 8.0,
     'ab_dnorm_g': 45.913,
     'ssm_conv_b': 8.0,
     'ssm_norm_g': 124.452,
     'final_g': 22.011,
     'norm_mlp_g': 5.944,
     'ab_lam_q2': 2.856}
    for name, (base, spread) in spreads.items():
        noise = np.random.default_rng([zlib.crc32(name.encode()), seed]).standard_normal(out[name].shape)
        drawn = base * np.exp(spread * noise) if base else spread * noise
        out[name] = __import__('jax').numpy.asarray(drawn.astype(out[name].dtype))
    for name, factor in factors.items():
        out[name] = (out[name] * factor).astype(out[name].dtype)
    return out
```

```python
from contextlib import ExitStack, contextmanager

import numpy as np

import concourse.bass as bass
from concourse import mybir

F32 = mybir.dt.float32
F32R = mybir.dt.float32r
ALU = mybir.AluOpType
ACT = mybir.ActivationFunctionType
AX = mybir.AxisListType

P = 128
HALF = 512
D = 1024
T = 1024
KD = D // P
NC = T // P
EPS = 1e-5
FF = 4 * D
FB = 4 * P
N_FB = FF // FB
MH, DH = 4, 128
AH, AD = 4, 64
G, HPG, SP_, NS = 8, 4, 64, 128
SH = G * HPG
INNER = SH * SP_
GW = HPG * SP_
NEG = -1.0e30
LEAST = -3.4e38
TINY = 1.0e-30
SLOPE = 0.25
LAM_INIT = 0.8 - 0.6


class Silent:

    def _take(self, *a, **k):
        return self

    dma_start = matmul = transpose = wait_ge = then_inc = sem_inc = _take
    activation = copy = tensor_copy = tensor_tensor = tensor_scalar = scalar_tensor_tensor = _take
    tensor_tensor_reduce = tensor_tensor_scan = tensor_reduce = reciprocal = memset = _take
    affine_select = drain = iota = _take


class Tally:

    def __init__(self, engine):
        self.e = engine
        self.base, self.rel, self.per, self.i = {}, {}, None, None

    def next(self, sem, by=1):
        key = sem.name
        self.rel[key] = self.rel.get(key, 0) + by
        value = self.base.get(key, 0) + self.rel[key]
        if self.i is not None:
            value = self.i * self.per[key] + value
        return value

    def skip(self, sem, by=1):
        self.rel[sem.name] = self.rel.get(sem.name, 0) + by

    def loop(self, n, body):
        engine, base = self.e, self.base
        for key, v in self.rel.items():
            base[key] = base.get(key, 0) + v
        self.rel, self.e = {}, Silent()
        body(0)
        self.per, self.rel, self.e = self.rel, {}, engine
        with engine.Fori(0, n) as i:
            self.i = i
            body(i)
        for key, v in self.per.items():
            base[key] = base.get(key, 0) + n * v
        self.rel, self.per, self.i = {}, None, None


def trunk(nc, x, norm_mix_g, norm_mlp_g, ab_w_in, ab_conv_w, ab_conv_b, ab_i_bias, ab_f_bias,
          ab_mnorm_g, ab_lam_q1, ab_lam_k1, ab_lam_q2, ab_lam_k2, ab_dnorm_g, ab_w_out, ssm_w_in,
          ssm_conv_w, ssm_conv_b, ssm_dt_bias, ssm_a_log, ssm_d, ssm_norm_g, ssm_w_out,
          mlp_w1, mlp_w2, final_g, out, phases=("ab", "mlp0", "ssm", "mlp1")):
    with ExitStack() as ctx:
        def sb(name, shape, dt=F32):
            return ctx.enter_context(nc.sbuf_tensor(name, shape, dt))

        def sem(name):
            return ctx.enter_context(nc.semaphore(name))

        X = sb("X", [P, KD, T])
        HH = sb("HH", [P, KD, T], F32R)
        HL = sb("HL", [P, KD, T], F32R)
        w_raw = sb("w_raw", [P, 2, T])
        w_hi = sb("w_hi", [P, 2, T], F32R)
        w_lo = sb("w_lo", [P, 2, T], F32R)
        ones = sb("ones", [P, P])
        ident = sb("ident", [P, P])
        R = sb("R", [P, T])
        gains = sb("gains", [P, 4, KD])
        eps_col = sb("eps_col", [P, 1])
        ss = sb("ss", [P, NC])
        rstd = sb("rstd", [P, NC])
        conv_w = sb("conv_w", [P, 4, 2 * MH])
        conv_b = sb("conv_b", [P, 2 * MH])
        gate_bias = sb("gate_bias", [36, 1])
        mnorm = sb("mnorm", [P, MH])
        dnorm = sb("dnorm", [P, AH])
        lam = sb("lam", [P, 3])
        step_cols = sb("step_cols", [P, 3, NC, SH])
        gate_cols = step_cols[:, 0, 0:3, :].rearrange("p q (c h) -> p q c h", c=NC)
        causal = sb("causal", [P, 1, P])
        m0 = sb("m0", [MH, NC])
        stat = sb("stat", [P, 6])
        den = sb("den", [P, 4, NC])
        n_all = sb("n_all", [P, NC])
        conv_in = sb("conv_in", [P, T + 4])
        z_hi = sb("z_hi", [P, 4, T], F32R)
        y_hi, y_lo = z_hi[:, 0:2, :], z_hi[:, 2:4, :]
        gate_hi, gate_lo = (z_hi[:, m, 0:KD * 36].rearrange("p (k n) -> p k n", k=KD) for m in range(2))
        ab_rows = nc.dram_tensor("ab_rows", [2, MH, T], F32).ap()
        sconv_w = sb("sconv_w", [P, 4, 2 * INNER // P])
        sconv_b = sb("sconv_b", [P, 2 * INNER // P])
        dt_bias = sb("dt_bias", [SH, 2])
        skip_d = sb("skip_d", [P, SH // 2])
        snorm = sb("snorm", [P, INNER // P])
        last_a = sb("last_a", [SH, NC])
        keep_a = sb("keep_a", [P, SH * NC])
        ssm_rows = nc.dram_tensor("ssm_rows", [2, SH, T], F32).ap()
        ssm_last = nc.dram_tensor("ssm_last", [SH, NC], F32).ap()
        ssm_at = phases.index("ssm") if "ssm" in phases else 0

        UNITS = 14
        with nc.sbuf_tensor("scratch", [P, UNITS * T], F32) as scratch:
            pass
        with nc.sbuf_tensor("below_z_lo", [P, (UNITS - 4) * T], F32), nc.sbuf_tensor("z_lo", [P, 4, T], F32R) as z_lo:
            pass

        def cut(k, n=1):
            return scratch[:, k * T:(k + n) * T]

        pair = [ctx.enter_context(nc.psum_tensor(f"pair{k}", [P, 2, HALF], F32)) for k in range(4)]

        w_loaded = [sem(f"w_loaded{s}") for s in range(2)]
        w_split = [sem(f"w_split{s}") for s in range(2)]
        unit_done = [sem(f"unit_done{s}") for s in range(2)]
        part_done = [sem(f"part_done{s}") for s in range(4)]
        pair_free = [sem(f"pair_free{s}") for s in range(4)]
        dve_done, act_done, pool_done = (sem(f"{n}_done") for n in ("dve", "act", "pool"))
        const_ready = sem("const_ready")
        small_loaded = sem("small_loaded")
        x_loaded = [sem(f"x_loaded{s}") for s in range(2)]
        turned_done = [sem(f"turned_done{s}") for s in range(2)]
        x_read = [sem(f"x_read{s}") for s in range(2)]
        x_ready = sem("x_ready")
        resid_ready = sem("resid_ready")
        high_ready = sem("high_ready")
        low_ready = sem("low_ready")
        sq_ready = sem("sq_ready")
        sq_used = sem("sq_used")
        sum_ready = sem("sum_ready")
        norm_sum = sem("norm_sum")
        r_ready = sem("r_ready")
        z_ready = sem("z_ready")
        z_high = sem("z_high")
        z_low = sem("z_low")
        begun = sem("begun")
        exp_free = [sem(f"exp_free{s}") for s in range(2)]
        exp_here = [sem(f"exp_here{s}") for s in range(2)]
        mix_free = [sem(f"mix_free{s}") for s in range(2)]
        mix_here = [sem(f"mix_here{s}") for s in range(2)]
        ab_small = sem("ab_small")
        ab_zeroed = sem("ab_zeroed")
        b_tok_ready = sem("b_tok_ready")
        b_turned = sem("b_turned")
        bc_ready = sem("bc_ready")
        cb_done = sem("cb_done")
        conv_ready = sem("conv_ready")
        decay_exp = sem("decay_exp")
        decay_ready = sem("decay_ready")
        dist_ready = sem("dist_ready")
        ea_ready = sem("ea_ready")
        exp_ready = sem("exp_ready")
        f_exp = sem("f_exp")
        f_log = sem("f_log")
        f_ready = sem("f_ready")
        gate_split = sem("gate_split")
        gates_done = sem("gates_done")
        gates_free = sem("gates_free")
        gates_here = sem("gates_here")
        h_ready = sem("h_ready")
        h_rstd = sem("h_rstd")
        h_squared = sem("h_squared")
        h_turned = sem("h_turned")
        hm_ready = sem("hm_ready")
        k_turned = sem("k_turned")
        keep_here = sem("keep_here")
        kw_ready = sem("kw_ready")
        lam_dots = sem("lam_dots")
        lam_exps = sem("lam_exps")
        max_ready = sem("max_ready")
        mix_ready = sem("mix_ready")
        mk_ready = sem("mk_ready")
        mo_ready = sem("mo_ready")
        mo_tanh = sem("mo_tanh")
        mv_ready = sem("mv_ready")
        num_ready = sem("num_ready")
        o_normed = sem("o_normed")
        o_rstd = sem("o_rstd")
        o_squared = sem("o_squared")
        o_sum = sem("o_sum")
        probs_ready = sem("probs_ready")
        probs_t_ready = sem("probs_t_ready")
        probs_turned = sem("probs_turned")
        qk_done = sem("qk_done")
        qk_ready = sem("qk_ready")
        rows_exp = sem("rows_exp")
        rows_kept = sem("rows_kept")
        rows_made = sem("rows_made")
        rows_turn = sem("rows_turn")
        rows_turned = sem("rows_turned")
        s_ready = sem("s_ready")
        scores_ready = sem("scores_ready")
        sq_done = sem("sq_done")
        srows_kept = sem("srows_kept")
        srows_made = sem("srows_made")
        ssm_small = sem("ssm_small")
        state_parts = sem("state_parts")
        states_ready = sem("states_ready")
        tanh_ready = sem("tanh_ready")
        v_tok_ready = sem("v_tok_ready")
        v_turned = sem("v_turned")
        values_ready = sem("values_ready")
        vd_here = sem("vd_here")
        vd_ready = sem("vd_ready")
        vd_turned = sem("vd_turned")
        weights_ready = sem("weights_ready")
        x_turned = sem("x_turned")
        xw_ready = sem("xw_ready")
        y_gated = sem("y_gated")
        y_high = sem("y_high")
        y_inner = sem("y_inner")
        y_made = sem("y_made")
        y_normed = sem("y_normed")
        y_outer = sem("y_outer")
        y_ready = sem("y_ready")
        y_rstd = sem("y_rstd")
        y_squares = sem("y_squares")
        y_sum = sem("y_sum")
        z_tanh = sem("z_tanh")
        stored = sem("stored")
        rstd_ready = sem("rstd_ready")
        rstd_used = sem("rstd_used")
        rows_ready = sem("rows_ready")
        row_gain = sem("row_gain")

        def load_unit(t, slot, dst, src):
            t.e.wait_ge(w_split[slot], t.next(w_split[slot]))
            t.e.sem_inc(begun, 1)
            t.e.dma_start(dst, src).then_inc(w_loaded[slot], 16)

        def split_unit(t, slot):
            t.e.wait_ge(w_loaded[slot], t.next(w_loaded[slot], 16))
            t.e.wait_ge(unit_done[slot], t.next(unit_done[slot]))
            t.e.sem_inc(begun, 1)
            t.e.tensor_copy(w_hi[:, slot, :], w_raw[:, slot, :]).then_inc(pool_done, 1)
            t.e.wait_ge(pool_done, t.next(pool_done))
            t.e.tensor_tensor(w_lo[:, slot, :], w_raw[:, slot, :], w_hi[:, slot, :].bitcast(F32),
                              ALU.subtract).then_inc(w_split[slot], 1)

        def products(t, ps, m, slot, col, rhs_hi, rhs_lo, first, last):
            for w, r in ((w_hi, rhs_hi), (w_hi, rhs_lo), (w_lo, rhs_hi)):
                for n in range(2):
                    ins = t.e.matmul(ps[0:m, n, :], w[:, slot, col:col + m], r[:, n * HALF:(n + 1) * HALF],
                                     start=first and w is w_hi and r is rhs_hi,
                                     stop=last and w is w_lo)
            return ins

        def project(t, slot, ksteps=None):
            t.e.wait_ge(w_split[slot], t.next(w_split[slot]))
            t.e.wait_ge(pair_free[slot], t.next(pair_free[slot]))
            for k in range(KD):
                ins = products(t, pair[slot], P, slot, k * P, HH[:, k, :], HL[:, k, :], k == 0, k == KD - 1)
            ins.then_inc(unit_done[slot], 1)

        x_in = cut(0, 2).rearrange("p (b n) -> p b n", b=2)

        def sp_x(t):
            def body(i):
                for b in range(2):
                    t.e.wait_ge(x_read[b], t.next(x_read[b]))
                    t.e.dma_start(x_in[:, b, :], x[0, bass.ds(i * 2 * P + b * P, P), :]).then_inc(x_loaded[b], 16)
            t.loop(NC // 2, body)

        def pe_x(t):
            t.e.wait_ge(const_ready, t.next(const_ready))

            def body(i):
                for b in range(2):
                    t.e.wait_ge(x_loaded[b], t.next(x_loaded[b], 16))
                    t.e.wait_ge(pair_free[b], t.next(pair_free[b]))
                    for k in range(KD):
                        ins = t.e.transpose(pair[b][:, k // 4, k % 4 * P:(k % 4 + 1) * P],
                                            x_in[:, b, k * P:(k + 1) * P], ident[:, :])
                    ins.then_inc(turned_done[b], 1)
            t.loop(NC // 2, body)

        def act_x(t):
            def body(i):
                for b in range(2):
                    t.e.wait_ge(turned_done[b], t.next(turned_done[b]))
                    t.e.sem_inc(x_read[b], 1)
                    t.e.activation(X[:, :, bass.ds(i * 2 * P + b * P, P)],
                                   pair[b][:, :, :].rearrange("p a (c n) -> p (a c) n", n=P),
                                   ACT.Copy).then_inc(pair_free[b], 1)
            t.loop(NC // 2, body)
            t.e.drain().then_inc(resid_ready, 1)

        squares = cut(0, 2).rearrange("p (b n) -> p b n", b=2)
        square_sum = cut(2)

        def act_norm(t, which, power):
            t.e.wait_ge(resid_ready, t.next(resid_ready))
            for k in range(KD):
                t.e.activation(HH[:, k, :], X[:, k, :], ACT.Copy,
                               scale=gains[:, which, k:k + 1]).then_inc(high_ready, 1)
                t.e.wait_ge(sq_used, t.next(sq_used))
                t.e.activation(squares[:, k % 2, :], X[:, k, :], ACT.Square).then_inc(sq_ready, 1)
            t.e.wait_ge(norm_sum, t.next(norm_sum))
            t.e.activation(R[:, :], pair[3][:, :, :].rearrange("p a n -> p (a n)"), ACT.Ln,
                           scale=1.0 / D, bias=eps_col[:, 0:1]).then_inc(act_done, 1)
            t.e.wait_ge(act_done, t.next(act_done))
            t.e.activation(R[:, :], R[:, :], ACT.Exp, scale=power).then_inc(r_ready, 1)

        def dve_norm(t, which):
            t.e.wait_ge(resid_ready, t.next(resid_ready))
            for k in range(KD):
                t.e.wait_ge(high_ready, t.next(high_ready))
                t.e.scalar_tensor_tensor(out=HL[:, k, :], in0=X[:, k, :], scalar=gains[:, which, k:k + 1],
                                         in1=HH[:, k, :].bitcast(F32), op0=ALU.mult,
                                         op1=ALU.subtract).then_inc(low_ready, 1)
                t.e.wait_ge(sq_ready, t.next(sq_ready))
                if k == 0:
                    t.e.tensor_copy(square_sum, squares[:, 0, :]).then_inc(dve_done, 1)
                    t.e.wait_ge(dve_done, t.next(dve_done))
                else:
                    t.e.tensor_tensor(square_sum, square_sum, squares[:, k % 2, :], ALU.add).then_inc(dve_done, 1)
                    t.e.wait_ge(dve_done, t.next(dve_done))
                t.e.sem_inc(sq_used, 1)
            t.e.sem_inc(sum_ready, 1)

        def pe_norm(t):
            for k in range(KD):
                t.e.wait_ge(low_ready, t.next(low_ready))
            t.e.wait_ge(sum_ready, t.next(sum_ready))
            for n in range(2):
                ins = t.e.matmul(pair[3][:, n, :], ones[:, :], square_sum[:, n * HALF:(n + 1) * HALF],
                                 start=True, stop=True)
            ins.then_inc(norm_sum, 1)

        z = cut(3, 2).rearrange("p (b n) -> p b n", b=2)

        def sp_mlp(t, l):
            w1 = mlp_w1[l].rearrange("(k p) n -> p k n", p=P)
            w2 = mlp_w2[l].rearrange("(k p) n -> p k n", p=P)

            def body(i):
                for j in range(4):
                    load_unit(t, j % 2, w_raw[:, j % 2, :].rearrange("p (k n) -> p k n", k=KD),
                              w1[:, :, bass.ds(i * FB + j * P, P)])
                for j in range(4):
                    load_unit(t, j % 2, w_raw[:, j % 2, :].rearrange("p (k n) -> p k n", k=4),
                              w2[:, bass.ds(i * 4, 4), j * 2 * P:(j + 1) * 2 * P])
            t.loop(N_FB, body)

        def pool_units(t, n, slots):
            def body(i):
                for s in slots:
                    split_unit(t, s)
            t.loop(n, body)

        def pe_mlp(t):
            def body(i):
                for j in range(4):
                    project(t, j % 2)
                for j in range(4):
                    t.e.wait_ge(w_split[j % 2], t.next(w_split[j % 2]))
                    for m in range(2):
                        p = j % 2 + 2 * (1 - m)
                        t.e.wait_ge(pair_free[p], t.next(pair_free[p]))
                        for k in range(4):
                            if j == 0 and m == 0:
                                t.e.wait_ge(z_low, t.next(z_low))
                            ins = products(t, pair[p], P, j % 2, k * 2 * P + m * P, z_hi[:, k, :],
                                           z_lo[:, k, :], k == 0, k == 3)
                        ins.then_inc(unit_done[j % 2] if m else part_done[p], 1)
            t.loop(N_FB, body)

        def dve_mlp(t):
            t.e.wait_ge(r_ready, t.next(r_ready))

            def body(i):
                for j in range(4):
                    t.e.wait_ge(unit_done[j % 2], t.next(unit_done[j % 2]))
                    t.e.tensor_scalar(z[:, j % 2, :], pair[j % 2].rearrange("p a n -> p (a n)"), 0.0, None, ALU.max).then_inc(dve_done, 1)
                    t.e.wait_ge(dve_done, t.next(dve_done))
                    t.e.sem_inc(pair_free[j % 2], 1)
                    t.e.tensor_tensor(z[:, j % 2, :], z[:, j % 2, :], R[:, :], ALU.mult).then_inc(dve_done, 1)
                    t.e.wait_ge(dve_done, t.next(dve_done))
                    t.e.tensor_tensor(z[:, j % 2, :], z[:, j % 2, :], z[:, j % 2, :], ALU.mult).then_inc(z_ready, 1)
                    t.e.wait_ge(z_ready, t.next(z_ready))
                    t.e.wait_ge(z_high, t.next(z_high))
                    t.e.tensor_tensor(z_lo[:, j, :], z[:, j % 2, :], z_hi[:, j, :].bitcast(F32),
                                      ALU.subtract).then_inc(z_low, 1)
                for j in range(4):
                    for m in range(2):
                        p = j % 2 + 2 * (1 - m)
                        t.e.wait_ge(unit_done[j % 2] if m else part_done[p], t.next(unit_done[j % 2] if m else part_done[p]))
                        t.e.tensor_tensor(X[:, 2 * j + m, :], X[:, 2 * j + m, :],
                                          pair[p].rearrange("p a n -> p (a n)"),
                                          ALU.add).then_inc(pair_free[p], 1)
            t.loop(N_FB, body)
            t.e.drain().then_inc(resid_ready, 1)

        def act_mlp(t):
            def body(i):
                for j in range(4):
                    t.e.wait_ge(z_ready, t.next(z_ready))
                    t.e.activation(z_hi[:, j, :], z[:, j % 2, :], ACT.Copy).then_inc(z_high, 1)
            t.loop(N_FB, body)

        C_MQ, C_MK, C_MV, C_MO = 0, MH * DH, 2 * MH * DH, 3 * MH * DH
        C_MI, C_MF = 4 * MH * DH, 4 * MH * DH + MH
        C_DQ = C_MF + MH
        C_DK, C_DV = C_DQ + 2 * AH * AD, C_DQ + 4 * AH * AD
        AB_UNITS = (C_DQ, C_DK, C_DV, C_MQ, C_MK, C_MV, C_MO)

        bias_dist = cut(0)
        qd, kd, vd = cut(1), cut(2), cut(3).rearrange("p (c e) -> p c e", c=NC)
        prob = [cut(4), cut(5)]
        prob_t = cut(12)
        o_t = cut(6)
        conv_y, conv_th = cut(7), cut(8)
        mq, mk = cut(9), cut(10)
        v_tok = vd
        kw_tok = cut(12).rearrange("p (c e) -> p c e", c=NC)
        gate_w = cut(11)
        inter = cut(13)
        c_all = conv_th.rearrange("p (c e) -> p c e", c=NC)
        h_tok = conv_y.rearrange("p (c e) -> p c e", c=NC)
        o_gate = mk
        hm_t = mq

        gate_raw = cut(13)[:, 0:KD * 36].rearrange("p (k n) -> p k n", k=KD)
        lam_rows = cut(12)[:, 0:4 * AD].rearrange("p (a n) -> p a n", a=4)

        def pair_chunks(p):
            return pair[p][:, :, :].rearrange("p a (c n) -> p (a c) n", n=P)

        def flat(ap):
            return ap.rearrange("p a n -> p (a n)")

        def chunks(ap):
            return ap.rearrange("p (c n) -> p c n", c=NC)

        def turned(p, c):
            return pair[p][:, c // 4, c % 4 * P:(c % 4 + 1) * P]

        def sp_ab_small(t):
            w = ab_w_in[0].rearrange("(k p) n -> p k n", p=P)
            col = dict(allow_slow_non_contiguous=True)
            t.e.wait_ge(ab_zeroed, t.next(ab_zeroed))
            for dst, src in (
                    (gate_raw[:, :, 0:MH], w[:, :, C_MI:C_MI + MH]),
                    (gate_raw[:, :, 32:32 + MH], w[:, :, C_MF:C_MF + MH]),
                    (conv_w[:, :, :], ab_conv_w[0].rearrange("j (m p) -> p j m", p=P)),
                    (conv_b[:, :], ab_conv_b[0].rearrange("(m p) -> p m", p=P)),
                    (gate_bias[0:MH, :], ab_i_bias[0].rearrange("(p a) -> p a", a=1)),
                    (gate_bias[32:32 + MH, :], ab_f_bias[0].rearrange("(p a) -> p a", a=1)),
                    (mnorm[:, :], ab_mnorm_g[0].rearrange("(m p) -> p m", p=P)),
                    (dnorm[:, :], ab_dnorm_g[0].rearrange("(m p) -> p m", p=P)),
                    (lam_rows[:, 0, :], ab_lam_q1.to_broadcast([P, AD])),
                    (lam_rows[:, 1, :], ab_lam_k1.to_broadcast([P, AD])),
                    (lam_rows[:, 2, :], ab_lam_q2.to_broadcast([P, AD])),
                    (lam_rows[:, 3, :], ab_lam_k2.to_broadcast([P, AD]))):
                t.e.dma_start(dst, src, **(col if len(dst.shape) == 3 or dst.shape[1] <= 8 else {})
                              ).then_inc(ab_small, 16)

        AB_SMALL = 12 * 16

        def sp_ab(t):
            w = ab_w_in[0].rearrange("(k p) n -> p k n", p=P)
            wo = ab_w_out[0].rearrange("(a r) n -> r a n", a=2)
            t.e.wait_ge(rows_made, t.next(rows_made, 2))
            t.e.dma_start(ab_rows[0], neg_g[0:MH, :]).then_inc(rows_kept, 16)
            t.e.dma_start(ab_rows[1], inter_row[0:MH, :]).then_inc(rows_kept, 16)
            t.e.wait_ge(rows_kept, t.next(rows_kept, 32))

            def body(i):
                for j, c in enumerate(AB_UNITS):
                    load_unit(t, j % 2, w_raw[:, j % 2, :].rearrange("p (k n) -> p k n", k=KD),
                              w[:, :, bass.ds(i * P + c, P)])
                    if j == 2:
                        t.e.wait_ge(gates_free, t.next(gates_free))
                        t.e.sem_inc(begun, 1)
                        t.e.dma_start(gate_w, ab_rows[0, bass.ds(i, 1), :].to_broadcast([P, T])).then_inc(gates_here, 16)
                        t.e.dma_start(inter, ab_rows[1, bass.ds(i, 1), :].to_broadcast([P, T])).then_inc(gates_here, 16)
                for j in range(2):
                    s = (7 + j) % 2
                    load_unit(t, s, w_raw[:, s, :].rearrange("p (a n) -> p a n", a=2),
                              wo[bass.ds(i * P, P), :, j * HALF:(j + 1) * HALF])
            t.loop(MH, body)

        rows_i, rows_f, rows_e, rows_l = cut(4), cut(5), cut(6), cut(7)
        row_b, row_g, row_big, row_d, row_rst = cut(8), cut(9), cut(10), cut(11), cut(12)
        neg_g, inter_row, row_w, row_m = cut(13), cut(1), cut(2), cut(3)

        def pe_gates(t):
            t.e.wait_ge(gate_split, t.next(gate_split))
            t.e.wait_ge(pair_free[2], t.next(pair_free[2]))
            M = 32 + MH
            for k in range(KD):
                for w, r in ((gate_hi, HH), (gate_hi, HL), (gate_lo, HH)):
                    for n in range(2):
                        ins = t.e.matmul(pair[2][0:M, n, :], w[:, k, :], r[:, k, n * HALF:(n + 1) * HALF],
                                         start=(k == 0 and w is gate_hi and r is HH),
                                         stop=(k == KD - 1 and w is gate_lo))
            ins.then_inc(gates_done, 1)
            t.e.wait_ge(rows_turn, t.next(rows_turn))
            t.e.wait_ge(pair_free[3], t.next(pair_free[3]))
            for q, row in enumerate((row_g, row_w, row_m)):
                for c in range(NC):
                    at = (q * NC + c) * MH
                    ins = t.e.transpose(pair[3][:, 0, at:at + MH], row[0:MH, c * P:(c + 1) * P], ident[0:MH, 0:MH])
            ins.then_inc(rows_turned, 1)

        def dve_gates(t):
            t.e.wait_ge(ab_small, t.next(ab_small, AB_SMALL))
            t.e.tensor_copy(gate_hi[:, :, :], gate_raw[:, :, :]).then_inc(dve_done, 1)
            t.e.wait_ge(dve_done, t.next(dve_done))
            t.e.tensor_tensor(gate_lo[:, :, :], gate_raw[:, :, :], gate_hi[:, :, :].bitcast(F32),
                              ALU.subtract).then_inc(gate_split, 1)
            t.e.tensor_scalar(conv_w[:, :, :], conv_w[:, :, :], 0.5, None, ALU.mult).then_inc(dve_done, 1)
            t.e.wait_ge(dve_done, t.next(dve_done))
            t.e.tensor_scalar(conv_b[:, :], conv_b[:, :], 0.5, None, ALU.mult).then_inc(dve_done, 1)
            t.e.wait_ge(dve_done, t.next(dve_done))
            t.e.tensor_scalar(mnorm[:, :], mnorm[:, :], 0.5, None, ALU.mult).then_inc(dve_done, 1)
            t.e.wait_ge(dve_done, t.next(dve_done))
            t.e.tensor_scalar(dnorm[:, :], dnorm[:, :], 1.0 - LAM_INIT, None, ALU.mult).then_inc(dve_done, 1)
            t.e.wait_ge(dve_done, t.next(dve_done))
            for m in range(2):
                t.e.tensor_tensor_reduce(lam_rows[:, 2 * m, :], lam_rows[:, 2 * m, :],
                                         lam_rows[:, 2 * m + 1, :], 1.0, 0.0, ALU.mult, ALU.add,
                                         lam[:, m:m + 1]).then_inc(dve_done, 1)
                t.e.wait_ge(dve_done, t.next(dve_done))
            t.e.sem_inc(lam_dots, 1)
            t.e.wait_ge(lam_exps, t.next(lam_exps))
            t.e.tensor_tensor(lam[:, 2:3], lam[:, 1:2], lam[:, 0:1], ALU.subtract).then_inc(dve_done, 1)
            t.e.wait_ge(dve_done, t.next(dve_done))
            t.e.tensor_scalar(lam[:, 2:3], lam[:, 2:3], -LAM_INIT, None, ALU.add).then_inc(dve_done, 1)
            t.e.wait_ge(dve_done, t.next(dve_done))
            t.e.wait_ge(r_ready, t.next(r_ready))
            t.e.wait_ge(gates_done, t.next(gates_done))
            h, f = slice(0, MH), slice(32, 32 + MH)
            t.e.tensor_tensor(rows_i[h, :], flat(pair[2])[h, :], R[h, :], ALU.mult).then_inc(dve_done, 1)
            t.e.wait_ge(dve_done, t.next(dve_done))
            t.e.tensor_tensor(rows_f[f, :], flat(pair[2])[f, :], R[f, :], ALU.mult).then_inc(dve_done, 1)
            t.e.wait_ge(dve_done, t.next(dve_done))
            t.e.sem_inc(pair_free[2], 1)
            t.e.tensor_scalar(rows_i[h, :], rows_i[h, :], gate_bias[h, :], None, ALU.add).then_inc(dve_done, 1)
            t.e.wait_ge(dve_done, t.next(dve_done))
            t.e.tensor_scalar(rows_f[f, :], rows_f[f, :], gate_bias[f, :], None, ALU.add).then_inc(dve_done, 1)
            t.e.wait_ge(dve_done, t.next(dve_done))
            t.e.sem_inc(f_ready, 1)
            t.e.wait_ge(f_exp, t.next(f_exp))
            t.e.tensor_scalar(rows_e[f, :], rows_e[f, :], 1.0, None, ALU.add).then_inc(dve_done, 1)
            t.e.wait_ge(dve_done, t.next(dve_done))
            t.e.sem_inc(f_ready, 1)
            t.e.wait_ge(f_log, t.next(f_log))
            t.e.scalar_tensor_tensor(out=row_d[h, :], in0=rows_f[f, :], scalar=0.0, in1=rows_l[f, :],
                                     op0=ALU.min, op1=ALU.subtract).then_inc(dve_done, 1)
            t.e.wait_ge(dve_done, t.next(dve_done))
            t.e.memset(row_rst[h, :], 1.0).then_inc(dve_done, 1)
            t.e.wait_ge(dve_done, t.next(dve_done))
            t.e.memset(chunks(row_rst)[h, :, 0:1], 0.0).then_inc(dve_done, 1)
            t.e.wait_ge(dve_done, t.next(dve_done))
            t.e.tensor_tensor_scan(row_b[h, :], row_rst[h, :], row_d[h, :], 0.0, ALU.mult, ALU.add).then_inc(dve_done, 1)
            t.e.wait_ge(dve_done, t.next(dve_done))
            t.e.tensor_tensor(row_g[h, :], rows_i[h, :], row_b[h, :], ALU.subtract).then_inc(dve_done, 1)
            t.e.wait_ge(dve_done, t.next(dve_done))
            t.e.memset(row_d[h, :], 0.0).then_inc(dve_done, 1)
            t.e.wait_ge(dve_done, t.next(dve_done))
            t.e.tensor_copy(chunks(row_d)[h, 1:NC, 0:1], chunks(row_b)[h, 0:NC - 1, P - 1:P]).then_inc(dve_done, 1)
            t.e.wait_ge(dve_done, t.next(dve_done))
            t.e.tensor_tensor_scan(row_big[h, :], row_d[h, :], row_g[h, :], 0.0, ALU.add, ALU.max).then_inc(dve_done, 1)
            t.e.wait_ge(dve_done, t.next(dve_done))
            t.e.memset(m0[h, 0:1], 0.0).then_inc(dve_done, 1)
            t.e.wait_ge(dve_done, t.next(dve_done))
            t.e.tensor_tensor(m0[h, 1:NC].rearrange("p (c a) -> p c a", a=1), chunks(row_big)[h, 0:NC - 1, P - 1:P],
                              chunks(row_b)[h, 0:NC - 1, P - 1:P], ALU.add).then_inc(dve_done, 1)
            t.e.wait_ge(dve_done, t.next(dve_done))
            t.e.tensor_tensor(chunks(inter_row)[h, :, :], m0[h, :].rearrange("p (c a) -> p c a", a=1).to_broadcast([MH, NC, P]),
                              chunks(row_big)[h, :, :], ALU.subtract).then_inc(dve_done, 1)
            t.e.wait_ge(dve_done, t.next(dve_done))
            t.e.tensor_tensor(chunks(row_w)[h, :, :], chunks(row_g)[h, :, :],
                              chunks(row_big)[h, :, P - 1:P].to_broadcast([MH, NC, P]), ALU.subtract).then_inc(dve_done, 1)
            t.e.wait_ge(dve_done, t.next(dve_done))
            t.e.tensor_tensor(row_m[h, :], row_b[h, :], row_big[h, :], ALU.add).then_inc(dve_done, 1)
            t.e.wait_ge(dve_done, t.next(dve_done))
            t.e.tensor_scalar(neg_g[h, :], row_big[h, :], -1.0, None, ALU.mult).then_inc(rows_made, 1)
            t.e.sem_inc(rows_exp, 1)
            t.e.wait_ge(rows_turned, t.next(rows_turned))
            t.e.tensor_copy(gate_cols.rearrange("p q c h -> p (q c h)"), pair[3][:, 0, 0:3 * NC * MH]).then_inc(dve_done, 1)
            t.e.wait_ge(dve_done, t.next(dve_done))
            t.e.sem_inc(pair_free[3], 1)

        def act_gates(t):
            t.e.wait_ge(lam_dots, t.next(lam_dots))
            t.e.activation(lam[:, 0:2], lam[:, 0:2], ACT.Exp).then_inc(lam_exps, 1)
            h, f = slice(0, MH), slice(32, 32 + MH)
            t.e.wait_ge(f_ready, t.next(f_ready))
            t.e.activation(rows_e[f, :], rows_f[f, :], ACT.Abs).then_inc(act_done, 1)
            t.e.wait_ge(act_done, t.next(act_done))
            t.e.activation(rows_e[f, :], rows_e[f, :], ACT.Exp, scale=-1.0).then_inc(f_exp, 1)
            t.e.wait_ge(f_ready, t.next(f_ready))
            t.e.activation(rows_l[f, :], rows_e[f, :], ACT.Ln).then_inc(f_log, 1)
            t.e.wait_ge(rows_exp, t.next(rows_exp))
            t.e.activation(inter_row[h, :], inter_row[h, :], ACT.Exp).then_inc(rows_made, 1)
            t.e.activation(row_w[h, :], row_w[h, :], ACT.Exp).then_inc(act_done, 1)
            t.e.wait_ge(act_done, t.next(act_done))
            t.e.activation(row_m[h, :], row_m[h, :], ACT.Exp, scale=-1.0).then_inc(rows_turn, 1)

        def pool_ab(t):
            t.e.memset(gate_raw[:, :, :], 0.0).then_inc(pool_done, 1)
            t.e.wait_ge(pool_done, t.next(pool_done))
            t.e.sem_inc(ab_zeroed, 1)
            t.e.wait_ge(norm_sum, t.next(norm_sum))
            t.e.iota(bias_dist, pattern=[[1, T]], base=-(T - P), channel_multiplier=-1,
                     allow_small_or_imprecise_dtypes=True).then_inc(pool_done, 1)
            t.e.wait_ge(pool_done, t.next(pool_done))
            t.e.tensor_scalar(bias_dist, bias_dist, SLOPE, None, ALU.mult).then_inc(pool_done, 1)
            t.e.wait_ge(pool_done, t.next(pool_done))
            t.e.affine_select(out=bias_dist, in_=bias_dist, compare_op=ALU.is_ge, fill=NEG,
                              base=T - P, pattern=[[-1, T]], channel_multiplier=1).then_inc(dist_ready, 1)

        def width(qb):
            return (qb + 1) * P

        def pe_scores(t, qb):
            for m in range(2):
                t.e.wait_ge(pair_free[2], t.next(pair_free[2]))
                part = slice(m * AD, (m + 1) * AD)
                for n in range((width(qb) + HALF - 1) // HALF):
                    w = min(HALF, width(qb) - n * HALF)
                    ins = t.e.matmul(pair[2][:, n, 0:w], qd[part, qb * P:(qb + 1) * P],
                                     kd[part, n * HALF:n * HALF + w], start=True, stop=True)
                ins.then_inc(scores_ready, 1)

        def pe_values(t, qb):
            t.e.wait_ge(probs_ready, t.next(probs_ready))
            t.e.wait_ge(pair_free[3], t.next(pair_free[3]))
            for n in range((width(qb) + HALF - 1) // HALF):
                for kb in range(4 * n, min(4 * n + 4, qb + 1)):
                    ins = t.e.transpose(pair[3][:, 0, kb % 4 * P:(kb % 4 + 1) * P],
                                        prob[1][:, kb * P:(kb + 1) * P], ident[:, :])
                ins.then_inc(probs_turned, 1)
                t.e.wait_ge(probs_t_ready, t.next(probs_t_ready))
            for kb in range(qb + 1):
                ins = t.e.matmul(pair[3][:, 1, 0:P], vd[:, kb, :], prob_t[:, kb * P:(kb + 1) * P],
                                 start=(kb == 0), stop=(kb == qb))
            ins.then_inc(values_ready, 1)

        def dve_scores(t, qb):
            w = width(qb)
            for m in range(2):
                t.e.wait_ge(scores_ready, t.next(scores_ready))
                if m == 1 and qb > 0:
                    for _ in range((width(qb - 1) + HALF - 1) // HALF):
                        t.e.wait_ge(probs_turned, t.next(probs_turned))
                t.e.sem_inc(begun, 1)
                t.e.tensor_tensor_reduce(prob[m][:, 0:w], flat(pair[2])[:, 0:w], bias_dist[:, T - w:T], 1.0,
                                         LEAST, ALU.add, ALU.max, stat[:, m:m + 1]).then_inc(dve_done, 1)
                t.e.wait_ge(dve_done, t.next(dve_done))
                t.e.sem_inc(pair_free[2], 1)
                t.e.tensor_scalar(stat[:, m:m + 1], stat[:, m:m + 1], -1.0, None, ALU.mult).then_inc(max_ready, 1)

        def dve_probs(t, qb):
            w = width(qb)
            for m in range(2):
                t.e.wait_ge(exp_ready, t.next(exp_ready))
            t.e.reciprocal(stat[:, 4:6], stat[:, 2:4]).then_inc(dve_done, 1)
            t.e.wait_ge(dve_done, t.next(dve_done))
            t.e.tensor_tensor(stat[:, 5:6], stat[:, 5:6], lam[:, 2:3], ALU.mult).then_inc(dve_done, 1)
            t.e.wait_ge(dve_done, t.next(dve_done))
            t.e.tensor_scalar(prob[0][:, 0:w], prob[0][:, 0:w], stat[:, 4:5], None, ALU.mult).then_inc(dve_done, 1)
            t.e.wait_ge(dve_done, t.next(dve_done))
            t.e.scalar_tensor_tensor(out=prob[1][:, 0:w], in0=prob[1][:, 0:w], scalar=stat[:, 5:6],
                                     in1=prob[0][:, 0:w], op0=ALU.mult, op1=ALU.add).then_inc(dve_done, 1)
            t.e.wait_ge(dve_done, t.next(dve_done))
            t.e.sem_inc(probs_ready, 1)

        def act_probs(t, qb):
            w = width(qb)
            for m in range(2):
                t.e.wait_ge(max_ready, t.next(max_ready))
                t.e.activation(prob[m][:, 0:w], prob[m][:, 0:w], ACT.Exp, bias=stat[:, m:m + 1],
                               accum_out=stat[:, 2 + m:3 + m]).then_inc(exp_ready, 1)

        def act_values(t, qb):
            for n in range((width(qb) + HALF - 1) // HALF):
                w = min(HALF, width(qb) - n * HALF)
                t.e.wait_ge(probs_turned, t.next(probs_turned))
                t.e.activation(prob_t[:, n * HALF:n * HALF + w], pair[3][:, 0, 0:w], ACT.Copy).then_inc(probs_t_ready, 1)
            t.e.wait_ge(values_ready, t.next(values_ready))
            t.e.activation(o_t[:, qb * P:(qb + 1) * P], pair[3][:, 1, 0:P], ACT.Copy).then_inc(act_done, 1)
            t.e.wait_ge(act_done, t.next(act_done))
            t.e.sem_inc(pair_free[3], 1)

        def turn(t, p, src):
            t.e.wait_ge(pair_free[p], t.next(pair_free[p]))
            for c in range(NC):
                ins = t.e.transpose(turned(p, c), src(c), ident[:, :])
            return ins

        def pe_ab(t):
            def body(i):
                for j in range(4):
                    project(t, j % 2)
                t.e.wait_ge(qk_ready, t.next(qk_ready, 2))
                pe_scores(t, 0)
                t.e.wait_ge(vd_ready, t.next(vd_ready))
                turn(t, 3, lambda c: o_t[:, c * P:(c + 1) * P]).then_inc(vd_turned, 1)
                for j, (a, b) in zip((4, 5, 6), ((1, 3), (3, 6), (6, 8))):
                    project(t, j % 2)
                    for qb in range(a, b):
                        pe_scores(t, qb)
                        pe_values(t, qb - 1)
                pe_values(t, NC - 1)
                t.e.wait_ge(o_squared, t.next(o_squared))
                t.e.wait_ge(pair_free[2], t.next(pair_free[2]))
                for n in range(2):
                    ins = t.e.matmul(pair[2][:, n, :], ones[:, :], prob[0][:, n * HALF:(n + 1) * HALF],
                                     start=True, stop=True)
                ins.then_inc(o_sum, 1)
                t.e.wait_ge(mk_ready, t.next(mk_ready))
                turn(t, 3, lambda c: mk[:, c * P:(c + 1) * P]).then_inc(k_turned, 1)
                t.e.wait_ge(mv_ready, t.next(mv_ready))
                turn(t, 2, lambda c: conv_y[:, c * P:(c + 1) * P]).then_inc(v_turned, 1)
                t.e.wait_ge(pair_free[3], t.next(pair_free[3]))
                for c in range(NC):
                    ins = t.e.matmul(turned(3, c), mk[:, c * P:(c + 1) * P], mq[:, c * P:(c + 1) * P],
                                     start=True, stop=True)
                ins.then_inc(qk_done, 1)
                t.e.wait_ge(kw_ready, t.next(kw_ready))
                t.e.wait_ge(v_tok_ready, t.next(v_tok_ready))
                t.e.wait_ge(pair_free[2], t.next(pair_free[2]))
                for c in range(NC - 1):
                    t.e.matmul(turned(2, c), kw_tok[:, c, :], v_tok[:, c, :], start=True, stop=True)
                    ins = t.e.matmul(pair[2][:, 1, 3 * P + c:3 * P + c + 1], kw_tok[:, c, :], ones[:, 0:1],
                                     start=True, stop=True)
                ins.then_inc(state_parts, 1)
                t.e.wait_ge(weights_ready, t.next(weights_ready))
                t.e.wait_ge(states_ready, t.next(states_ready))
                t.e.wait_ge(pair_free[3], t.next(pair_free[3]))
                t.e.wait_ge(pair_free[2], t.next(pair_free[2]))
                for c in range(NC):
                    w = gate_w[:, c * P:(c + 1) * P]
                    q = mq[:, c * P:(c + 1) * P]
                    t.e.matmul(turned(3, c), w, v_tok[:, c, :], start=True, stop=(c == 0))
                    if c > 0:
                        t.e.matmul(turned(3, c), q, c_all[:, c, :], start=False, stop=True)
                    ins = t.e.matmul(pair[2][:, 0, c:c + 1], w, ones[:, 0:1], start=True, stop=(c == 0))
                    if c > 0:
                        ins = t.e.matmul(pair[2][:, 0, c:c + 1], q, n_all[:, c:c + 1], start=False, stop=True)
                ins.then_inc(num_ready, 1)
                t.e.wait_ge(h_ready, t.next(h_ready))
                turn(t, 3, lambda c: h_tok[:, c, :]).then_inc(h_turned, 1)
                t.e.wait_ge(y_ready, t.next(y_ready, 2))
                for j in range(2):
                    s = (7 + j) % 2
                    t.e.wait_ge(w_split[s], t.next(w_split[s]))
                    for m in range(4):
                        p = s + 2 * (1 - m % 2)
                        t.e.wait_ge(pair_free[p], t.next(pair_free[p]))
                        for k in range(2):
                            ins = products(t, pair[p], P, s, k * HALF + m * P, y_hi[:, k, :], y_lo[:, k, :],
                                           k == 0, k == 1)
                        ins.then_inc(unit_done[s] if m == 3 else part_done[p], 1)
            t.loop(MH, body)

        def scaled(t, out, s):
            t.e.wait_ge(unit_done[s], t.next(unit_done[s]))
            t.e.tensor_tensor(out, flat(pair[s]), R[:, :], ALU.mult).then_inc(dve_done, 1)
            t.e.wait_ge(dve_done, t.next(dve_done))
            t.e.sem_inc(pair_free[s], 1)

        def dve_conv(t, out, s, j):
            scaled(t, conv_in[:, 3:3 + T], s)
            t.e.tensor_scalar(conv_y, conv_in[:, 3:3 + T], conv_w[:, 3, j], conv_b[:, j], ALU.mult, ALU.add).then_inc(dve_done, 1)
            t.e.wait_ge(dve_done, t.next(dve_done))
            for tap in range(3):
                t.e.scalar_tensor_tensor(out=conv_y, in0=conv_in[:, tap:tap + T], scalar=conv_w[:, tap, j],
                                         in1=conv_y, op0=ALU.mult, op1=ALU.add).then_inc(dve_done, 1)
                t.e.wait_ge(dve_done, t.next(dve_done))
            t.e.sem_inc(conv_ready, 1)
            t.e.wait_ge(tanh_ready, t.next(tanh_ready))
            t.e.scalar_tensor_tensor(out=out, in0=conv_th, scalar=1.0, in1=conv_y, op0=ALU.add, op1=ALU.mult).then_inc(dve_done, 1)
            t.e.wait_ge(dve_done, t.next(dve_done))

        def act_tanh(t):
            t.e.wait_ge(conv_ready, t.next(conv_ready))
            t.e.activation(conv_th, conv_y, ACT.Tanh).then_inc(tanh_ready, 1)

        def dve_ab(t):
            t.e.wait_ge(dist_ready, t.next(dist_ready))

            def body(i):
                scaled(t, qd, 0)
                t.e.tensor_scalar(qd, qd, AD ** -0.5, None, ALU.mult).then_inc(dve_done, 1)
                t.e.wait_ge(dve_done, t.next(dve_done))
                t.e.sem_inc(qk_ready, 1)
                scaled(t, kd, 1)
                t.e.sem_inc(qk_ready, 1)
                scaled(t, o_t, 0)
                t.e.sem_inc(vd_ready, 1)
                dve_conv(t, mq, 1, bass.ds(i, 1))
                dve_scores(t, 0)
                t.e.wait_ge(vd_turned, t.next(vd_turned))
                t.e.tensor_copy(vd, pair_chunks(3)).then_inc(dve_done, 1)
                t.e.wait_ge(dve_done, t.next(dve_done))
                t.e.sem_inc(pair_free[3], 1)
                t.e.sem_inc(vd_here, 1)
                for j, (a, b) in zip((4, 5, 6), ((1, 3), (3, 6), (6, 8))):
                    if j == 4:
                        dve_conv(t, mk, 0, bass.ds(i + MH, 1))
                        t.e.sem_inc(mk_ready, 1)
                    elif j == 5:
                        scaled(t, conv_y, 1)
                        t.e.sem_inc(mv_ready, 1)
                    else:
                        scaled(t, conv_in[:, 3:3 + T], 0)
                        t.e.sem_inc(mo_ready, 1)
                    for qb in range(a, b):
                        dve_probs(t, qb - 1)
                        dve_scores(t, qb)
                dve_probs(t, NC - 1)
                for _ in range(2):
                    t.e.wait_ge(probs_turned, t.next(probs_turned))
                t.e.tensor_scalar(bias_dist, bias_dist, SLOPE, None, ALU.mult).then_inc(dve_done, 1)
                t.e.wait_ge(dve_done, t.next(dve_done))
                t.e.wait_ge(o_rstd, t.next(o_rstd))
                t.e.tensor_tensor(o_t, o_t, prob[1], ALU.mult).then_inc(dve_done, 1)
                t.e.wait_ge(dve_done, t.next(dve_done))
                t.e.sem_inc(o_normed, 1)
                t.e.wait_ge(y_high, t.next(y_high))
                t.e.scalar_tensor_tensor(out=y_lo[:, 1, :], in0=o_t, scalar=dnorm[:, bass.ds(i, 1)],
                                         in1=y_hi[:, 1, :].bitcast(F32), op0=ALU.mult,
                                         op1=ALU.subtract).then_inc(y_ready, 1)
                t.e.wait_ge(gates_here, t.next(gates_here, 32))
                g_col = gate_cols[:, 0, :, bass.ds(i, 1)]
                t.e.tensor_tensor(chunks(gate_w), chunks(gate_w), g_col.to_broadcast([P, NC, P]), ALU.add).then_inc(dve_done, 1)
                t.e.wait_ge(dve_done, t.next(dve_done))
                t.e.scalar_tensor_tensor(out=chunks(gate_w), in0=chunks(gate_w), scalar=0.0,
                                         in1=causal[:, :, :].to_broadcast([P, NC, P]), op0=ALU.min, op1=ALU.add).then_inc(dve_done, 1)
                t.e.wait_ge(dve_done, t.next(dve_done))
                t.e.sem_inc(decay_ready, 1)
                t.e.wait_ge(k_turned, t.next(k_turned))
                t.e.tensor_tensor(kw_tok, pair_chunks(3), gate_cols[:, 1, :, bass.ds(i, 1)].to_broadcast([P, NC, P]),
                                  ALU.mult).then_inc(dve_done, 1)
                t.e.wait_ge(dve_done, t.next(dve_done))
                t.e.sem_inc(pair_free[3], 1)
                t.e.sem_inc(kw_ready, 1)
                t.e.wait_ge(qk_done, t.next(qk_done))
                t.e.wait_ge(decay_exp, t.next(decay_exp))
                t.e.scalar_tensor_tensor(out=gate_w, in0=flat(pair[3]), scalar=DH ** -0.5, in1=gate_w,
                                         op0=ALU.mult, op1=ALU.mult).then_inc(dve_done, 1)
                t.e.wait_ge(dve_done, t.next(dve_done))
                t.e.sem_inc(pair_free[3], 1)
                t.e.sem_inc(weights_ready, 1)
                t.e.scalar_tensor_tensor(out=mq, in0=mq, scalar=DH ** -0.5, in1=inter, op0=ALU.mult,
                                         op1=ALU.mult).then_inc(dve_done, 1)
                t.e.wait_ge(dve_done, t.next(dve_done))
                t.e.wait_ge(state_parts, t.next(state_parts))
                keep = chunks(inter)
                t.e.tensor_copy(c_all[:, 1, :], turned(2, 0)).then_inc(dve_done, 1)
                t.e.wait_ge(dve_done, t.next(dve_done))
                t.e.tensor_copy(n_all[:, 1:2], pair[2][:, 1, 3 * P:3 * P + 1]).then_inc(dve_done, 1)
                t.e.wait_ge(dve_done, t.next(dve_done))
                for c in range(1, NC - 1):
                    t.e.scalar_tensor_tensor(out=c_all[:, c + 1, :], in0=c_all[:, c, :], scalar=keep[:, c, P - 1:P],
                                             in1=turned(2, c), op0=ALU.mult, op1=ALU.add)
                    t.e.scalar_tensor_tensor(out=n_all[:, c + 1:c + 2], in0=n_all[:, c:c + 1],
                                             scalar=keep[:, c, P - 1:P], in1=pair[2][:, 1, 3 * P + c:3 * P + c + 1],
                                             op0=ALU.mult, op1=ALU.add).then_inc(dve_done, 1)
                    t.e.wait_ge(dve_done, t.next(dve_done))
                t.e.sem_inc(pair_free[2], 1)
                t.e.sem_inc(states_ready, 1)
                t.e.wait_ge(num_ready, t.next(num_ready))
                t.e.tensor_copy(den[:, 0, :], pair[2][:, 0, 0:NC]).then_inc(dve_done, 1)
                t.e.wait_ge(dve_done, t.next(dve_done))
                t.e.sem_inc(pair_free[2], 1)
                t.e.scalar_tensor_tensor(out=den[:, 1, :], in0=den[:, 0, :], scalar=-1.0, in1=den[:, 0, :],
                                         op0=ALU.mult, op1=ALU.max).then_inc(dve_done, 1)
                t.e.wait_ge(dve_done, t.next(dve_done))
                t.e.tensor_tensor(den[:, 0, :], den[:, 1, :],
                                  gate_cols[:, 2, :, bass.ds(i, 1)].rearrange("p c a -> p (c a)"), ALU.max).then_inc(dve_done, 1)
                t.e.wait_ge(dve_done, t.next(dve_done))
                t.e.reciprocal(den[:, 1, :], den[:, 0, :]).then_inc(dve_done, 1)
                t.e.wait_ge(dve_done, t.next(dve_done))
                t.e.tensor_tensor(h_tok, pair_chunks(3),
                                  den[:, 1, :].rearrange("p (c a) -> p c a", a=1).to_broadcast([P, NC, P]), ALU.mult).then_inc(dve_done, 1)
                t.e.wait_ge(dve_done, t.next(dve_done))
                t.e.sem_inc(pair_free[3], 1)
                t.e.tensor_tensor(kw_tok, h_tok, h_tok, ALU.mult).then_inc(dve_done, 1)
                t.e.wait_ge(dve_done, t.next(dve_done))
                t.e.tensor_reduce(den[:, 2, :], kw_tok, AX.X, ALU.add).then_inc(dve_done, 1)
                t.e.wait_ge(dve_done, t.next(dve_done))
                t.e.sem_inc(h_squared, 1)
                t.e.wait_ge(h_rstd, t.next(h_rstd))
                t.e.tensor_tensor(h_tok, h_tok, den[:, 3, :].rearrange("p (c a) -> p c a", a=1).to_broadcast([P, NC, P]),
                                  ALU.mult).then_inc(dve_done, 1)
                t.e.wait_ge(dve_done, t.next(dve_done))
                t.e.sem_inc(h_ready, 1)
                t.e.wait_ge(h_turned, t.next(h_turned))
                t.e.wait_ge(mo_tanh, t.next(mo_tanh))
                t.e.scalar_tensor_tensor(out=hm_t, in0=o_gate, scalar=1.0, in1=flat(pair[3]), op0=ALU.add,
                                         op1=ALU.mult).then_inc(dve_done, 1)
                t.e.wait_ge(dve_done, t.next(dve_done))
                t.e.sem_inc(pair_free[3], 1)
                t.e.sem_inc(gates_free, 1)
                t.e.sem_inc(hm_ready, 1)
                t.e.wait_ge(y_high, t.next(y_high))
                t.e.scalar_tensor_tensor(out=y_lo[:, 0, :], in0=hm_t, scalar=mnorm[:, bass.ds(i, 1)],
                                         in1=y_hi[:, 0, :].bitcast(F32), op0=ALU.mult,
                                         op1=ALU.subtract).then_inc(y_ready, 1)
                for j in range(2):
                    s = (7 + j) % 2
                    for m in range(4):
                        p = s + 2 * (1 - m % 2)
                        t.e.wait_ge(unit_done[s] if m == 3 else part_done[p], t.next(unit_done[s] if m == 3 else part_done[p]))
                        t.e.tensor_tensor(X[:, 4 * j + m, :], X[:, 4 * j + m, :], flat(pair[p]),
                                          ALU.add).then_inc(pair_free[p], 1)
            t.loop(MH, body)
            t.e.drain().then_inc(resid_ready, 1)

        def act_ab(t):
            def body(i):
                act_tanh(t)
                act_probs(t, 0)
                t.e.wait_ge(vd_here, t.next(vd_here))
                for j, (a, b) in zip((4, 5, 6), ((1, 3), (3, 6), (6, 8))):
                    if j == 4:
                        act_tanh(t)
                    for qb in range(a, b):
                        act_values(t, qb - 1)
                        act_probs(t, qb)
                act_values(t, NC - 1)
                t.e.activation(prob[0], o_t, ACT.Square).then_inc(o_squared, 1)
                t.e.wait_ge(o_sum, t.next(o_sum))
                t.e.activation(prob[1], flat(pair[2]), ACT.Ln, scale=1.0 / DH, bias=eps_col[:, 0:1]).then_inc(act_done, 1)
                t.e.wait_ge(act_done, t.next(act_done))
                t.e.sem_inc(pair_free[2], 1)
                t.e.activation(prob[1], prob[1], ACT.Exp, scale=-0.5).then_inc(o_rstd, 1)
                t.e.wait_ge(o_normed, t.next(o_normed))
                t.e.activation(y_hi[:, 1, :], o_t, ACT.Copy, scale=dnorm[:, bass.ds(i, 1)]).then_inc(y_high, 1)
                t.e.wait_ge(decay_ready, t.next(decay_ready))
                t.e.activation(gate_w, gate_w, ACT.Exp).then_inc(decay_exp, 1)
                t.e.wait_ge(v_turned, t.next(v_turned))
                t.e.activation(v_tok, pair_chunks(2), ACT.Copy).then_inc(act_done, 1)
                t.e.wait_ge(act_done, t.next(act_done))
                t.e.sem_inc(pair_free[2], 1)
                t.e.sem_inc(v_tok_ready, 1)
                t.e.wait_ge(mo_ready, t.next(mo_ready))
                t.e.wait_ge(qk_done, t.next(qk_done))
                t.e.wait_ge(k_turned, t.next(k_turned))
                t.e.activation(o_gate, conv_in[:, 3:3 + T], ACT.Tanh, scale=0.5).then_inc(mo_tanh, 1)
                t.e.wait_ge(h_squared, t.next(h_squared))
                t.e.activation(den[:, 3, :], den[:, 2, :], ACT.Ln, scale=1.0 / DH, bias=eps_col[:, 0:1]).then_inc(act_done, 1)
                t.e.wait_ge(act_done, t.next(act_done))
                t.e.activation(den[:, 3, :], den[:, 3, :], ACT.Exp, scale=-0.5).then_inc(h_rstd, 1)
                t.e.wait_ge(hm_ready, t.next(hm_ready))
                t.e.activation(y_hi[:, 0, :], hm_t, ACT.Copy, scale=mnorm[:, bass.ds(i, 1)]).then_inc(y_high, 1)
            t.loop(MH, body)

        C_Z, C_X, C_B, C_C = 0, INNER, 2 * INNER, 2 * INNER + G * NS
        C_DT = C_C + G * NS
        M_B, M_C = INNER // P, INNER // P + G

        c_t, b_t = cut(0), cut(1)
        x_t = [cut(2), cut(3)]
        z_t = [cut(4), cut(5)]
        b_tok = chunks(cut(6))
        x_dt = cut(7, 2).rearrange("p (c e) -> p c e", c=NC)
        x_w = cut(9, 2).rearrange("p (c e) -> p c e", c=NC)
        s_all = x_w
        cb = cut(11)
        mix = [cut(12), cut(13)]
        ssm_y, ssm_th = cut(9), cut(10)
        y_t = [b_t, cut(6)]
        exp_a = [conv_in[:, 3:3 + T], cb]
        dt_row, dta_row, a_row, ea_row = cut(0), cut(1), cut(2), cut(3)
        na_row, wa_row, u_row, l_row, rs_row = cut(4), cut(5), cut(6), cut(7), cut(8)
        dt_raw = cut(13)[:, 0:KD * SH].rearrange("p (k n) -> p k n", k=KD)

        def sp_ssm_small(t):
            w = ssm_w_in[0].rearrange("(k p) n -> p k n", p=P)
            col = dict(allow_slow_non_contiguous=True)
            t.skip(resid_ready, ssm_at)
            t.e.wait_ge(resid_ready, t.next(resid_ready))
            for dst, src in (
                    (dt_raw, w[:, :, C_DT:C_DT + SH]),
                    (sconv_w[:, :, :], ssm_conv_w[0].rearrange("j (m p) -> p j m", p=P)),
                    (sconv_b[:, :], ssm_conv_b[0].rearrange("(m p) -> p m", p=P)),
                    (dt_bias[:, 0:1], ssm_dt_bias[0].rearrange("(p a) -> p a", a=1)),
                    (dt_bias[:, 1:2], ssm_a_log[0].rearrange("(p a) -> p a", a=1)),
                    (skip_d[0:SP_, :], ssm_d.rearrange("a (m b) -> a b m", b=2)[:, 0, :].to_broadcast([SP_, SH // 2])),
                    (skip_d[SP_:P, :], ssm_d.rearrange("a (m b) -> a b m", b=2)[:, 1, :].to_broadcast([SP_, SH // 2])),
                    (snorm[:, :], ssm_norm_g[0].rearrange("(m p) -> p m", p=P))):
                t.e.dma_start(dst, src, **col).then_inc(ssm_small, 16)

        SSM_SMALL = 8 * 16

        def sp_ssm(t):
            w = ssm_w_in[0].rearrange("(k p) n -> p k n", p=P)
            wo = ssm_w_out[0].rearrange("(q a p) n -> q p a n", a=2, p=P)
            t.e.wait_ge(srows_made, t.next(srows_made, 2))
            t.e.dma_start(ssm_rows[0], a_row[0:SH, :]).then_inc(srows_kept, 16)
            t.e.dma_start(ssm_rows[1], ea_row[0:SH, :]).then_inc(srows_kept, 16)
            t.e.dma_start(ssm_last[:, :], last_a[:, :]).then_inc(srows_kept, 16)
            t.e.wait_ge(srows_kept, t.next(srows_kept, 48))
            t.e.dma_start(keep_a[:, :], ssm_last.rearrange("(a h) c -> a (h c)", a=1).to_broadcast([P, SH * NC])
                          ).then_inc(keep_here, 16)

            def body(i):
                def unit(s, at):
                    load_unit(t, s, w_raw[:, s, :].rearrange("p (k n) -> p k n", k=KD), w[:, :, at])

                def row(m, r):
                    t.e.wait_ge(mix_free[m], t.next(mix_free[m]))
                    t.e.sem_inc(begun, 1)
                    t.e.dma_start(mix[m], ssm_rows[0, bass.ds(i * HPG + r, 1), :].to_broadcast([P, T])).then_inc(mix_here[m], 16)

                def exps(m):
                    t.e.wait_ge(exp_free[m], t.next(exp_free[m]))
                    t.e.sem_inc(begun, 1)
                    for b in range(2):
                        t.e.dma_start(exp_a[m][b * SP_:(b + 1) * SP_, :],
                                      ssm_rows[1, bass.ds(i * HPG + 2 * m + b, 1), :].to_broadcast([SP_, T])
                                      ).then_inc(exp_here[m], 16)

                unit(0, bass.ds(i * NS + C_B, P))
                unit(1, bass.ds(i * NS + C_C, P))
                unit(0, bass.ds(i * GW + C_X, P))
                unit(1, bass.ds(i * GW + C_X + P, P))
                row(0, 0)
                row(1, 1)
                unit(0, bass.ds(i * GW + C_Z, P))
                unit(1, bass.ds(i * GW + C_Z + P, P))
                exps(0)
                for j in range(2):
                    load_unit(t, j, w_raw[:, j, :].rearrange("p (a n) -> p a n", a=2),
                              wo[bass.ds(i, 1), :, :, j * HALF:(j + 1) * HALF].rearrange("q p a n -> (q p) a n"))
                row(0, 2)
                row(1, 3)
                exps(1)
            t.loop(G, body)

        def pe_steps(t):
            t.e.wait_ge(gate_split, t.next(gate_split))
            t.e.wait_ge(pair_free[2], t.next(pair_free[2]))
            for k in range(KD):
                for w, r in ((gate_hi, HH), (gate_hi, HL), (gate_lo, HH)):
                    for n in range(2):
                        ins = t.e.matmul(pair[2][0:SH, n, :], w[:, k, 0:SH], r[:, k, n * HALF:(n + 1) * HALF],
                                         start=(k == 0 and w is gate_hi and r is HH),
                                         stop=(k == KD - 1 and w is gate_lo))
            ins.then_inc(gates_done, 1)
            t.e.wait_ge(rows_turn, t.next(rows_turn))
            t.e.wait_ge(pair_free[3], t.next(pair_free[3]))
            for q, row in enumerate((dt_row, na_row, wa_row)):
                for c in range(NC):
                    at = q * NC * SH + c * SH
                    ins = t.e.transpose(pair[3][:, at // HALF, at % HALF:at % HALF + SH], row[0:SH, c * P:(c + 1) * P],
                                        ident[0:SH, 0:SH])
            ins.then_inc(rows_turned, 1)

        def dve_steps(t):
            t.e.wait_ge(ssm_small, t.next(ssm_small, SSM_SMALL))
            t.e.tensor_copy(gate_hi[:, :, 0:SH], dt_raw).then_inc(dve_done, 1)
            t.e.wait_ge(dve_done, t.next(dve_done))
            t.e.tensor_tensor(gate_lo[:, :, 0:SH], dt_raw, gate_hi[:, :, 0:SH].bitcast(F32),
                              ALU.subtract).then_inc(gate_split, 1)
            t.e.tensor_scalar(sconv_w[:, :, :], sconv_w[:, :, :], 0.5, None, ALU.mult).then_inc(dve_done, 1)
            t.e.wait_ge(dve_done, t.next(dve_done))
            t.e.tensor_scalar(sconv_b[:, :], sconv_b[:, :], 0.5, None, ALU.mult).then_inc(dve_done, 1)
            t.e.wait_ge(dve_done, t.next(dve_done))
            t.e.wait_ge(r_ready, t.next(r_ready))
            t.e.wait_ge(gates_done, t.next(gates_done))
            h = slice(0, SH)
            t.e.tensor_tensor(dt_row[h, :], flat(pair[2])[h, :], R[h, :], ALU.mult).then_inc(dve_done, 1)
            t.e.wait_ge(dve_done, t.next(dve_done))
            t.e.sem_inc(pair_free[2], 1)
            t.e.tensor_scalar(dt_row[h, :], dt_row[h, :], dt_bias[:, 0:1], None, ALU.add).then_inc(dve_done, 1)
            t.e.wait_ge(dve_done, t.next(dve_done))
            t.e.sem_inc(f_ready, 1)
            t.e.wait_ge(f_exp, t.next(f_exp))
            t.e.tensor_scalar(rs_row[h, :], u_row[h, :], 1.0, None, ALU.add).then_inc(dve_done, 1)
            t.e.wait_ge(dve_done, t.next(dve_done))
            t.e.sem_inc(f_ready, 1)
            t.e.tensor_scalar(rs_row[h, :], rs_row[h, :], -1.0, TINY, ALU.add, ALU.add).then_inc(dve_done, 1)
            t.e.wait_ge(dve_done, t.next(dve_done))
            t.e.reciprocal(rs_row[h, :], rs_row[h, :]).then_inc(dve_done, 1)
            t.e.wait_ge(dve_done, t.next(dve_done))
            t.e.wait_ge(f_log, t.next(f_log))
            t.e.scalar_tensor_tensor(out=l_row[h, :], in0=l_row[h, :], scalar=TINY, in1=rs_row[h, :],
                                     op0=ALU.add, op1=ALU.mult).then_inc(dve_done, 1)
            t.e.wait_ge(dve_done, t.next(dve_done))
            t.e.tensor_tensor(l_row[h, :], l_row[h, :], u_row[h, :], ALU.mult).then_inc(dve_done, 1)
            t.e.wait_ge(dve_done, t.next(dve_done))
            t.e.scalar_tensor_tensor(out=dt_row[h, :], in0=dt_row[h, :], scalar=0.0, in1=l_row[h, :],
                                     op0=ALU.max, op1=ALU.add).then_inc(dve_done, 1)
            t.e.wait_ge(dve_done, t.next(dve_done))
            t.e.tensor_scalar(dta_row[h, :], dt_row[h, :], dt_bias[:, 1:2], -1.0, ALU.mult, ALU.mult).then_inc(dve_done, 1)
            t.e.wait_ge(dve_done, t.next(dve_done))
            t.e.memset(rs_row[h, :], 1.0).then_inc(dve_done, 1)
            t.e.wait_ge(dve_done, t.next(dve_done))
            t.e.memset(chunks(rs_row)[h, :, 0:1], 0.0).then_inc(dve_done, 1)
            t.e.wait_ge(dve_done, t.next(dve_done))
            t.e.tensor_tensor_scan(a_row[h, :], rs_row[h, :], dta_row[h, :], 0.0, ALU.mult, ALU.add).then_inc(dve_done, 1)
            t.e.wait_ge(dve_done, t.next(dve_done))
            t.e.tensor_tensor(chunks(wa_row)[h, :, :], chunks(a_row)[h, :, P - 1:P].to_broadcast([SH, NC, P]),
                              chunks(a_row)[h, :, :], ALU.subtract).then_inc(dve_done, 1)
            t.e.wait_ge(dve_done, t.next(dve_done))
            t.e.tensor_scalar(na_row[h, :], a_row[h, :], -1.0, None, ALU.mult).then_inc(dve_done, 1)
            t.e.wait_ge(dve_done, t.next(dve_done))
            t.e.sem_inc(rows_exp, 1)
            t.e.wait_ge(ea_ready, t.next(ea_ready))
            t.e.tensor_copy(last_a[:, :].rearrange("p (c a) -> p c a", a=1), chunks(ea_row)[h, :, P - 1:P]).then_inc(srows_made, 1)
            t.e.wait_ge(rows_turned, t.next(rows_turned))
            t.e.tensor_copy(step_cols.rearrange("p q c h -> p (q c h)"), flat(pair[3])[:, 0:3 * NC * SH]).then_inc(dve_done, 1)
            t.e.wait_ge(dve_done, t.next(dve_done))
            t.e.sem_inc(pair_free[3], 1)

        def act_steps(t):
            h = slice(0, SH)
            t.e.wait_ge(ssm_small, t.next(ssm_small, SSM_SMALL))
            t.e.activation(dt_bias[:, 1:2], dt_bias[:, 1:2], ACT.Exp).then_inc(begun, 1)
            t.e.wait_ge(f_ready, t.next(f_ready))
            t.e.activation(u_row[h, :], dt_row[h, :], ACT.Abs).then_inc(act_done, 1)
            t.e.wait_ge(act_done, t.next(act_done))
            t.e.activation(u_row[h, :], u_row[h, :], ACT.Exp, scale=-1.0).then_inc(act_done, 1)
            t.e.wait_ge(act_done, t.next(act_done))
            t.e.sem_inc(f_exp, 1)
            t.e.wait_ge(f_ready, t.next(f_ready))
            t.e.activation(l_row[h, :], u_row[h, :], ACT.Ln, bias=1.0).then_inc(f_log, 1)
            t.e.wait_ge(rows_exp, t.next(rows_exp))
            t.e.activation(wa_row[h, :], wa_row[h, :], ACT.Exp).then_inc(act_done, 1)
            t.e.wait_ge(act_done, t.next(act_done))
            t.e.sem_inc(rows_turn, 1)
            t.e.activation(ea_row[h, :], a_row[h, :], ACT.Exp).then_inc(act_done, 1)
            t.e.wait_ge(act_done, t.next(act_done))
            t.e.sem_inc(ea_ready, 1)
            t.e.sem_inc(srows_made, 1)

        def pe_ssm(t):
            def body(i):
                project(t, 0)
                project(t, 1)
                project(t, 0)
                t.e.wait_ge(bc_ready, t.next(bc_ready, 2))
                turn(t, 2, lambda c: b_t[:, c * P:(c + 1) * P]).then_inc(b_turned, 1)
                t.e.wait_ge(pair_free[3], t.next(pair_free[3]))
                for c in range(NC):
                    ins = t.e.matmul(turned(3, c), b_t[:, c * P:(c + 1) * P], c_t[:, c * P:(c + 1) * P],
                                     start=True, stop=True)
                ins.then_inc(cb_done, 1)
                project(t, 1)
                project(t, 0)
                for m in range(2):
                    t.e.wait_ge(x_ready, t.next(x_ready))
                    turn(t, 2 + m, lambda c: x_t[m][:, c * P:(c + 1) * P]).then_inc(x_turned, 1)
                project(t, 1)
                t.e.wait_ge(b_tok_ready, t.next(b_tok_ready))
                t.e.wait_ge(xw_ready, t.next(xw_ready))
                for m in range(2):
                    t.e.wait_ge(pair_free[2 + m], t.next(pair_free[2 + m]))
                    for c in range(NC - 1):
                        ins = t.e.matmul(turned(2 + m, c), b_tok[:, c, :], x_w[:, c, m * P:(m + 1) * P],
                                         start=True, stop=True)
                    ins.then_inc(state_parts, 1)
                for m in range(2):
                    t.e.wait_ge(pair_free[2], t.next(pair_free[2]))
                    for b in range(2):
                        t.e.wait_ge(mix_ready, t.next(mix_ready))
                        for c in range(NC):
                            ins = t.e.matmul(turned(2, c)[b * SP_:(b + 1) * SP_, :],
                                             x_dt[:, c, m * P + b * SP_:m * P + (b + 1) * SP_],
                                             mix[b][:, c * P:(c + 1) * P], start=True, stop=True)
                    ins.then_inc(y_inner, 1)
                    if m == 0:
                        t.e.wait_ge(s_ready, t.next(s_ready))
                    t.e.wait_ge(pair_free[3], t.next(pair_free[3]))
                    for c in range(1, NC):
                        ins = t.e.matmul(turned(3, c), s_all[:, c, m * P:(m + 1) * P], c_t[:, c * P:(c + 1) * P],
                                         start=True, stop=True)
                    ins.then_inc(y_outer, 1)
                t.e.wait_ge(y_squares, t.next(y_squares))
                t.e.wait_ge(pair_free[2], t.next(pair_free[2]))
                for n in range(2):
                    ins = t.e.matmul(pair[2][:, n, :], ones[:, :], mix[0][:, n * HALF:(n + 1) * HALF],
                                     start=True, stop=True)
                ins.then_inc(y_sum, 1)
                t.e.wait_ge(y_ready, t.next(y_ready, 2))
                for j in range(2):
                    t.e.wait_ge(w_split[j], t.next(w_split[j]))
                    for m in range(4):
                        p = j + 2 * (1 - m % 2)
                        t.e.wait_ge(pair_free[p], t.next(pair_free[p]))
                        for k in range(2):
                            ins = products(t, pair[p], P, j, k * HALF + m * P, y_hi[:, k, :], y_lo[:, k, :],
                                           k == 0, k == 1)
                        ins.then_inc(unit_done[j] if m == 3 else part_done[p], 1)
            t.loop(G, body)

        def dve_sconv(t, out, s, m):
            scaled(t, conv_in[:, 3:3 + T], s)
            t.e.tensor_scalar(ssm_y, conv_in[:, 3:3 + T], sconv_w[:, 3, m], sconv_b[:, m], ALU.mult, ALU.add).then_inc(dve_done, 1)
            t.e.wait_ge(dve_done, t.next(dve_done))
            for tap in range(3):
                t.e.scalar_tensor_tensor(out=ssm_y, in0=conv_in[:, tap:tap + T], scalar=sconv_w[:, tap, m],
                                         in1=ssm_y, op0=ALU.mult, op1=ALU.add).then_inc(dve_done, 1)
                t.e.wait_ge(dve_done, t.next(dve_done))
            t.e.sem_inc(conv_ready, 1)
            t.e.wait_ge(tanh_ready, t.next(tanh_ready))
            t.e.scalar_tensor_tensor(out=out, in0=ssm_th, scalar=1.0, in1=ssm_y, op0=ALU.add, op1=ALU.mult).then_inc(dve_done, 1)
            t.e.wait_ge(dve_done, t.next(dve_done))

        def dve_ssm(t):
            t.e.wait_ge(keep_here, t.next(keep_here, 16))

            def body(i):
                def by_head(q, lo, n):
                    return step_cols[:, q, :, bass.ds(i * HPG + lo, n)].rearrange("p c (r a) -> p c r a", a=1)

                def decay(r):
                    m = r % 2
                    t.e.wait_ge(mix_here[m], t.next(mix_here[m], 16))
                    t.e.tensor_tensor(chunks(mix[m]), chunks(mix[m]),
                                      step_cols[:, 1, :, bass.ds(i * HPG + r, 1)].to_broadcast([P, NC, P]), ALU.add).then_inc(dve_done, 1)
                    t.e.wait_ge(dve_done, t.next(dve_done))
                    t.e.tensor_scalar(mix[m], mix[m], 0.0, None, ALU.min).then_inc(dve_done, 1)
                    t.e.wait_ge(dve_done, t.next(dve_done))
                    t.e.sem_inc(decay_ready, 1)

                def weights(r):
                    t.e.wait_ge(decay_exp, t.next(decay_exp))
                    t.e.tensor_tensor(mix[r % 2], mix[r % 2], cb, ALU.mult).then_inc(dve_done, 1)
                    t.e.wait_ge(dve_done, t.next(dve_done))
                    t.e.sem_inc(mix_ready, 1)

                def output(m):
                    t.e.wait_ge(exp_here[m], t.next(exp_here[m], 32))
                    t.e.wait_ge(y_inner, t.next(y_inner))
                    if m == 0:
                        t.e.sem_inc(mix_free[0], 1)
                        t.e.sem_inc(mix_free[1], 1)
                    t.e.scalar_tensor_tensor(out=y_t[m], in0=x_t[m], scalar=skip_d[:, bass.ds(i * 2 + m, 1)],
                                             in1=flat(pair[2]), op0=ALU.mult, op1=ALU.add).then_inc(dve_done, 1)
                    t.e.wait_ge(dve_done, t.next(dve_done))
                    t.e.sem_inc(pair_free[2], 1)
                    t.e.wait_ge(y_outer, t.next(y_outer))
                    t.e.tensor_tensor(x_t[m][:, P:T], flat(pair[3])[:, P:T], exp_a[m][:, P:T], ALU.mult).then_inc(dve_done, 1)
                    t.e.wait_ge(dve_done, t.next(dve_done))
                    t.e.sem_inc(pair_free[3], 1)
                    t.e.tensor_tensor(y_t[m][:, P:T], y_t[m][:, P:T], x_t[m][:, P:T], ALU.add).then_inc(dve_done, 1)
                    t.e.wait_ge(dve_done, t.next(dve_done))

                dve_sconv(t, b_t, 0, bass.ds(i + M_B, 1))
                t.e.sem_inc(bc_ready, 1)
                dve_sconv(t, c_t, 1, bass.ds(i + M_C, 1))
                t.e.sem_inc(bc_ready, 1)
                dve_sconv(t, x_t[0], 0, bass.ds(i * 2, 1))
                t.e.sem_inc(x_ready, 1)
                t.e.wait_ge(cb_done, t.next(cb_done))
                t.e.scalar_tensor_tensor(out=chunks(cb), in0=causal[:, :, :].to_broadcast([P, NC, P]), scalar=0.0,
                                         in1=pair_chunks(3), op0=ALU.is_ge, op1=ALU.mult).then_inc(dve_done, 1)
                t.e.wait_ge(dve_done, t.next(dve_done))
                t.e.sem_inc(pair_free[3], 1)
                dve_sconv(t, x_t[1], 1, bass.ds(i * 2 + 1, 1))
                t.e.sem_inc(x_ready, 1)
                t.e.sem_inc(exp_free[0], 1)
                decay(0)
                decay(1)
                scaled(t, z_t[0], 0)
                for m in range(2):
                    t.e.wait_ge(x_turned, t.next(x_turned))
                    t.e.tensor_tensor(x_dt[:, :, m * P:(m + 1) * P].rearrange("p c (r e) -> p c r e", r=2),
                                      pair_chunks(2 + m).rearrange("p c (r e) -> p c r e", r=2),
                                      by_head(0, 2 * m, 2).to_broadcast([P, NC, 2, SP_]), ALU.mult).then_inc(dve_done, 1)
                    t.e.wait_ge(dve_done, t.next(dve_done))
                    t.e.sem_inc(pair_free[2 + m], 1)
                t.e.tensor_tensor(x_w.rearrange("p c (r e) -> p c r e", r=HPG),
                                  x_dt.rearrange("p c (r e) -> p c r e", r=HPG),
                                  by_head(2, 0, HPG).to_broadcast([P, NC, HPG, SP_]), ALU.mult).then_inc(dve_done, 1)
                t.e.wait_ge(dve_done, t.next(dve_done))
                t.e.sem_inc(xw_ready, 1)
                weights(0)
                weights(1)
                scaled(t, z_t[1], 1)
                t.e.wait_ge(state_parts, t.next(state_parts, 2))
                for m in range(2):
                    t.e.tensor_copy(s_all[:, 1, m * P:(m + 1) * P], turned(2 + m, 0)).then_inc(dve_done, 1)
                for m in range(2):
                    t.e.wait_ge(dve_done, t.next(dve_done))
                for c in range(1, NC - 1):
                    for r in range(HPG):
                        part = slice(r * SP_, (r + 1) * SP_)
                        t.e.scalar_tensor_tensor(out=s_all[:, c + 1, part], in0=s_all[:, c, part],
                                                 scalar=keep_a[:, bass.ds(i * HPG * NC + r * NC + c, 1)],
                                                 in1=turned(2 + r // 2, c)[:, r % 2 * SP_:(r % 2 + 1) * SP_],
                                                 op0=ALU.mult, op1=ALU.add).then_inc(dve_done, 1)
                    for r in range(HPG):
                        t.e.wait_ge(dve_done, t.next(dve_done))
                for m in range(2):
                    t.e.sem_inc(pair_free[2 + m], 1)
                t.e.sem_inc(s_ready, 1)
                output(0)
                decay(2)
                decay(3)
                weights(2)
                weights(3)
                t.e.sem_inc(exp_free[1], 1)
                output(1)
                t.e.sem_inc(y_made, 1)
                for m in range(2):
                    t.e.wait_ge(z_tanh, t.next(z_tanh))
                    t.e.scalar_tensor_tensor(out=z_t[m], in0=mix[m], scalar=1.0, in1=z_t[m], op0=ALU.add, op1=ALU.mult).then_inc(dve_done, 1)
                    t.e.wait_ge(dve_done, t.next(dve_done))
                    t.e.scalar_tensor_tensor(out=y_t[m], in0=z_t[m], scalar=0.5, in1=y_t[m], op0=ALU.mult, op1=ALU.mult).then_inc(dve_done, 1)
                    t.e.wait_ge(dve_done, t.next(dve_done))
                    t.e.sem_inc(y_gated, 1)
                t.e.wait_ge(sq_done, t.next(sq_done, 2))
                t.e.tensor_tensor(mix[0], mix[0], mix[1], ALU.add).then_inc(dve_done, 1)
                t.e.wait_ge(dve_done, t.next(dve_done))
                t.e.sem_inc(y_squares, 1)
                t.e.wait_ge(y_rstd, t.next(y_rstd))
                for m in range(2):
                    t.e.tensor_tensor(y_t[m], y_t[m], mix[1], ALU.mult).then_inc(dve_done, 1)
                    t.e.wait_ge(dve_done, t.next(dve_done))
                    t.e.sem_inc(y_normed, 1)
                for m in range(2):
                    t.e.wait_ge(y_high, t.next(y_high))
                    t.e.scalar_tensor_tensor(out=y_lo[:, m, :], in0=y_t[m], scalar=snorm[:, bass.ds(i * 2 + m, 1)],
                                             in1=y_hi[:, m, :].bitcast(F32), op0=ALU.mult,
                                             op1=ALU.subtract).then_inc(y_ready, 1)
                for m in range(2):
                    t.e.sem_inc(mix_free[m], 1)
                for j in range(2):
                    for m in range(4):
                        p = j + 2 * (1 - m % 2)
                        t.e.wait_ge(unit_done[j] if m == 3 else part_done[p], t.next(unit_done[j] if m == 3 else part_done[p]))
                        t.e.tensor_tensor(X[:, 4 * j + m, :], X[:, 4 * j + m, :], flat(pair[p]),
                                          ALU.add).then_inc(pair_free[p], 1)
            t.loop(G, body)
            t.e.drain().then_inc(resid_ready, 1)

        def act_ssm(t):
            def body(i):
                def tanh():
                    t.e.wait_ge(conv_ready, t.next(conv_ready))
                    t.e.activation(ssm_th, ssm_y, ACT.Tanh).then_inc(tanh_ready, 1)

                def exp(r):
                    t.e.wait_ge(decay_ready, t.next(decay_ready))
                    t.e.activation(mix[r % 2], mix[r % 2], ACT.Exp).then_inc(decay_exp, 1)

                tanh()
                tanh()
                tanh()
                t.e.wait_ge(b_turned, t.next(b_turned))
                t.e.activation(b_tok, pair_chunks(2), ACT.Copy).then_inc(act_done, 1)
                t.e.wait_ge(act_done, t.next(act_done))
                t.e.sem_inc(pair_free[2], 1)
                t.e.sem_inc(b_tok_ready, 1)
                tanh()
                for r in range(HPG):
                    exp(r)
                t.e.wait_ge(y_made, t.next(y_made))
                for m in range(2):
                    t.e.activation(mix[m], z_t[m], ACT.Tanh, scale=0.5).then_inc(z_tanh, 1)
                for m in range(2):
                    t.e.wait_ge(y_gated, t.next(y_gated))
                    t.e.activation(mix[m], y_t[m], ACT.Square).then_inc(sq_done, 1)
                t.e.wait_ge(y_sum, t.next(y_sum))
                t.e.activation(mix[1], flat(pair[2]), ACT.Ln, scale=1.0 / GW, bias=eps_col[:, 0:1]).then_inc(act_done, 1)
                t.e.wait_ge(act_done, t.next(act_done))
                t.e.sem_inc(pair_free[2], 1)
                t.e.activation(mix[1], mix[1], ACT.Exp, scale=-0.5).then_inc(y_rstd, 1)
                for m in range(2):
                    t.e.wait_ge(y_normed, t.next(y_normed))
                    t.e.activation(y_hi[:, m, :], y_t[m], ACT.Copy, scale=snorm[:, bass.ds(i * 2 + m, 1)]).then_inc(y_high, 1)
            t.loop(G, body)

        final_row = cut(5)
        y_out = cut(6, 2).rearrange("p (b n) -> p b n", b=2)
        sq_out = cut(8, 2).rearrange("p (b n) -> p b n", b=2)

        def pe_final(t):
            t.e.wait_ge(resid_ready, t.next(resid_ready))
            for c in range(NC):
                b = c % 2
                t.e.wait_ge(pair_free[b], t.next(pair_free[b]))
                for k in range(KD):
                    ins = t.e.transpose(pair[b][:, k // 4, k % 4 * P:(k % 4 + 1) * P],
                                        X[:, k, c * P:(c + 1) * P], ident[:, :])
                ins.then_inc(turned_done[b], 1)

        def act_final(t):
            for c in range(NC):
                b = c % 2
                t.e.wait_ge(turned_done[b], t.next(turned_done[b]))
                t.e.activation(sq_out[:, b, :], pair[b][:, :, :].rearrange("p a n -> p (a n)"), ACT.Square,
                               accum_out=ss[:, c:c + 1]).then_inc(act_done, 1)
                t.e.wait_ge(act_done, t.next(act_done))
                t.e.activation(rstd[:, c:c + 1], ss[:, c:c + 1], ACT.Ln, scale=1.0 / D,
                               bias=eps_col[:, 0:1]).then_inc(act_done, 1)
                t.e.wait_ge(act_done, t.next(act_done))
                t.e.activation(rstd[:, c:c + 1], rstd[:, c:c + 1], ACT.Exp, scale=-0.5).then_inc(rstd_ready, 1)

        def dve_final(t):
            t.e.wait_ge(row_gain, t.next(row_gain, 16))
            for c in range(NC):
                b = c % 2
                t.e.wait_ge(rstd_ready, t.next(rstd_ready))
                if c >= 2:
                    t.e.wait_ge(stored, t.next(stored, 16))
                t.e.scalar_tensor_tensor(out=y_out[:, b, :], in0=pair[b][:, :, :].rearrange("p a n -> p (a n)"),
                                         scalar=rstd[:, c:c + 1], in1=final_row, op0=ALU.mult,
                                         op1=ALU.mult).then_inc(dve_done, 1)
                t.e.wait_ge(dve_done, t.next(dve_done))
                t.e.sem_inc(pair_free[b], 1)
                t.e.sem_inc(rows_ready, 1)

        def sp_final(t):
            t.e.wait_ge(resid_ready, t.next(resid_ready))
            t.e.dma_start(final_row, final_g.rearrange("(a n) -> a n", a=1).to_broadcast([P, D])).then_inc(row_gain, 16)
            for c in range(NC):
                t.e.wait_ge(rows_ready, t.next(rows_ready))
                t.e.dma_start(out[0, c * P:(c + 1) * P, :], y_out[:, c % 2, :]).then_inc(stored, 16)
                t.e.wait_ge(stored, t.next(stored, 16))

        block = ctx.enter_context(nc.Block())
        n_phases = len(phases)

        @block.sync
        def _(sp):
            t = Tally(sp)
            for i, g in enumerate((norm_mix_g, norm_mlp_g)):
                for l in range(2):
                    sp.dma_start(gains[:, 2 * i + l, :], g[l].rearrange("(k p) -> p k", p=P),
                                 allow_slow_non_contiguous=True).then_inc(small_loaded, 16)
            sp_x(t)
            for ph in phases:
                if ph == "ab":
                    sp_ab_small(t)
                    sp_ab(t)
                if ph == "ssm":
                    sp_ssm_small(t)
                    sp_ssm(t)
                if ph[:3] == "mlp":
                    sp_mlp(t, int(ph[3]))
            t.skip(resid_ready, n_phases - (ssm_at + 1 if "ssm" in phases else 0))
            sp_final(t)

        @block.gpsimd
        def _(pool):
            t = Tally(pool)
            pool.memset(ones[:, :], 1.0)
            pool.memset(conv_in[:, 0:3], 0.0)
            pool.memset(eps_col[:, :], EPS)
            pool.memset(ident[:, :], 0.0).then_inc(pool_done, 1)
            t.e.wait_ge(pool_done, t.next(pool_done))
            pool.memset(causal[:, :, :], 0.0).then_inc(pool_done, 1)
            t.e.wait_ge(pool_done, t.next(pool_done))
            pool.affine_select(out=causal[:, 0, :], in_=causal[:, 0, :], compare_op=ALU.is_ge, fill=NEG, base=0,
                        pattern=[[1, P]], channel_multiplier=-1).then_inc(pool_done, 1)
            t.e.wait_ge(pool_done, t.next(pool_done))
            pool.affine_select(out=ident[:, :], in_=ident[:, :], compare_op=ALU.not_equal, fill=1.0, base=0,
                               pattern=[[-1, P]], channel_multiplier=1).then_inc(const_ready, 1)
            for s in range(2):
                pool.sem_inc(w_split[s], 1)
                pool.sem_inc(unit_done[s], 1)
                pool.sem_inc(x_read[s], 1)
            for s in range(4):
                pool.sem_inc(pair_free[s], 1)
            pool.sem_inc(sq_used, 2)
            pool.sem_inc(gates_free, 1)
            for s in range(2):
                pool.sem_inc(mix_free[s], 1)
            for ph in phases:
                if ph == "ab":
                    pool_ab(t)
                    pool_units(t, MH, (0, 1, 0, 1, 0, 1, 0, 1, 0))
                if ph == "ssm":
                    pool_units(t, G, (0, 1) * 4)
                if ph[:3] == "mlp":
                    pool_units(t, N_FB, (0, 1) * 4)

        @block.tensor
        def _(pe):
            t = Tally(pe)
            for s in range(2):
                t.skip(w_split[s])
            pe_x(t)
            for ph in phases:
                pe_norm(t)
                if ph == "ab":
                    pe_gates(t)
                    pe_ab(t)
                if ph == "ssm":
                    pe_steps(t)
                    pe_ssm(t)
                if ph[:3] == "mlp":
                    pe_mlp(t)
            t.skip(resid_ready, n_phases)
            pe_final(t)

        @block.scalar
        def _(act):
            t = Tally(act)
            t.e.wait_ge(const_ready, t.next(const_ready))
            t.e.wait_ge(small_loaded, t.next(small_loaded, 64))
            act_x(t)
            for ph in phases:
                w = {"ab": 0, "ssm": 1, "mlp0": 2, "mlp1": 3}[ph]
                act_norm(t, w, -0.5)
                if ph == "ab":
                    act_gates(t)
                    act_ab(t)
                if ph == "ssm":
                    act_steps(t)
                    act_ssm(t)
                if ph[:3] == "mlp":
                    act_mlp(t)
            act_final(t)

        @block.vector
        def _(dve):
            t = Tally(dve)
            for s in range(2):
                t.skip(unit_done[s])
            t.e.wait_ge(const_ready, t.next(const_ready))
            t.e.wait_ge(small_loaded, t.next(small_loaded, 64))
            for ph in phases:
                w = {"ab": 0, "ssm": 1, "mlp0": 2, "mlp1": 3}[ph]
                dve_norm(t, w)
                if ph == "ab":
                    dve_gates(t)
                    t.e.wait_ge(rows_kept, t.next(rows_kept, 32))
                    dve_ab(t)
                if ph == "ssm":
                    dve_steps(t)
                    dve_ssm(t)
                if ph[:3] == "mlp":
                    dve_mlp(t)
            dve_final(t)


_INS = ["x", "norm_mix_g", "norm_mlp_g", "ab_w_in", "ab_conv_w", "ab_conv_b", "ab_i_bias", "ab_f_bias",
        "ab_mnorm_g", "ab_lam_q1", "ab_lam_k1", "ab_lam_q2", "ab_lam_k2", "ab_dnorm_g", "ab_w_out", "ssm_w_in",
        "ssm_conv_w", "ssm_conv_b", "ssm_dt_bias", "ssm_a_log", "ssm_d", "ssm_norm_g", "ssm_w_out",
        "mlp_w1", "mlp_w2", "final_g"]


def kernel(**inputs):
    import numpy as _np
    import concourse.bacc as _bacc
    from concourse import mybir as _mybir
    from concourse.bass_utils import run_bass_kernel_spmd as _run

    nc = _bacc.Bacc("TRN2", target_bir_lowering=False, num_devices=1)
    arrays, args = {}, []
    for name in _INS:
        a = _np.ascontiguousarray(inputs[name])
        arrays[f"in_{name}_dram"] = a
        args.append(nc.dram_tensor(f"in_{name}_dram", a.shape, _mybir.dt.from_np(a.dtype), kind="ExternalInput").ap())
    args.append(nc.dram_tensor("out_0_dram", (1, T, D), _mybir.dt.float32, kind="ExternalOutput").ap())
    trunk(nc, *args)
    r = _run(nc, [arrays], core_ids=[0])
    return r.results[0]["out_0_dram"]
```

```python
from contextlib import ExitStack, contextmanager

import numpy as np

import concourse.bass as bass
from concourse import mybir

F32 = mybir.dt.float32
F32R = mybir.dt.float32r
ALU = mybir.AluOpType
ACT = mybir.ActivationFunctionType
AX = mybir.AxisListType

P = 128
HALF = 512
D = 1024
T = 1024
KD = D // P
NC = T // P
EPS = 1e-5
FF = 4 * D
FB = 4 * P
N_FB = FF // FB
MH, DH = 4, 128
AH, AD = 4, 64
G, HPG, SP_, NS = 8, 4, 64, 128
SH = G * HPG
INNER = SH * SP_
GW = HPG * SP_
NEG = -1.0e30
LEAST = -3.4e38
TINY = 1.0e-30
SLOPE = 0.25
LAM_INIT = 0.8 - 0.6


class Silent:

    def _take(self, *a, **k):
        return self

    dma_start = matmul = transpose = wait_ge = then_inc = sem_inc = _take
    activation = copy = tensor_copy = tensor_tensor = tensor_scalar = scalar_tensor_tensor = _take
    tensor_tensor_reduce = tensor_tensor_scan = tensor_reduce = reciprocal = memset = _take
    affine_select = drain = iota = _take


class Tally:

    def __init__(self, engine):
        self.e = engine
        self.base, self.rel, self.per, self.i = {}, {}, None, None

    def next(self, sem, by=1):
        key = sem.name
        self.rel[key] = self.rel.get(key, 0) + by
        value = self.base.get(key, 0) + self.rel[key]
        if self.i is not None:
            value = self.i * self.per[key] + value
        return value

    def skip(self, sem, by=1):
        self.rel[sem.name] = self.rel.get(sem.name, 0) + by

    def loop(self, n, body):
        engine, base = self.e, self.base
        for key, v in self.rel.items():
            base[key] = base.get(key, 0) + v
        self.rel, self.e = {}, Silent()
        body(0)
        self.per, self.rel, self.e = self.rel, {}, engine
        with engine.Fori(0, n) as i:
            self.i = i
            body(i)
        for key, v in self.per.items():
            base[key] = base.get(key, 0) + n * v
        self.rel, self.per, self.i = {}, None, None


def trunk(nc, x, norm_mix_g, norm_mlp_g, ab_w_in, ab_conv_w, ab_conv_b, ab_i_bias, ab_f_bias,
          ab_mnorm_g, ab_lam_q1, ab_lam_k1, ab_lam_q2, ab_lam_k2, ab_dnorm_g, ab_w_out, ssm_w_in,
          ssm_conv_w, ssm_conv_b, ssm_dt_bias, ssm_a_log, ssm_d, ssm_norm_g, ssm_w_out,
          mlp_w1, mlp_w2, final_g, out, phases=("ab", "mlp0", "ssm", "mlp1")):
    with ExitStack() as ctx:
        def sb(name, shape, dt=F32):
            return ctx.enter_context(nc.sbuf_tensor(name, shape, dt))

        def sem(name):
            return ctx.enter_context(nc.semaphore(name))

        X = sb("X", [P, KD, T])
        HH = sb("HH", [P, KD, T], F32R)
        HL = sb("HL", [P, KD, T], F32R)
        w_raw = sb("w_raw", [P, 2, T])
        w_hi = sb("w_hi", [P, 2, T], F32R)
        w_lo = sb("w_lo", [P, 2, T], F32R)
        ones = sb("ones", [P, P])
        ident = sb("ident", [P, P])
        R = sb("R", [P, T])
        gains = sb("gains", [P, 4, KD])
        eps_col = sb("eps_col", [P, 1])
        ss = sb("ss", [P, NC])
        rstd = sb("rstd", [P, NC])
        conv_w = sb("conv_w", [P, 4, 2 * MH])
        conv_b = sb("conv_b", [P, 2 * MH])
        gate_bias = sb("gate_bias", [36, 1])
        mnorm = sb("mnorm", [P, MH])
        dnorm = sb("dnorm", [P, AH])
        lam = sb("lam", [P, 3])
        step_cols = sb("step_cols", [P, 3, NC, SH])
        gate_cols = step_cols[:, 0, 0:3, :].rearrange("p q (c h) -> p q c h", c=NC)
        causal = sb("causal", [P, 1, P])
        m0 = sb("m0", [MH, NC])
        stat = sb("stat", [P, 2, 6])
        den = sb("den", [P, 4, NC])
        n_all = sb("n_all", [P, NC])
        conv_in = sb("conv_in", [P, T + 4])
        z_hi = sb("z_hi", [P, 4, T], F32R)
        y_hi, y_lo = z_hi[:, 0:2, :], z_hi[:, 2:4, :]
        gate_hi, gate_lo = (z_hi[:, m, 0:KD * 36].rearrange("p (k n) -> p k n", k=KD) for m in range(2))
        ab_rows = nc.dram_tensor("ab_rows", [2, MH, T], F32).ap()
        sconv_w = sb("sconv_w", [P, 4, 2 * INNER // P])
        sconv_b = sb("sconv_b", [P, 2 * INNER // P])
        dt_bias = sb("dt_bias", [SH, 2])
        skip_d = sb("skip_d", [P, SH // 2])
        snorm = sb("snorm", [P, INNER // P])
        last_a = sb("last_a", [SH, NC])
        keep_a = sb("keep_a", [P, SH * NC])
        ssm_rows = nc.dram_tensor("ssm_rows", [2, SH, T], F32).ap()
        ssm_last = nc.dram_tensor("ssm_last", [SH, NC], F32).ap()
        ssm_at = phases.index("ssm") if "ssm" in phases else 0

        UNITS = 14
        with nc.sbuf_tensor("scratch", [P, UNITS * T], F32) as scratch:
            pass
        with nc.sbuf_tensor("below_z_lo", [P, (UNITS - 4) * T], F32), nc.sbuf_tensor("z_lo", [P, 4, T], F32R) as z_lo:
            pass

        def cut(k, n=1):
            return scratch[:, k * T:(k + n) * T]

        pair = [ctx.enter_context(nc.psum_tensor(f"pair{k}", [P, 2, HALF], F32)) for k in range(4)]

        w_loaded = [sem(f"w_loaded{s}") for s in range(2)]
        w_split = [sem(f"w_split{s}") for s in range(2)]
        unit_done = [sem(f"unit_done{s}") for s in range(2)]
        part_done = [sem(f"part_done{s}") for s in range(4)]
        pair_free = [sem(f"pair_free{s}") for s in range(4)]
        dve_done, act_done, pool_done = (sem(f"{n}_done") for n in ("dve", "act", "pool"))
        const_ready = sem("const_ready")
        small_loaded = sem("small_loaded")
        x_loaded = [sem(f"x_loaded{s}") for s in range(2)]
        turned_done = [sem(f"turned_done{s}") for s in range(2)]
        x_read = [sem(f"x_read{s}") for s in range(2)]
        x_ready = sem("x_ready")
        resid_ready = sem("resid_ready")
        x_tile_ready = sem("x_tile_ready")
        high_ready = sem("high_ready")
        low_ready = sem("low_ready")
        sq_ready = sem("sq_ready")
        sq_used = sem("sq_used")
        sum_ready = sem("sum_ready")
        norm_sum = sem("norm_sum")
        r_ready = sem("r_ready")
        z_ready = sem("z_ready")
        z_high = sem("z_high")
        z_low = sem("z_low")
        begun = sem("begun")
        exp_free = [sem(f"exp_free{s}") for s in range(2)]
        exp_here = [sem(f"exp_here{s}") for s in range(2)]
        mix_free = [sem(f"mix_free{s}") for s in range(2)]
        mix_here = [sem(f"mix_here{s}") for s in range(2)]
        ab_small = sem("ab_small")
        ab_zeroed = sem("ab_zeroed")
        b_tok_ready = sem("b_tok_ready")
        b_turned = sem("b_turned")
        bc_ready = sem("bc_ready")
        cb_done = sem("cb_done")
        conv_begun = sem("conv_begun")
        conv_ready = sem("conv_ready")
        conv_summed = sem("conv_summed")
        decay_exp = sem("decay_exp")
        decay_ready = sem("decay_ready")
        dist_ready = sem("dist_ready")
        ea_ready = sem("ea_ready")
        exp_ready = sem("exp_ready")
        f_exp = sem("f_exp")
        f_log = sem("f_log")
        f_ready = sem("f_ready")
        gate_split = sem("gate_split")
        gates_done = sem("gates_done")
        gates_free = sem("gates_free")
        gates_here = sem("gates_here")
        h_ready = sem("h_ready")
        h_rstd = sem("h_rstd")
        h_squared = sem("h_squared")
        h_turned = sem("h_turned")
        hm_ready = sem("hm_ready")
        k_turned = sem("k_turned")
        keep_here = sem("keep_here")
        kw_ready = sem("kw_ready")
        lam_dots = sem("lam_dots")
        lam_exps = sem("lam_exps")
        max_ready = sem("max_ready")
        mix_ready = sem("mix_ready")
        mqk_ready = sem("mqk_ready")
        mo_ready = sem("mo_ready")
        mo_tanh = sem("mo_tanh")
        mv_ready = sem("mv_ready")
        num_ready = sem("num_ready")
        o_normed = sem("o_normed")
        o_rstd = sem("o_rstd")
        o_squared = sem("o_squared")
        o_sum = sem("o_sum")
        probs_ready = sem("probs_ready")
        probs_t_ready = sem("probs_t_ready")
        probs_turned = sem("probs_turned")
        qk_done = sem("qk_done")
        qk_ready = sem("qk_ready")
        rows_exp = sem("rows_exp")
        rows_kept = sem("rows_kept")
        rows_made = sem("rows_made")
        rows_turn = sem("rows_turn")
        rows_turned = sem("rows_turned")
        s_ready = sem("s_ready")
        scores_ready = sem("scores_ready")
        sq_done = sem("sq_done")
        srows_kept = sem("srows_kept")
        srows_made = sem("srows_made")
        ssm_small = sem("ssm_small")
        state_parts = sem("state_parts")
        states_ready = sem("states_ready")
        tanh_ready = sem("tanh_ready")
        v_tok_ready = sem("v_tok_ready")
        v_turned = sem("v_turned")
        values_ready = sem("values_ready")
        vd_ready = sem("vd_ready")
        vd_turned = sem("vd_turned")
        weights_ready = sem("weights_ready")
        x_turned = sem("x_turned")
        xw_ready = sem("xw_ready")
        y_gated = sem("y_gated")
        y_high = sem("y_high")
        y_inner = sem("y_inner")
        y_made = sem("y_made")
        y_normed = sem("y_normed")
        y_outer = sem("y_outer")
        y_ready = sem("y_ready")
        y_rstd = sem("y_rstd")
        y_squares = sem("y_squares")
        y_sum = sem("y_sum")
        z_scaled = sem("z_scaled")
        z_tanh = sem("z_tanh")
        stored = [sem(f"stored{s}") for s in range(4)]
        rstd_ready = sem("rstd_ready")
        rstd_used = sem("rstd_used")
        rows_ready = sem("rows_ready")
        row_gain = sem("row_gain")

        def load_unit(t, slot, dst, src):
            t.e.wait_ge(w_split[slot], t.next(w_split[slot]))
            t.e.sem_inc(begun, 1)
            t.e.dma_start(dst, src).then_inc(w_loaded[slot], 16)

        def split_unit(t, slot):
            t.e.wait_ge(w_loaded[slot], t.next(w_loaded[slot], 16))
            t.e.wait_ge(unit_done[slot], t.next(unit_done[slot]))
            t.e.sem_inc(begun, 1)
            t.e.tensor_copy(w_hi[:, slot, :], w_raw[:, slot, :]).then_inc(pool_done, 1)
            t.e.wait_ge(pool_done, t.next(pool_done))
            t.e.tensor_tensor(w_lo[:, slot, :], w_raw[:, slot, :], w_hi[:, slot, :].bitcast(F32),
                              ALU.subtract).then_inc(w_split[slot], 1)

        def products(t, ps, m, slot, col, rhs_hi, rhs_lo, first, last):
            for w, r in ((w_hi, rhs_hi), (w_hi, rhs_lo), (w_lo, rhs_hi)):
                for n in range(2):
                    ins = t.e.matmul(ps[0:m, n, :], w[:, slot, col:col + m], r[:, n * HALF:(n + 1) * HALF],
                                     start=first and w is w_hi and r is rhs_hi,
                                     stop=last and w is w_lo)
            return ins

        def project(t, slot, ks=range(KD), fresh=False):
            if 0 in ks:
                t.e.wait_ge(w_split[slot], t.next(w_split[slot]))
                t.e.wait_ge(pair_free[slot], t.next(pair_free[slot]))
            for k in ks:
                if fresh:
                    t.e.wait_ge(low_ready, t.next(low_ready))
                ins = products(t, pair[slot], P, slot, k * P, HH[:, k, :], HL[:, k, :], k == 0, k == KD - 1)
            if KD - 1 in ks:
                ins.then_inc(unit_done[slot], 1)

        def flat(ap):
            return ap.rearrange("p a n -> p (a n)")

        x_in = cut(0, 2).rearrange("p (b n) -> p b n", b=2)

        def sp_x(t):
            def body(i):
                for b in range(2):
                    t.e.wait_ge(x_read[b], t.next(x_read[b]))
                    t.e.dma_start(x_in[:, b, :], x[0, bass.ds(i * 2 * P + b * P, P), :]).then_inc(x_loaded[b], 16)
            t.loop(NC // 2, body)

        def pe_x(t):
            t.e.wait_ge(const_ready, t.next(const_ready))

            def body(i):
                for b in range(2):
                    t.e.wait_ge(x_loaded[b], t.next(x_loaded[b], 16))
                    t.e.wait_ge(pair_free[b], t.next(pair_free[b]))
                    for k in range(KD):
                        ins = t.e.transpose(pair[b][:, k // 4, k % 4 * P:(k % 4 + 1) * P],
                                            x_in[:, b, k * P:(k + 1) * P], ident[:, :])
                    ins.then_inc(turned_done[b], 1)
            t.loop(NC // 2, body)

        def act_x(t):
            def body(i):
                for b in range(2):
                    t.e.wait_ge(turned_done[b], t.next(turned_done[b]))
                    t.e.sem_inc(x_read[b], 1)
                    t.e.activation(X[:, :, bass.ds(i * 2 * P + b * P, P)],
                                   pair[b][:, :, :].rearrange("p a (c n) -> p (a c) n", n=P),
                                   ACT.Copy).then_inc(pair_free[b], 1)
            t.loop(NC // 2, body)
            t.e.drain().then_inc(resid_ready, 1)

        squares = cut(0, 2).rearrange("p (b n) -> p b n", b=2)
        square_sum = cut(2)

        def act_norm(t, which, power=-0.5):
            for k in range(KD):
                t.e.wait_ge(x_tile_ready, t.next(x_tile_ready))
                t.e.activation(HH[:, k, :], X[:, k, :], ACT.Copy,
                               scale=gains[:, which, k:k + 1]).then_inc(high_ready, 1)
                t.e.wait_ge(sq_used, t.next(sq_used))
                t.e.activation(squares[:, k % 2, :], X[:, k, :], ACT.Square).then_inc(sq_ready, 1)
            t.e.wait_ge(norm_sum, t.next(norm_sum))
            t.e.activation(R[:, :], flat(pair[3]), ACT.Ln, scale=1.0 / D, bias=eps_col[:, 0:1]).then_inc(act_done, 1)
            t.e.wait_ge(act_done, t.next(act_done))
            t.e.sem_inc(pair_free[3], 1)
            t.e.activation(R[:, :], R[:, :], ACT.Exp, scale=power).then_inc(r_ready, 1)

        def norm_tile(t, which, k):
            t.e.wait_ge(high_ready, t.next(high_ready))
            t.e.scalar_tensor_tensor(out=HL[:, k, :], in0=X[:, k, :], scalar=gains[:, which, k:k + 1],
                                     in1=HH[:, k, :].bitcast(F32), op0=ALU.mult,
                                     op1=ALU.subtract).then_inc(low_ready, 1)
            t.e.wait_ge(sq_ready, t.next(sq_ready))
            if k == 0:
                t.e.tensor_copy(square_sum, squares[:, 0, :]).then_inc(dve_done, 1)
                t.e.wait_ge(dve_done, t.next(dve_done))
            else:
                t.e.tensor_tensor(square_sum, square_sum, squares[:, k % 2, :], ALU.add).then_inc(dve_done, 1)
                t.e.wait_ge(dve_done, t.next(dve_done))
            t.e.sem_inc(sq_used, 1)
            if k == KD - 1:
                t.e.sem_inc(sum_ready, 1)

        def add_tile(t, k, p, norm):
            if norm is None:
                t.e.tensor_tensor(X[:, k, :], X[:, k, :], flat(pair[p]), ALU.add).then_inc(pair_free[p], 1)
            else:
                t.e.tensor_tensor(X[:, k, :], X[:, k, :], flat(pair[p]), ALU.add).then_inc(dve_done, 1)
                t.e.wait_ge(dve_done, t.next(dve_done))
                t.e.sem_inc(pair_free[p], 1)
                t.e.sem_inc(x_tile_ready, 1)
                if k > 0:
                    norm_tile(t, norm, k - 1)
                if k == KD - 1:
                    norm_tile(t, norm, k)

        def pe_first_unit(t):
            project(t, 0, fresh=True)
            t.e.wait_ge(sum_ready, t.next(sum_ready))
            t.e.wait_ge(pair_free[3], t.next(pair_free[3]))
            for n in range(2):
                ins = t.e.matmul(pair[3][:, n, :], ones[:, :], square_sum[:, n * HALF:(n + 1) * HALF],
                                 start=True, stop=True)
            ins.then_inc(norm_sum, 1)

        z = cut(3, 2).rearrange("p (b n) -> p b n", b=2)

        def sp_mlp(t, l):
            w1 = mlp_w1[l].rearrange("(k p) n -> p k n", p=P)
            w2 = mlp_w2[l].rearrange("(k p) n -> p k n", p=P)

            def body(i):
                for j in range(4):
                    load_unit(t, j % 2, w_raw[:, j % 2, :].rearrange("p (k n) -> p k n", k=KD),
                              w1[:, :, bass.ds(i * FB + j * P, P)])
                for j in range(4):
                    load_unit(t, j % 2, w_raw[:, j % 2, :].rearrange("p (k n) -> p k n", k=4),
                              w2[:, bass.ds(i * 4, 4), j * 2 * P:(j + 1) * 2 * P])
            t.loop(N_FB, body)

        def pool_units(t, n, slots):
            def body(i):
                for s in slots:
                    split_unit(t, s)
            t.loop(n, body)

        Z_LATE = [(m, k) for m in range(2) for k in range(3)] + [(0, 3), (1, 3)]
        Z_IN_TURN = [(m, k) for m in range(2) for k in range(4)]

        def mlp_pair(j, m):
            return j % 2 + 2 * (1 - m)

        def pe_mlp(t):
            def body(i, first):
                for j in range(1 if first else 0, 4):
                    project(t, j % 2)
                for j in range(4):
                    t.e.wait_ge(w_split[j % 2], t.next(w_split[j % 2]))
                    for m, k in Z_IN_TURN if j else Z_LATE:
                        p = mlp_pair(j, m)
                        if k == 0:
                            t.e.wait_ge(pair_free[p], t.next(pair_free[p]))
                        if j == 0 and m == 0:
                            t.e.wait_ge(z_low, t.next(z_low))
                        ins = products(t, pair[p], P, j % 2, k * 2 * P + m * P, z_hi[:, k, :],
                                       z_lo[:, k, :], k == 0, k == 3)
                        if k == 3:
                            ins.then_inc(unit_done[j % 2] if m else part_done[p], 1)
            body(0, True)
            t.loop(N_FB - 1, lambda i: body(i, False))

        def dve_mlp(t, norm):
            t.e.wait_ge(r_ready, t.next(r_ready))

            def body(i, norm):
                for j in range(4):
                    t.e.wait_ge(unit_done[j % 2], t.next(unit_done[j % 2]))
                    t.e.scalar_tensor_tensor(out=z[:, j % 2, :], in0=flat(pair[j % 2]), scalar=0.0, in1=R[:, :],
                                             op0=ALU.max, op1=ALU.mult).then_inc(dve_done, 1)
                    t.e.wait_ge(dve_done, t.next(dve_done))
                    t.e.sem_inc(z_ready, 1)
                    t.e.sem_inc(pair_free[j % 2], 1)
                    t.e.wait_ge(z_high, t.next(z_high))
                    t.e.tensor_tensor(z_lo[:, j, :], z[:, j % 2, :], z_hi[:, j, :].bitcast(F32),
                                      ALU.subtract).then_inc(z_low, 1)
                for j in range(4):
                    for m in range(2):
                        p = mlp_pair(j, m)
                        if m:
                            t.e.wait_ge(unit_done[j % 2], t.next(unit_done[j % 2]))
                        else:
                            t.e.wait_ge(part_done[p], t.next(part_done[p]))
                        add_tile(t, 2 * j + m, p, norm)
            t.loop(N_FB - 1, lambda i: body(i, None))
            body(N_FB - 1, norm)

        def act_mlp(t):
            def body(i):
                for j in range(4):
                    t.e.wait_ge(z_ready, t.next(z_ready))
                    t.e.activation(z[:, j % 2, :], z[:, j % 2, :], ACT.Square).then_inc(act_done, 1)
                    t.e.wait_ge(act_done, t.next(act_done))
                    t.e.activation(z_hi[:, j, :], z[:, j % 2, :], ACT.Copy).then_inc(z_high, 1)
            t.loop(N_FB, body)

        C_MQ, C_MK, C_MV, C_MO = 0, MH * DH, 2 * MH * DH, 3 * MH * DH
        C_MI, C_MF = 4 * MH * DH, 4 * MH * DH + MH
        C_DQ = C_MF + MH
        C_DK, C_DV = C_DQ + 2 * AH * AD, C_DQ + 4 * AH * AD
        AB_UNITS = (C_DQ, C_DK, C_DV, C_MQ, C_MK, C_MV, C_MO)

        bias_dist = cut(0)
        qd, kd, vd = cut(1), cut(2), cut(3).rearrange("p (c e) -> p c e", c=NC)
        gate_w = cut(11)
        inter = cut(13)
        prob = [[cut(4), cut(5)], [gate_w, inter]]
        prob_t = cut(12)
        o_t = cut(6)
        conv_y, conv_th = cut(7), cut(8)
        mq, mk = cut(9), cut(10)
        v_tok = cut(4).rearrange("p (c e) -> p c e", c=NC)
        kw_tok = cut(12).rearrange("p (c e) -> p c e", c=NC)
        c_all = conv_th.rearrange("p (c e) -> p c e", c=NC)
        h_tok = conv_y.rearrange("p (c e) -> p c e", c=NC)
        o_gate = mk
        hm_t = mq

        gate_raw = cut(13)[:, 0:KD * 36].rearrange("p (k n) -> p k n", k=KD)
        lam_rows = cut(12)[:, 0:4 * AD].rearrange("p (a n) -> p a n", a=4)

        def pair_chunks(p):
            return pair[p][:, :, :].rearrange("p a (c n) -> p (a c) n", n=P)

        def chunks(ap):
            return ap.rearrange("p (c n) -> p c n", c=NC)

        def turned(p, c):
            return pair[p][:, c // 4, c % 4 * P:(c % 4 + 1) * P]

        def act_ab_small(t):
            w = ab_w_in[0].rearrange("(k p) n -> p k n", p=P)
            col = dict(allow_slow_non_contiguous=True)
            t.e.wait_ge(ab_zeroed, t.next(ab_zeroed))
            for dst, src in (
                    (gate_raw[:, :, 0:MH], w[:, :, C_MI:C_MI + MH]),
                    (gate_raw[:, :, 32:32 + MH], w[:, :, C_MF:C_MF + MH]),
                    (conv_w[:, :, :], ab_conv_w[0].rearrange("j (m p) -> p j m", p=P)),
                    (conv_b[:, :], ab_conv_b[0].rearrange("(m p) -> p m", p=P)),
                    (gate_bias[0:MH, :], ab_i_bias[0].rearrange("(p a) -> p a", a=1)),
                    (gate_bias[32:32 + MH, :], ab_f_bias[0].rearrange("(p a) -> p a", a=1)),
                    (mnorm[:, :], ab_mnorm_g[0].rearrange("(m p) -> p m", p=P)),
                    (dnorm[:, :], ab_dnorm_g[0].rearrange("(m p) -> p m", p=P)),
                    (lam_rows[:, 0, :], ab_lam_q1.to_broadcast([P, AD])),
                    (lam_rows[:, 1, :], ab_lam_k1.to_broadcast([P, AD])),
                    (lam_rows[:, 2, :], ab_lam_q2.to_broadcast([P, AD])),
                    (lam_rows[:, 3, :], ab_lam_k2.to_broadcast([P, AD]))):
                t.e.dma_start(dst, src, **(col if len(dst.shape) == 3 or dst.shape[1] <= 8 else {})
                              ).then_inc(ab_small, 16)

        AB_SMALL = 12 * 16

        rows_i, rows_f, rows_e, rows_l = cut(4), cut(5), cut(6), cut(3)
        row_b, row_g, row_big, row_d, row_rst = cut(5), cut(4), cut(6), cut(11), cut(12)
        neg_g, inter_row, row_w, row_m = cut(13), cut(1), cut(2), cut(3)

        def pe_gates(t):
            t.e.wait_ge(gate_split, t.next(gate_split))
            t.e.wait_ge(pair_free[2], t.next(pair_free[2]))
            M = 32 + MH
            for k in range(KD):
                for w, r in ((gate_hi, HH), (gate_hi, HL), (gate_lo, HH)):
                    for n in range(2):
                        ins = t.e.matmul(pair[2][0:M, n, :], w[:, k, :], r[:, k, n * HALF:(n + 1) * HALF],
                                         start=(k == 0 and w is gate_hi and r is HH),
                                         stop=(k == KD - 1 and w is gate_lo))
            ins.then_inc(gates_done, 1)

        def pe_gate_cols(t):
            t.e.wait_ge(rows_turn, t.next(rows_turn))
            t.e.wait_ge(pair_free[1], t.next(pair_free[1]))
            for q, row in enumerate((row_g, row_w, row_m)):
                for c in range(NC):
                    at = (q * NC + c) * MH
                    ins = t.e.transpose(pair[1][:, 0, at:at + MH], row[0:MH, c * P:(c + 1) * P], ident[0:MH, 0:MH])
            ins.then_inc(rows_turned, 1)

        def dve_gates(t):
            t.e.wait_ge(ab_small, t.next(ab_small, AB_SMALL))
            t.e.tensor_copy(gate_hi[:, :, :], gate_raw[:, :, :]).then_inc(dve_done, 1)
            t.e.wait_ge(dve_done, t.next(dve_done))
            t.e.tensor_tensor(gate_lo[:, :, :], gate_raw[:, :, :], gate_hi[:, :, :].bitcast(F32),
                              ALU.subtract).then_inc(gate_split, 1)
            t.e.tensor_scalar(conv_w[:, :, :], conv_w[:, :, :], 0.5, None, ALU.mult).then_inc(dve_done, 1)
            t.e.wait_ge(dve_done, t.next(dve_done))
            t.e.tensor_scalar(conv_b[:, :], conv_b[:, :], 0.5, None, ALU.mult).then_inc(dve_done, 1)
            t.e.wait_ge(dve_done, t.next(dve_done))
            t.e.tensor_scalar(mnorm[:, :], mnorm[:, :], 0.5, None, ALU.mult).then_inc(dve_done, 1)
            t.e.wait_ge(dve_done, t.next(dve_done))
            t.e.tensor_scalar(dnorm[:, :], dnorm[:, :], 1.0 - LAM_INIT, None, ALU.mult).then_inc(dve_done, 1)
            t.e.wait_ge(dve_done, t.next(dve_done))
            for m in range(2):
                t.e.tensor_tensor_reduce(lam_rows[:, 2 * m, :], lam_rows[:, 2 * m, :],
                                         lam_rows[:, 2 * m + 1, :], 1.0, 0.0, ALU.mult, ALU.add,
                                         lam[:, m:m + 1]).then_inc(dve_done, 1)
                t.e.wait_ge(dve_done, t.next(dve_done))
            t.e.sem_inc(lam_dots, 1)
            t.e.wait_ge(lam_exps, t.next(lam_exps))
            t.e.tensor_tensor(lam[:, 2:3], lam[:, 1:2], lam[:, 0:1], ALU.subtract).then_inc(dve_done, 1)
            t.e.wait_ge(dve_done, t.next(dve_done))
            t.e.tensor_scalar(lam[:, 2:3], lam[:, 2:3], -LAM_INIT, None, ALU.add).then_inc(dve_done, 1)
            t.e.wait_ge(dve_done, t.next(dve_done))
            t.e.wait_ge(r_ready, t.next(r_ready))
            t.e.wait_ge(gates_done, t.next(gates_done))
            h, f = slice(0, MH), slice(32, 32 + MH)
            t.e.tensor_tensor(rows_i[h, :], flat(pair[2])[h, :], R[h, :], ALU.mult).then_inc(dve_done, 1)
            t.e.wait_ge(dve_done, t.next(dve_done))
            t.e.tensor_tensor(rows_f[f, :], flat(pair[2])[f, :], R[f, :], ALU.mult).then_inc(dve_done, 1)
            t.e.wait_ge(dve_done, t.next(dve_done))
            t.e.sem_inc(pair_free[2], 1)
            t.e.tensor_scalar(rows_i[h, :], rows_i[h, :], gate_bias[h, :], None, ALU.add).then_inc(dve_done, 1)
            t.e.wait_ge(dve_done, t.next(dve_done))
            t.e.tensor_scalar(rows_f[f, :], rows_f[f, :], gate_bias[f, :], None, ALU.add).then_inc(dve_done, 1)
            t.e.wait_ge(dve_done, t.next(dve_done))
            t.e.sem_inc(f_ready, 1)
            dve_unit(t, 0, 0)
            t.e.wait_ge(f_exp, t.next(f_exp))
            t.e.tensor_scalar(rows_e[f, :], rows_e[f, :], 1.0, None, ALU.add).then_inc(dve_done, 1)
            t.e.wait_ge(dve_done, t.next(dve_done))
            t.e.sem_inc(f_ready, 1)
            dve_unit(t, 1, 0)
            t.e.wait_ge(f_log, t.next(f_log))
            t.e.scalar_tensor_tensor(out=row_d[h, :], in0=rows_f[f, :], scalar=0.0, in1=rows_l[f, :],
                                     op0=ALU.min, op1=ALU.subtract).then_inc(dve_done, 1)
            t.e.wait_ge(dve_done, t.next(dve_done))
            t.e.memset(row_rst[h, :], 1.0).then_inc(dve_done, 1)
            t.e.wait_ge(dve_done, t.next(dve_done))
            t.e.memset(chunks(row_rst)[h, :, 0:1], 0.0).then_inc(dve_done, 1)
            t.e.wait_ge(dve_done, t.next(dve_done))
            t.e.tensor_tensor_scan(row_b[h, :], row_rst[h, :], row_d[h, :], 0.0, ALU.mult, ALU.add).then_inc(dve_done, 1)
            t.e.wait_ge(dve_done, t.next(dve_done))
            t.e.tensor_tensor(row_g[h, :], rows_i[h, :], row_b[h, :], ALU.subtract).then_inc(dve_done, 1)
            t.e.wait_ge(dve_done, t.next(dve_done))
            dve_unit(t, 2, 0)
            t.e.memset(row_d[h, :], 0.0).then_inc(dve_done, 1)
            t.e.wait_ge(dve_done, t.next(dve_done))
            t.e.tensor_copy(chunks(row_d)[h, 1:NC, 0:1], chunks(row_b)[h, 0:NC - 1, P - 1:P]).then_inc(dve_done, 1)
            t.e.wait_ge(dve_done, t.next(dve_done))
            t.e.tensor_tensor_scan(row_big[h, :], row_d[h, :], row_g[h, :], 0.0, ALU.add, ALU.max).then_inc(dve_done, 1)
            t.e.wait_ge(dve_done, t.next(dve_done))
            t.e.memset(m0[h, 0:1], 0.0).then_inc(dve_done, 1)
            t.e.wait_ge(dve_done, t.next(dve_done))
            t.e.tensor_tensor(m0[h, 1:NC].rearrange("p (c a) -> p c a", a=1), chunks(row_big)[h, 0:NC - 1, P - 1:P],
                              chunks(row_b)[h, 0:NC - 1, P - 1:P], ALU.add).then_inc(dve_done, 1)
            t.e.wait_ge(dve_done, t.next(dve_done))
            t.e.tensor_tensor(chunks(inter_row)[h, :, :], m0[h, :].rearrange("p (c a) -> p c a", a=1).to_broadcast([MH, NC, P]),
                              chunks(row_big)[h, :, :], ALU.subtract).then_inc(dve_done, 1)
            t.e.wait_ge(dve_done, t.next(dve_done))
            t.e.tensor_tensor(chunks(row_w)[h, :, :], chunks(row_g)[h, :, :],
                              chunks(row_big)[h, :, P - 1:P].to_broadcast([MH, NC, P]), ALU.subtract).then_inc(dve_done, 1)
            t.e.wait_ge(dve_done, t.next(dve_done))
            t.e.tensor_tensor(row_m[h, :], row_b[h, :], row_big[h, :], ALU.add).then_inc(dve_done, 1)
            t.e.wait_ge(dve_done, t.next(dve_done))
            t.e.tensor_scalar(neg_g[h, :], row_big[h, :], -1.0, None, ALU.mult).then_inc(rows_made, 1)
            t.e.sem_inc(rows_exp, 1)
            dve_unit(t, 3, 0)
            t.e.wait_ge(rows_turned, t.next(rows_turned))
            t.e.tensor_copy(gate_cols.rearrange("p q c h -> p (q c h)"), pair[1][:, 0, 0:3 * NC * MH]).then_inc(dve_done, 1)
            t.e.wait_ge(dve_done, t.next(dve_done))
            t.e.sem_inc(pair_free[1], 1)

        def act_gates(t):
            t.e.wait_ge(lam_dots, t.next(lam_dots))
            t.e.activation(lam[:, 0:2], lam[:, 0:2], ACT.Exp).then_inc(lam_exps, 1)
            h, f = slice(0, MH), slice(32, 32 + MH)
            t.e.wait_ge(f_ready, t.next(f_ready))
            t.e.activation(rows_e[f, :], rows_f[f, :], ACT.Abs).then_inc(act_done, 1)
            t.e.wait_ge(act_done, t.next(act_done))
            t.e.activation(rows_e[f, :], rows_e[f, :], ACT.Exp, scale=-1.0).then_inc(f_exp, 1)
            act_unit(t, 0, 0)
            t.e.wait_ge(f_ready, t.next(f_ready))
            t.e.activation(rows_l[f, :], rows_e[f, :], ACT.Ln).then_inc(f_log, 1)
            act_unit(t, 1, 0)
            t.e.wait_ge(rows_exp, t.next(rows_exp))
            t.e.activation(inter_row[h, :], inter_row[h, :], ACT.Exp).then_inc(rows_made, 1)
            t.e.activation(row_w[h, :], row_w[h, :], ACT.Exp).then_inc(act_done, 1)
            t.e.wait_ge(act_done, t.next(act_done))
            t.e.activation(row_m[h, :], row_m[h, :], ACT.Exp, scale=-1.0).then_inc(rows_turn, 1)

        def pool_ab(t):
            t.e.memset(gate_raw[:, :, :], 0.0).then_inc(pool_done, 1)
            t.e.wait_ge(pool_done, t.next(pool_done))
            t.e.sem_inc(ab_zeroed, 1)
            split_unit(t, 0)
            split_unit(t, 1)
            t.e.wait_ge(norm_sum, t.next(norm_sum))
            t.e.iota(bias_dist, pattern=[[1, T]], base=-(T - P), channel_multiplier=-1,
                     allow_small_or_imprecise_dtypes=True).then_inc(pool_done, 1)
            t.e.wait_ge(pool_done, t.next(pool_done))
            t.e.tensor_scalar(bias_dist, bias_dist, SLOPE, None, ALU.mult).then_inc(pool_done, 1)
            t.e.wait_ge(pool_done, t.next(pool_done))
            t.e.affine_select(out=bias_dist, in_=bias_dist, compare_op=ALU.is_ge, fill=NEG,
                              base=T - P, pattern=[[-1, T]], channel_multiplier=1).then_inc(dist_ready, 1)

        def width(qb):
            return (qb + 1) * P

        def halves(qb):
            return (width(qb) + HALF - 1) // HALF

        def pe_scores(t, qb, m):
            t.e.wait_ge(pair_free[2], t.next(pair_free[2]))
            part = slice(m * AD, (m + 1) * AD)
            for n in range(halves(qb)):
                w = min(HALF, width(qb) - n * HALF)
                ins = t.e.matmul(pair[2][:, n, 0:w], qd[part, qb * P:(qb + 1) * P],
                                 kd[part, n * HALF:n * HALF + w], start=True, stop=True)
            ins.then_inc(scores_ready, 1)

        def pe_turn_probs(t, qb, n):
            if n == 0:
                t.e.wait_ge(probs_ready, t.next(probs_ready))
                t.e.wait_ge(pair_free[3], t.next(pair_free[3]))
            else:
                t.e.wait_ge(probs_t_ready, t.next(probs_t_ready))
            for kb in range(4 * n, min(4 * n + 4, qb + 1)):
                ins = t.e.transpose(pair[3][:, 0, kb % 4 * P:(kb % 4 + 1) * P],
                                    prob[qb % 2][1][:, kb * P:(kb + 1) * P], ident[:, :])
            ins.then_inc(probs_turned, 1)

        def pe_values(t, qb):
            t.e.wait_ge(probs_t_ready, t.next(probs_t_ready))
            for kb in range(qb + 1):
                ins = t.e.matmul(pair[3][:, 1, 0:P], vd[:, kb, :], prob_t[:, kb * P:(kb + 1) * P],
                                 start=(kb == 0), stop=(kb == qb))
            ins.then_inc(values_ready, 1)

        def dve_scores(t, qb, m):
            w, b = width(qb), qb % 2
            t.e.wait_ge(scores_ready, t.next(scores_ready))
            if m == 1 and qb >= 2:
                for _ in range(halves(qb - 2)):
                    t.e.wait_ge(probs_turned, t.next(probs_turned))
            t.e.sem_inc(begun, 1)
            t.e.tensor_tensor_reduce(prob[b][m][:, 0:w], flat(pair[2])[:, 0:w], bias_dist[:, T - w:T], 1.0,
                                     LEAST, ALU.add, ALU.max, stat[:, b, m:m + 1]).then_inc(dve_done, 1)
            t.e.wait_ge(dve_done, t.next(dve_done))
            t.e.sem_inc(pair_free[2], 1)
            t.e.tensor_scalar(stat[:, b, m:m + 1], stat[:, b, m:m + 1], -1.0, None, ALU.mult).then_inc(max_ready, 1)

        def dve_probs(t, qb):
            w, b = width(qb), qb % 2
            for m in range(2):
                t.e.wait_ge(exp_ready, t.next(exp_ready))
            t.e.reciprocal(stat[:, b, 4:6], stat[:, b, 2:4]).then_inc(dve_done, 1)
            t.e.wait_ge(dve_done, t.next(dve_done))
            t.e.tensor_tensor(stat[:, b, 5:6], stat[:, b, 5:6], lam[:, 2:3], ALU.mult).then_inc(dve_done, 1)
            t.e.tensor_scalar(prob[b][0][:, 0:w], prob[b][0][:, 0:w], stat[:, b, 4:5], None, ALU.mult).then_inc(dve_done, 1)
            t.e.wait_ge(dve_done, t.next(dve_done, 2))
            t.e.scalar_tensor_tensor(out=prob[b][1][:, 0:w], in0=prob[b][1][:, 0:w], scalar=stat[:, b, 5:6],
                                     in1=prob[b][0][:, 0:w], op0=ALU.mult, op1=ALU.add).then_inc(probs_ready, 1)

        def act_probs(t, qb, m):
            w, b = width(qb), qb % 2
            t.e.wait_ge(max_ready, t.next(max_ready))
            t.e.activation(prob[b][m][:, 0:w], prob[b][m][:, 0:w], ACT.Exp, bias=stat[:, b, m:m + 1],
                           accum_out=stat[:, b, 2 + m:3 + m]).then_inc(exp_ready, 1)

        def act_turned(t, qb, n):
            w = min(HALF, width(qb) - n * HALF)
            t.e.wait_ge(probs_turned, t.next(probs_turned))
            t.e.activation(prob_t[:, n * HALF:n * HALF + w], pair[3][:, 0, 0:w], ACT.Copy).then_inc(probs_t_ready, 1)

        def act_values(t, qb):
            t.e.wait_ge(values_ready, t.next(values_ready))
            t.e.activation(o_t[:, qb * P:(qb + 1) * P], pair[3][:, 1, 0:P], ACT.Copy).then_inc(act_done, 1)
            t.e.wait_ge(act_done, t.next(act_done))
            t.e.sem_inc(pair_free[3], 1)

        def turn(t, p, src):
            t.e.wait_ge(pair_free[p], t.next(pair_free[p]))
            for c in range(NC):
                ins = t.e.transpose(turned(p, c), src(c), ident[:, :])
            return ins

        def scaled(t, out, s, by=1.0):
            t.e.wait_ge(unit_done[s], t.next(unit_done[s]))
            t.e.scalar_tensor_tensor(out=out, in0=flat(pair[s]), scalar=by, in1=R[:, :], op0=ALU.mult,
                                     op1=ALU.mult).then_inc(dve_done, 1)
            t.e.wait_ge(dve_done, t.next(dve_done))
            t.e.sem_inc(pair_free[s], 1)

        def nothing():
            pass

        def dve_conv_sum(t, y, s, w, m, beside=nothing):
            scaled(t, conv_in[:, 3:3 + T], s)
            t.e.sem_inc(conv_begun, 1)
            beside()
            for tap in range(3):
                if tap == 0:
                    t.e.wait_ge(conv_ready, t.next(conv_ready))
                else:
                    t.e.wait_ge(dve_done, t.next(dve_done))
                ins = t.e.scalar_tensor_tensor(out=y, in0=conv_in[:, tap:tap + T], scalar=w[:, tap, m],
                                               in1=y, op0=ALU.mult, op1=ALU.add)
                ins.then_inc(conv_summed if tap == 2 else dve_done, 1)

        def dve_conv_silu(t, out, y, th):
            t.e.wait_ge(tanh_ready, t.next(tanh_ready))
            t.e.scalar_tensor_tensor(out=out, in0=th, scalar=1.0, in1=y, op0=ALU.add, op1=ALU.mult).then_inc(dve_done, 1)
            t.e.wait_ge(dve_done, t.next(dve_done))

        def dve_conv(t, out, y, th, s, w, m, beside=nothing, late=nothing):
            dve_conv_sum(t, y, s, w, m, beside)
            late()
            dve_conv_silu(t, out, y, th)

        def act_conv_tap(t, y, w, b, m):
            t.e.wait_ge(conv_begun, t.next(conv_begun))
            t.e.activation(y, conv_in[:, 3:3 + T], ACT.Identity, scale=w[:, 3, m], bias=b[:, m]).then_inc(conv_ready, 1)

        def act_conv_tanh(t, y, th):
            t.e.wait_ge(conv_summed, t.next(conv_summed))
            t.e.activation(th, y, ACT.Tanh).then_inc(tanh_ready, 1)

        def act_conv(t, y, th, w, b, m):
            act_conv_tap(t, y, w, b, m)
            act_conv_tanh(t, y, th)

        def sp_projections(t, i, units):
            w = ab_w_in[0].rearrange("(k p) n -> p k n", p=P)
            for j, c in enumerate(units):
                load_unit(t, j % 2, w_raw[:, j % 2, :].rearrange("p (k n) -> p k n", k=KD),
                          w[:, :, bass.ds(i * P + c, P)])

        def pe_attend(t, beside):
            for qb in range(NC + 1):
                if qb < NC:
                    pe_scores(t, qb, 0)
                if qb >= 1:
                    pe_turn_probs(t, qb - 1, 0)
                if qb < NC:
                    if beside:
                        project(t, qb // 2 % 2, range(4 * (qb % 2), 4 * (qb % 2) + 2))
                    pe_scores(t, qb, 1)
                if qb >= 1 and halves(qb - 1) > 1:
                    pe_turn_probs(t, qb - 1, 1)
                if qb < NC and beside:
                    project(t, qb // 2 % 2, range(4 * (qb % 2) + 2, 4 * (qb % 2) + 4))
                if qb >= 1:
                    pe_values(t, qb - 1)
            t.e.wait_ge(o_squared, t.next(o_squared))
            t.e.wait_ge(pair_free[2], t.next(pair_free[2]))
            for n in range(2):
                ins = t.e.matmul(pair[2][:, n, :], ones[:, :], prob[0][0][:, n * HALF:(n + 1) * HALF],
                                 start=True, stop=True)
            ins.then_inc(o_sum, 1)

        def dve_unit(t, j, i):
            if j < 2:
                dve_conv(t, (mq, mk)[j], conv_y, conv_th, j % 2, conv_w, bass.ds(i + j * MH, 1))
                t.e.sem_inc(mqk_ready, 1)
            elif j == 2:
                scaled(t, conv_y, 0)
                t.e.sem_inc(mv_ready, 1)
            else:
                scaled(t, conv_in[:, 3:3 + T], 1)
                t.e.sem_inc(mo_ready, 1)

        def act_unit(t, j, i):
            if j < 2:
                act_conv(t, conv_y, conv_th, conv_w, conv_b, bass.ds(i + j * MH, 1))

        def dve_attend(t, i, beside):
            for qb in range(NC):
                dve_scores(t, qb, 0)
                if beside and qb == 6:
                    dve_unit(t, 2, i + 1)
                dve_scores(t, qb, 1)
                dve_probs(t, qb)
                if beside and qb in (2, 4):
                    dve_conv_sum(t, conv_y, qb // 2 - 1, conv_w, bass.ds(i + 1 + (qb // 2 - 1) * MH, 1))
                if beside and qb in (3, 5):
                    dve_conv_silu(t, (mq, mk)[qb // 2 - 1], conv_y, conv_th)
                    t.e.sem_inc(mqk_ready, 1)
            if beside:
                dve_unit(t, 3, i + 1)
            for _ in range(2 * halves(NC - 1)):
                t.e.wait_ge(probs_turned, t.next(probs_turned))
            t.e.tensor_scalar(bias_dist, bias_dist, SLOPE, None, ALU.mult).then_inc(dve_done, 1)
            t.e.wait_ge(dve_done, t.next(dve_done))
            t.e.sem_inc(gates_free, 1)
            t.e.wait_ge(o_rstd, t.next(o_rstd))
            t.e.tensor_tensor(o_t, o_t, prob[0][1], ALU.mult).then_inc(o_normed, 1)
            t.e.wait_ge(y_high, t.next(y_high))
            t.e.scalar_tensor_tensor(out=y_lo[:, 1, :], in0=o_t, scalar=dnorm[:, bass.ds(i, 1)],
                                     in1=y_hi[:, 1, :].bitcast(F32), op0=ALU.mult,
                                     op1=ALU.subtract).then_inc(y_ready, 1)

        def act_attend(t, i, beside):
            for qb in range(NC + 1):
                if beside and qb in (3, 5):
                    act_conv_tanh(t, conv_y, conv_th)
                if qb < NC:
                    act_probs(t, qb, 0)
                if qb >= 1:
                    act_turned(t, qb - 1, 0)
                if qb < NC:
                    act_probs(t, qb, 1)
                if qb >= 1 and halves(qb - 1) > 1:
                    act_turned(t, qb - 1, 1)
                if qb >= 1:
                    act_values(t, qb - 1)
                if beside and qb in (2, 4):
                    act_conv_tap(t, conv_y, conv_w, conv_b, bass.ds(i + 1 + (qb // 2 - 1) * MH, 1))
            t.e.activation(prob[0][0], o_t, ACT.Square).then_inc(o_squared, 1)
            t.e.wait_ge(o_sum, t.next(o_sum))
            t.e.activation(prob[0][1], flat(pair[2]), ACT.Ln, scale=1.0 / DH, bias=eps_col[:, 0:1]).then_inc(act_done, 1)
            t.e.wait_ge(act_done, t.next(act_done))
            t.e.sem_inc(pair_free[2], 1)
            t.e.activation(prob[0][1], prob[0][1], ACT.Exp, scale=-0.5).then_inc(o_rstd, 1)
            t.e.wait_ge(o_normed, t.next(o_normed))
            t.e.activation(y_hi[:, 1, :], o_t, ACT.Copy, scale=dnorm[:, bass.ds(i, 1)]).then_inc(y_high, 1)

        def sp_gate_rows(t, i):
            t.e.wait_ge(gates_free, t.next(gates_free))
            t.e.sem_inc(begun, 1)
            t.e.dma_start(gate_w, ab_rows[0, bass.ds(i, 1), :].to_broadcast([P, T])).then_inc(gates_here, 16)
            t.e.dma_start(inter, ab_rows[1, bass.ds(i, 1), :].to_broadcast([P, T])).then_inc(gates_here, 16)

        def sp_out(t, i):
            wo = ab_w_out[0].rearrange("(a r) n -> r a n", a=2)
            for j in range(2):
                load_unit(t, j, w_raw[:, j, :].rearrange("p (a n) -> p a n", a=2),
                          wo[bass.ds(i * P, P), :, j * HALF:(j + 1) * HALF])

        def pe_out(t, j):
            t.e.wait_ge(w_split[j], t.next(w_split[j]))
            for m in range(4):
                p = 2 + m % 2
                t.e.wait_ge(pair_free[p], t.next(pair_free[p]))
                for k in range(2):
                    ins = products(t, pair[p], P, j, k * HALF + m * P, y_hi[:, k, :], y_lo[:, k, :], k == 0, k == 1)
                ins.then_inc(unit_done[j] if m == 3 else part_done[p], 1)

        def dve_out(t, j, ms=range(4), norm=None):
            for m in ms:
                p = 2 + m % 2
                if m == 3:
                    t.e.wait_ge(unit_done[j], t.next(unit_done[j]))
                else:
                    t.e.wait_ge(part_done[p], t.next(part_done[p]))
                add_tile(t, 4 * j + m, p, norm)

        def pe_mlstm(t, out):
            t.e.wait_ge(mqk_ready, t.next(mqk_ready, 2))
            turn(t, 3, lambda c: mk[:, c * P:(c + 1) * P]).then_inc(k_turned, 1)
            t.e.wait_ge(mv_ready, t.next(mv_ready))
            turn(t, 2, lambda c: conv_y[:, c * P:(c + 1) * P]).then_inc(v_turned, 1)
            if out:
                project(t, 0)
            t.e.wait_ge(pair_free[3], t.next(pair_free[3]))
            for c in range(NC):
                ins = t.e.matmul(turned(3, c), mk[:, c * P:(c + 1) * P], mq[:, c * P:(c + 1) * P],
                                 start=True, stop=True)
            ins.then_inc(qk_done, 1)
            t.e.wait_ge(kw_ready, t.next(kw_ready))
            t.e.wait_ge(v_tok_ready, t.next(v_tok_ready))
            t.e.wait_ge(pair_free[2], t.next(pair_free[2]))
            for c in range(NC - 1):
                t.e.matmul(turned(2, c), kw_tok[:, c, :], v_tok[:, c, :], start=True, stop=True)
                ins = t.e.matmul(pair[2][:, 1, 3 * P + c:3 * P + c + 1], kw_tok[:, c, :], ones[:, 0:1],
                                 start=True, stop=True)
            ins.then_inc(state_parts, 1)
            project(t, 1)
            if out:
                t.e.wait_ge(y_ready, t.next(y_ready, 2))
                pe_out(t, 0)
            t.e.wait_ge(weights_ready, t.next(weights_ready))
            t.e.wait_ge(states_ready, t.next(states_ready))
            t.e.wait_ge(pair_free[3], t.next(pair_free[3]))
            t.e.wait_ge(pair_free[2], t.next(pair_free[2]))
            for c in range(NC):
                w = gate_w[:, c * P:(c + 1) * P]
                q = mq[:, c * P:(c + 1) * P]
                t.e.matmul(turned(3, c), w, v_tok[:, c, :], start=True, stop=(c == 0))
                if c > 0:
                    t.e.matmul(turned(3, c), q, c_all[:, c, :], start=False, stop=True)
                ins = t.e.matmul(pair[2][:, 0, c:c + 1], w, ones[:, 0:1], start=True, stop=(c == 0))
                if c > 0:
                    ins = t.e.matmul(pair[2][:, 0, c:c + 1], q, n_all[:, c:c + 1], start=False, stop=True)
            ins.then_inc(num_ready, 1)
            if out:
                pe_out(t, 1)
            project(t, 0)
            t.e.wait_ge(h_ready, t.next(h_ready))
            turn(t, 3, lambda c: h_tok[:, c, :]).then_inc(h_turned, 1)
            t.e.wait_ge(vd_ready, t.next(vd_ready))
            turn(t, 2, lambda c: o_t[:, c * P:(c + 1) * P]).then_inc(vd_turned, 1)

        def dve_mlstm(t, i, out):
            t.e.wait_ge(gates_here, t.next(gates_here, 32))
            g_col = gate_cols[:, 0, :, bass.ds(i, 1)]
            t.e.tensor_tensor(chunks(gate_w), chunks(gate_w), g_col.to_broadcast([P, NC, P]), ALU.add).then_inc(dve_done, 1)
            t.e.wait_ge(dve_done, t.next(dve_done))
            t.e.scalar_tensor_tensor(out=chunks(gate_w), in0=chunks(gate_w), scalar=0.0,
                                     in1=causal[:, :, :].to_broadcast([P, NC, P]), op0=ALU.min,
                                     op1=ALU.add).then_inc(decay_ready, 1)
            t.e.wait_ge(k_turned, t.next(k_turned))
            t.e.tensor_tensor(kw_tok, pair_chunks(3), gate_cols[:, 1, :, bass.ds(i, 1)].to_broadcast([P, NC, P]),
                              ALU.mult).then_inc(dve_done, 1)
            t.e.wait_ge(dve_done, t.next(dve_done))
            t.e.sem_inc(pair_free[3], 1)
            t.e.sem_inc(kw_ready, 1)
            scaled(t, qd, 0, AD ** -0.5)
            t.e.wait_ge(qk_done, t.next(qk_done))
            t.e.wait_ge(decay_exp, t.next(decay_exp))
            t.e.scalar_tensor_tensor(out=gate_w, in0=flat(pair[3]), scalar=DH ** -0.5, in1=gate_w,
                                     op0=ALU.mult, op1=ALU.mult).then_inc(dve_done, 1)
            t.e.wait_ge(dve_done, t.next(dve_done))
            t.e.sem_inc(pair_free[3], 1)
            t.e.sem_inc(weights_ready, 1)
            t.e.scalar_tensor_tensor(out=mq, in0=mq, scalar=DH ** -0.5, in1=inter, op0=ALU.mult,
                                     op1=ALU.mult).then_inc(dve_done, 1)
            t.e.wait_ge(dve_done, t.next(dve_done))
            t.e.wait_ge(state_parts, t.next(state_parts))
            keep = chunks(inter)
            t.e.tensor_copy(c_all[:, 1, :], turned(2, 0)).then_inc(dve_done, 1)
            t.e.tensor_copy(n_all[:, 1:2], pair[2][:, 1, 3 * P:3 * P + 1]).then_inc(dve_done, 1)
            for c in range(1, NC - 1):
                t.e.wait_ge(dve_done, t.next(dve_done, 2))
                t.e.scalar_tensor_tensor(out=c_all[:, c + 1, :], in0=c_all[:, c, :], scalar=keep[:, c, P - 1:P],
                                         in1=turned(2, c), op0=ALU.mult, op1=ALU.add).then_inc(dve_done, 1)
                t.e.scalar_tensor_tensor(out=n_all[:, c + 1:c + 2], in0=n_all[:, c:c + 1],
                                         scalar=keep[:, c, P - 1:P], in1=pair[2][:, 1, 3 * P + c:3 * P + c + 1],
                                         op0=ALU.mult, op1=ALU.add).then_inc(dve_done, 1)
            t.e.wait_ge(dve_done, t.next(dve_done, 2))
            t.e.sem_inc(pair_free[2], 1)
            t.e.sem_inc(states_ready, 1)
            scaled(t, kd, 1)
            t.e.sem_inc(qk_ready, 1)
            if out:
                dve_out(t, 0)
            t.e.wait_ge(num_ready, t.next(num_ready))
            t.e.tensor_copy(den[:, 0, :], pair[2][:, 0, 0:NC]).then_inc(dve_done, 1)
            t.e.wait_ge(dve_done, t.next(dve_done))
            t.e.sem_inc(pair_free[2], 1)
            t.e.scalar_tensor_tensor(out=den[:, 1, :], in0=den[:, 0, :], scalar=-1.0, in1=den[:, 0, :],
                                     op0=ALU.mult, op1=ALU.max).then_inc(dve_done, 1)
            t.e.wait_ge(dve_done, t.next(dve_done))
            t.e.tensor_tensor(den[:, 0, :], den[:, 1, :],
                              gate_cols[:, 2, :, bass.ds(i, 1)].rearrange("p c a -> p (c a)"), ALU.max).then_inc(dve_done, 1)
            t.e.wait_ge(dve_done, t.next(dve_done))
            t.e.reciprocal(den[:, 1, :], den[:, 0, :]).then_inc(dve_done, 1)
            t.e.wait_ge(dve_done, t.next(dve_done))
            t.e.tensor_tensor(h_tok, pair_chunks(3),
                              den[:, 1, :].rearrange("p (c a) -> p c a", a=1).to_broadcast([P, NC, P]),
                              ALU.mult).then_inc(dve_done, 1)
            t.e.wait_ge(dve_done, t.next(dve_done))
            t.e.sem_inc(pair_free[3], 1)
            t.e.tensor_tensor(kw_tok, h_tok, h_tok, ALU.mult).then_inc(dve_done, 1)
            if out:
                dve_out(t, 1, (0, 1))
            t.e.wait_ge(dve_done, t.next(dve_done))
            t.e.tensor_reduce(den[:, 2, :], kw_tok, AX.X, ALU.add).then_inc(h_squared, 1)
            if out:
                dve_out(t, 1, (2, 3))
            t.e.wait_ge(h_rstd, t.next(h_rstd))
            t.e.tensor_tensor(h_tok, h_tok, den[:, 3, :].rearrange("p (c a) -> p c a", a=1).to_broadcast([P, NC, P]),
                              ALU.mult).then_inc(h_ready, 1)
            scaled(t, o_t, 0)
            t.e.sem_inc(vd_ready, 1)
            t.e.wait_ge(h_turned, t.next(h_turned))
            t.e.wait_ge(mo_tanh, t.next(mo_tanh))
            t.e.scalar_tensor_tensor(out=hm_t, in0=o_gate, scalar=1.0, in1=flat(pair[3]), op0=ALU.add,
                                     op1=ALU.mult).then_inc(dve_done, 1)
            t.e.wait_ge(dve_done, t.next(dve_done))
            t.e.sem_inc(pair_free[3], 1)
            t.e.sem_inc(hm_ready, 1)
            t.e.wait_ge(y_high, t.next(y_high))
            t.e.scalar_tensor_tensor(out=y_lo[:, 0, :], in0=hm_t, scalar=mnorm[:, bass.ds(i, 1)],
                                     in1=y_hi[:, 0, :].bitcast(F32), op0=ALU.mult,
                                     op1=ALU.subtract).then_inc(y_ready, 1)

        def act_mlstm(t, i):
            t.e.wait_ge(decay_ready, t.next(decay_ready))
            t.e.activation(gate_w, gate_w, ACT.Exp).then_inc(decay_exp, 1)
            t.e.wait_ge(v_turned, t.next(v_turned))
            t.e.activation(v_tok, pair_chunks(2), ACT.Copy).then_inc(act_done, 1)
            t.e.wait_ge(act_done, t.next(act_done))
            t.e.sem_inc(pair_free[2], 1)
            t.e.sem_inc(v_tok_ready, 1)
            t.e.wait_ge(mo_ready, t.next(mo_ready))
            t.e.wait_ge(qk_done, t.next(qk_done))
            t.e.wait_ge(k_turned, t.next(k_turned))
            t.e.activation(o_gate, conv_in[:, 3:3 + T], ACT.Tanh, scale=0.5).then_inc(mo_tanh, 1)
            t.e.wait_ge(h_squared, t.next(h_squared))
            t.e.activation(den[:, 3, :], den[:, 2, :], ACT.Ln, scale=1.0 / DH, bias=eps_col[:, 0:1]).then_inc(act_done, 1)
            t.e.wait_ge(act_done, t.next(act_done))
            t.e.activation(den[:, 3, :], den[:, 3, :], ACT.Exp, scale=-0.5).then_inc(h_rstd, 1)
            t.e.wait_ge(hm_ready, t.next(hm_ready))
            t.e.activation(y_hi[:, 0, :], hm_t, ACT.Copy, scale=mnorm[:, bass.ds(i, 1)]).then_inc(y_high, 1)
            t.e.wait_ge(vd_turned, t.next(vd_turned))
            t.e.activation(vd, pair_chunks(2), ACT.Copy).then_inc(act_done, 1)
            t.e.wait_ge(act_done, t.next(act_done))
            t.e.sem_inc(pair_free[2], 1)

        U_MLSTM = (C_MQ, C_MK, C_MV, C_MO)

        def sp_ab(t):
            sp_projections(t, 0, U_MLSTM + (C_DQ,))
            t.e.wait_ge(rows_made, t.next(rows_made, 2))
            t.e.dma_start(ab_rows[0], neg_g[0:MH, :]).then_inc(rows_kept, 16)
            t.e.dma_start(ab_rows[1], inter_row[0:MH, :]).then_inc(rows_kept, 16)
            t.e.wait_ge(rows_kept, t.next(rows_kept, 32))
            sp_gate_rows(t, 0)
            w = ab_w_in[0].rearrange("(k p) n -> p k n", p=P)
            for s, c in ((1, C_DK), (0, C_DV)):
                load_unit(t, s, w_raw[:, s, :].rearrange("p (k n) -> p k n", k=KD), w[:, :, c:c + P])

            def body(i):
                sp_projections(t, i + 1, U_MLSTM)
                w = ab_w_in[0].rearrange("(k p) n -> p k n", p=P)
                for j, c in enumerate((C_DQ, C_DK)):
                    load_unit(t, j, w_raw[:, j, :].rearrange("p (k n) -> p k n", k=KD), w[:, :, bass.ds((i + 1) * P + c, P)])
                    if j == 0:
                        sp_gate_rows(t, i + 1)
                sp_out(t, i)
                load_unit(t, 0, w_raw[:, 0, :].rearrange("p (k n) -> p k n", k=KD), w[:, :, bass.ds((i + 1) * P + C_DV, P)])
            t.loop(MH - 1, body)
            sp_out(t, MH - 1)

        def pool_ab_units(t):
            for s in (0, 1, 0, 1, 0):
                split_unit(t, s)
            pool_units(t, MH - 1, (0, 1, 0, 1, 0, 1, 0, 1, 0))
            for s in (0, 1):
                split_unit(t, s)

        def pe_ab(t):
            for j in range(1, 5):
                project(t, j % 2)
            pe_gate_cols(t)
            pe_mlstm(t, False)

            def body(i):
                t.e.wait_ge(qk_ready, t.next(qk_ready))
                pe_attend(t, True)
                pe_mlstm(t, True)
            t.loop(MH - 1, body)
            t.e.wait_ge(qk_ready, t.next(qk_ready))
            pe_attend(t, False)
            t.e.wait_ge(y_ready, t.next(y_ready, 2))
            pe_out(t, 0)
            pe_out(t, 1)

        def dve_ab(t, norm):
            t.e.wait_ge(dist_ready, t.next(dist_ready))
            dve_mlstm(t, 0, False)

            def body(i):
                dve_attend(t, i, True)
                dve_mlstm(t, i + 1, True)
            t.loop(MH - 1, body)
            dve_attend(t, MH - 1, False)
            dve_out(t, 0, norm=norm)
            dve_out(t, 1, norm=norm)

        def act_ab(t):
            act_mlstm(t, 0)

            def body(i):
                act_attend(t, i, True)
                act_mlstm(t, i + 1)
            t.loop(MH - 1, body)
            act_attend(t, MH - 1, False)

        C_Z, C_X, C_B, C_C = 0, INNER, 2 * INNER, 2 * INNER + G * NS
        C_DT = C_C + G * NS
        M_B, M_C = INNER // P, INNER // P + G

        c_t, b_t = cut(0), cut(1)
        x_t = [cut(2), cut(3)]
        z_t = [cut(4), cut(5)]
        b_tok = chunks(cut(6))
        x_dt = cut(7, 2).rearrange("p (c e) -> p c e", c=NC)
        x_w = cut(9, 2).rearrange("p (c e) -> p c e", c=NC)
        s_all = x_w
        cb = cut(11)
        mix = [cut(12), cut(13)]
        ssm_y, ssm_th = cut(9), cut(10)
        y_t = [b_t, cut(6)]
        exp_a = [conv_in[:, 3:3 + T], cb]
        dt_row, dta_row, a_row, ea_row = cut(6), cut(11), cut(4), cut(13)
        wa_row, u_row, l_row, rs_row = cut(5), cut(7), cut(8), cut(12)
        dt_raw = cut(9)[:, 0:KD * SH].rearrange("p (k n) -> p k n", k=KD)

        def sp_ssm_small(t):
            w = ssm_w_in[0].rearrange("(k p) n -> p k n", p=P)
            col = dict(allow_slow_non_contiguous=True)
            t.skip(resid_ready, max(ssm_at - 1, 0))
            t.e.wait_ge(resid_ready, t.next(resid_ready))
            for dst, src in (
                    (dt_raw, w[:, :, C_DT:C_DT + SH]),
                    (sconv_w[:, :, :], ssm_conv_w[0].rearrange("j (m p) -> p j m", p=P)),
                    (sconv_b[:, :], ssm_conv_b[0].rearrange("(m p) -> p m", p=P)),
                    (dt_bias[:, 0:1], ssm_dt_bias[0].rearrange("(p a) -> p a", a=1)),
                    (dt_bias[:, 1:2], ssm_a_log[0].rearrange("(p a) -> p a", a=1)),
                    (skip_d[0:SP_, :], ssm_d.rearrange("a (m b) -> a b m", b=2)[:, 0, :].to_broadcast([SP_, SH // 2])),
                    (skip_d[SP_:P, :], ssm_d.rearrange("a (m b) -> a b m", b=2)[:, 1, :].to_broadcast([SP_, SH // 2])),
                    (snorm[:, :], ssm_norm_g[0].rearrange("(m p) -> p m", p=P))):
                t.e.dma_start(dst, src, **col).then_inc(ssm_small, 16)

        SSM_SMALL = 8 * 16

        def pe_steps(t):
            t.e.wait_ge(gate_split, t.next(gate_split))
            t.e.wait_ge(pair_free[2], t.next(pair_free[2]))
            for k in range(KD):
                for w, r in ((gate_hi, HH), (gate_hi, HL), (gate_lo, HH)):
                    for n in range(2):
                        ins = t.e.matmul(pair[2][0:SH, n, :], w[:, k, 0:SH], r[:, k, n * HALF:(n + 1) * HALF],
                                         start=(k == 0 and w is gate_hi and r is HH),
                                         stop=(k == KD - 1 and w is gate_lo))
            ins.then_inc(gates_done, 1)

        def pe_step_cols(t):
            t.e.wait_ge(rows_turn, t.next(rows_turn))
            t.e.wait_ge(pair_free[3], t.next(pair_free[3]))
            for q, row in enumerate((dt_row, a_row, wa_row)):
                for c in range(NC):
                    at = q * NC * SH + c * SH
                    ins = t.e.transpose(pair[3][:, at // HALF, at % HALF:at % HALF + SH], row[0:SH, c * P:(c + 1) * P],
                                        ident[0:SH, 0:SH])
            ins.then_inc(rows_turned, 1)

        def dve_steps(t):
            t.e.wait_ge(ssm_small, t.next(ssm_small, SSM_SMALL))
            t.e.tensor_copy(gate_hi[:, :, 0:SH], dt_raw).then_inc(dve_done, 1)
            t.e.wait_ge(dve_done, t.next(dve_done))
            t.e.tensor_tensor(gate_lo[:, :, 0:SH], dt_raw, gate_hi[:, :, 0:SH].bitcast(F32),
                              ALU.subtract).then_inc(gate_split, 1)
            t.e.tensor_scalar(sconv_w[:, :, :], sconv_w[:, :, :], 0.5, None, ALU.mult).then_inc(dve_done, 1)
            t.e.wait_ge(dve_done, t.next(dve_done))
            t.e.tensor_scalar(sconv_b[:, :], sconv_b[:, :], 0.5, None, ALU.mult).then_inc(dve_done, 1)
            t.e.wait_ge(dve_done, t.next(dve_done))
            t.e.wait_ge(r_ready, t.next(r_ready))
            t.e.wait_ge(gates_done, t.next(gates_done))
            h = slice(0, SH)
            t.e.tensor_tensor(dt_row[h, :], flat(pair[2])[h, :], R[h, :], ALU.mult).then_inc(dve_done, 1)
            t.e.wait_ge(dve_done, t.next(dve_done))
            t.e.sem_inc(pair_free[2], 1)
            t.e.tensor_scalar(dt_row[h, :], dt_row[h, :], dt_bias[:, 0:1], None, ALU.add).then_inc(dve_done, 1)
            t.e.wait_ge(dve_done, t.next(dve_done))
            t.e.sem_inc(f_ready, 1)
            dve_conv(t, c_t, ssm_y, ssm_th, 0, sconv_w, bass.ds(M_C, 1))
            t.e.sem_inc(bc_ready, 1)
            t.e.wait_ge(f_exp, t.next(f_exp))
            t.e.tensor_scalar(rs_row[h, :], u_row[h, :], 1.0, None, ALU.add).then_inc(dve_done, 1)
            t.e.wait_ge(dve_done, t.next(dve_done))
            t.e.sem_inc(f_ready, 1)
            t.e.tensor_scalar(rs_row[h, :], rs_row[h, :], -1.0, TINY, ALU.add, ALU.add).then_inc(dve_done, 1)
            t.e.wait_ge(dve_done, t.next(dve_done))
            t.e.reciprocal(rs_row[h, :], rs_row[h, :]).then_inc(dve_done, 1)
            t.e.wait_ge(dve_done, t.next(dve_done))
            dve_conv(t, b_t, ssm_y, ssm_th, 1, sconv_w, bass.ds(M_B, 1))
            t.e.sem_inc(bc_ready, 1)
            t.e.wait_ge(f_log, t.next(f_log))
            t.e.scalar_tensor_tensor(out=l_row[h, :], in0=l_row[h, :], scalar=TINY, in1=rs_row[h, :],
                                     op0=ALU.add, op1=ALU.mult).then_inc(dve_done, 1)
            t.e.wait_ge(dve_done, t.next(dve_done))
            t.e.tensor_tensor(l_row[h, :], l_row[h, :], u_row[h, :], ALU.mult).then_inc(dve_done, 1)
            t.e.wait_ge(dve_done, t.next(dve_done))
            t.e.scalar_tensor_tensor(out=dt_row[h, :], in0=dt_row[h, :], scalar=0.0, in1=l_row[h, :],
                                     op0=ALU.max, op1=ALU.add).then_inc(dve_done, 1)
            t.e.wait_ge(dve_done, t.next(dve_done))
            t.e.tensor_scalar(dta_row[h, :], dt_row[h, :], dt_bias[:, 1:2], -1.0, ALU.mult, ALU.mult).then_inc(dve_done, 1)
            t.e.wait_ge(dve_done, t.next(dve_done))
            t.e.memset(rs_row[h, :], 1.0).then_inc(dve_done, 1)
            t.e.wait_ge(dve_done, t.next(dve_done))
            t.e.memset(chunks(rs_row)[h, :, 0:1], 0.0).then_inc(dve_done, 1)
            t.e.wait_ge(dve_done, t.next(dve_done))
            t.e.tensor_tensor_scan(a_row[h, :], rs_row[h, :], dta_row[h, :], 0.0, ALU.mult, ALU.add).then_inc(dve_done, 1)
            t.e.wait_ge(dve_done, t.next(dve_done))
            t.e.tensor_tensor(chunks(wa_row)[h, :, :], chunks(a_row)[h, :, P - 1:P].to_broadcast([SH, NC, P]),
                              chunks(a_row)[h, :, :], ALU.subtract).then_inc(dve_done, 1)
            t.e.wait_ge(dve_done, t.next(dve_done))
            t.e.sem_inc(rows_exp, 1)
            t.e.wait_ge(ea_ready, t.next(ea_ready))
            t.e.tensor_copy(last_a[:, :].rearrange("p (c a) -> p c a", a=1), chunks(ea_row)[h, :, P - 1:P]).then_inc(srows_made, 1)
            t.e.wait_ge(rows_turned, t.next(rows_turned))
            t.e.tensor_copy(step_cols.rearrange("p q c h -> p (q c h)"), flat(pair[3])[:, 0:3 * NC * SH]).then_inc(dve_done, 1)
            t.e.wait_ge(dve_done, t.next(dve_done))
            t.e.sem_inc(pair_free[3], 1)

        def act_steps(t):
            h = slice(0, SH)
            t.e.wait_ge(ssm_small, t.next(ssm_small, SSM_SMALL))
            t.e.activation(dt_bias[:, 1:2], dt_bias[:, 1:2], ACT.Exp).then_inc(begun, 1)
            t.e.wait_ge(f_ready, t.next(f_ready))
            t.e.activation(u_row[h, :], dt_row[h, :], ACT.Abs).then_inc(act_done, 1)
            t.e.wait_ge(act_done, t.next(act_done))
            t.e.activation(u_row[h, :], u_row[h, :], ACT.Exp, scale=-1.0).then_inc(act_done, 1)
            t.e.wait_ge(act_done, t.next(act_done))
            t.e.sem_inc(f_exp, 1)
            act_conv(t, ssm_y, ssm_th, sconv_w, sconv_b, bass.ds(M_C, 1))
            t.e.wait_ge(f_ready, t.next(f_ready))
            t.e.activation(l_row[h, :], u_row[h, :], ACT.Ln, bias=1.0).then_inc(f_log, 1)
            act_conv(t, ssm_y, ssm_th, sconv_w, sconv_b, bass.ds(M_B, 1))
            t.e.wait_ge(rows_exp, t.next(rows_exp))
            t.e.activation(wa_row[h, :], wa_row[h, :], ACT.Exp).then_inc(act_done, 1)
            t.e.wait_ge(act_done, t.next(act_done))
            t.e.sem_inc(rows_turn, 1)
            t.e.activation(ea_row[h, :], a_row[h, :], ACT.Exp).then_inc(act_done, 1)
            t.e.wait_ge(act_done, t.next(act_done))
            t.e.sem_inc(ea_ready, 1)
            t.e.sem_inc(srows_made, 1)

        def sp_ssm(t):
            w = ssm_w_in[0].rearrange("(k p) n -> p k n", p=P)
            wo = ssm_w_out[0].rearrange("(q a p) n -> q p a n", a=2, p=P)
            def unit(s, at):
                load_unit(t, s, w_raw[:, s, :].rearrange("p (k n) -> p k n", k=KD), w[:, :, at])

            def out_unit(i, j):
                load_unit(t, j, w_raw[:, j, :].rearrange("p (a n) -> p a n", a=2),
                          wo[bass.ds(i, 1), :, :, j * HALF:(j + 1) * HALF].rearrange("q p a n -> (q p) a n"))

            def row(i, r):
                t.e.wait_ge(mix_free[r % 2], t.next(mix_free[r % 2]))
                t.e.sem_inc(begun, 1)
                t.e.dma_start(mix[r % 2], ssm_rows[0, bass.ds(i * HPG + r, 1), :].to_broadcast([P, T])
                              ).then_inc(mix_here[r % 2], 16)

            def exps(i, m):
                t.e.wait_ge(exp_free[m], t.next(exp_free[m]))
                t.e.sem_inc(begun, 1)
                for b in range(2):
                    t.e.dma_start(exp_a[m][b * SP_:(b + 1) * SP_, :],
                                  ssm_rows[1, bass.ds(i * HPG + 2 * m + b, 1), :].to_broadcast([SP_, T])
                                  ).then_inc(exp_here[m], 16)

            def group(i, out, more):
                if out:
                    unit(0, bass.ds(i * GW + C_X, P))
                    unit(1, bass.ds(i * GW + C_X + P, P))
                row(i, 0)
                row(i, 1)
                if out:
                    out_unit(i - 1, 0)
                unit(1, bass.ds(i * GW + C_Z, P))
                unit(0, bass.ds(i * GW + C_Z + P, P))
                if out:
                    out_unit(i - 1, 1)
                exps(i, 0)
                row(i, 2)
                row(i, 3)
                if more:
                    unit(0, bass.ds((i + 1) * NS + C_C, P))
                exps(i, 1)
                if more:
                    unit(1, bass.ds((i + 1) * NS + C_B, P))

            unit(0, bass.ds(C_C, P))
            unit(1, bass.ds(C_B, P))
            unit(0, bass.ds(C_X, P))
            unit(1, bass.ds(C_X + P, P))
            t.e.wait_ge(srows_made, t.next(srows_made, 2))
            t.e.dma_start(ssm_rows[0], a_row[0:SH, :]).then_inc(srows_kept, 16)
            t.e.dma_start(ssm_rows[1], ea_row[0:SH, :]).then_inc(srows_kept, 16)
            t.e.dma_start(ssm_last[:, :], last_a[:, :]).then_inc(srows_kept, 16)
            t.e.wait_ge(srows_kept, t.next(srows_kept, 48))
            t.e.dma_start(keep_a[:, :], ssm_last.rearrange("(a h) c -> a (h c)", a=1).to_broadcast([P, SH * NC])
                          ).then_inc(keep_here, 16)
            group(0, False, True)
            t.loop(G - 2, lambda i: group(i + 1, True, True))
            group(G - 1, True, False)
            out_unit(G - 1, 0)
            out_unit(G - 1, 1)

        def pool_ssm_units(t):
            for s in (0, 1, 0, 1, 1, 0, 0, 1):
                split_unit(t, s)
            pool_units(t, G - 2, (0, 1) * 4)
            for s in (0, 1) * 4:
                split_unit(t, s)

        OUT_PAIRS = ((0, 2, 1, 3), (1, 0, 2, 3))

        def pe_ssm_out(t, j):
            t.e.wait_ge(w_split[j], t.next(w_split[j]))
            for m, p in enumerate(OUT_PAIRS[j]):
                t.e.wait_ge(pair_free[p], t.next(pair_free[p]))
                for k in range(2):
                    ins = products(t, pair[p], P, j, k * HALF + m * P, y_hi[:, k, :], y_lo[:, k, :], k == 0, k == 1)
                ins.then_inc(unit_done[j] if m == 3 else part_done[p], 1)

        def dve_ssm_out(t, j, lo, hi, norm=None):
            for m in range(lo, hi):
                p = OUT_PAIRS[j][m]
                if m == 3:
                    t.e.wait_ge(unit_done[j], t.next(unit_done[j]))
                else:
                    t.e.wait_ge(part_done[p], t.next(part_done[p]))
                add_tile(t, 4 * j + m, p, norm)

        def pe_ssm(t):
            def y(m):
                t.e.wait_ge(pair_free[2], t.next(pair_free[2]))
                for b in range(2):
                    t.e.wait_ge(mix_ready, t.next(mix_ready))
                    for c in range(NC):
                        ins = t.e.matmul(turned(2, c)[b * SP_:(b + 1) * SP_, :],
                                         x_dt[:, c, m * P + b * SP_:m * P + (b + 1) * SP_],
                                         mix[b][:, c * P:(c + 1) * P], start=True, stop=True)
                ins.then_inc(y_inner, 1)
                if m == 0:
                    t.e.wait_ge(s_ready, t.next(s_ready))
                t.e.wait_ge(pair_free[3], t.next(pair_free[3]))
                for c in range(1, NC):
                    ins = t.e.matmul(turned(3, c), s_all[:, c, m * P:(m + 1) * P], c_t[:, c * P:(c + 1) * P],
                                     start=True, stop=True)
                ins.then_inc(y_outer, 1)

            def group(out, more):
                project(t, 0)
                project(t, 1)
                if not out:
                    pe_step_cols(t)
                t.e.wait_ge(bc_ready, t.next(bc_ready, 2))
                turn(t, 2, lambda c: b_t[:, c * P:(c + 1) * P]).then_inc(b_turned, 1)
                t.e.wait_ge(pair_free[3], t.next(pair_free[3]))
                for c in range(NC):
                    ins = t.e.matmul(turned(3, c), b_t[:, c * P:(c + 1) * P], c_t[:, c * P:(c + 1) * P],
                                     start=True, stop=True)
                ins.then_inc(cb_done, 1)
                t.e.wait_ge(x_ready, t.next(x_ready))
                turn(t, 2, lambda c: x_t[0][:, c * P:(c + 1) * P]).then_inc(x_turned, 1)
                if out:
                    t.e.wait_ge(y_ready, t.next(y_ready, 2))
                    pe_ssm_out(t, 0)
                t.e.wait_ge(x_ready, t.next(x_ready))
                turn(t, 2, lambda c: x_t[1][:, c * P:(c + 1) * P]).then_inc(x_turned, 1)
                project(t, 1)
                t.e.wait_ge(b_tok_ready, t.next(b_tok_ready))
                t.e.wait_ge(xw_ready, t.next(xw_ready))
                for m in range(2):
                    t.e.wait_ge(pair_free[2 + m], t.next(pair_free[2 + m]))
                    for c in range(NC - 1):
                        ins = t.e.matmul(turned(2 + m, c), b_tok[:, c, :], x_w[:, c, m * P:(m + 1) * P],
                                         start=True, stop=True)
                    ins.then_inc(state_parts, 1)
                project(t, 0)
                y(0)
                if out:
                    pe_ssm_out(t, 1)
                y(1)
                if more:
                    project(t, 0)
                t.e.wait_ge(y_squares, t.next(y_squares))
                t.e.wait_ge(pair_free[2], t.next(pair_free[2]))
                for n in range(2):
                    ins = t.e.matmul(pair[2][:, n, :], ones[:, :], z_t[0][:, n * HALF:(n + 1) * HALF],
                                     start=True, stop=True)
                ins.then_inc(y_sum, 1)
                if more:
                    project(t, 1)

            project(t, 1)
            group(False, True)
            t.loop(G - 2, lambda i: group(True, True))
            group(True, False)
            t.e.wait_ge(y_ready, t.next(y_ready, 2))
            pe_ssm_out(t, 0)
            pe_ssm_out(t, 1)

        def dve_ssm(t, norm):
            def conv(out, s, m, beside=nothing, late=nothing):
                dve_conv(t, out, ssm_y, ssm_th, s, sconv_w, m, beside, late)

            def group(i, out, more):
                def by_head(q, lo, n):
                    return step_cols[:, q, :, bass.ds(i * HPG + lo, n)].rearrange("p c (r a) -> p c r a", a=1)

                def out_tiles(j, lo, hi):
                    dve_ssm_out(t, j, lo, hi)

                def weights(r):
                    t.e.wait_ge(decay_exp, t.next(decay_exp))
                    t.e.tensor_tensor(mix[r % 2], mix[r % 2], cb, ALU.mult).then_inc(mix_ready, 1)

                def times_dt(m):
                    t.e.wait_ge(x_turned, t.next(x_turned))
                    t.e.tensor_tensor(x_dt[:, :, m * P:(m + 1) * P].rearrange("p c (r e) -> p c r e", r=2),
                                      pair_chunks(2).rearrange("p c (r e) -> p c r e", r=2),
                                      by_head(0, 2 * m, 2).to_broadcast([P, NC, 2, SP_]), ALU.mult).then_inc(dve_done, 1)
                    t.e.wait_ge(dve_done, t.next(dve_done))
                    t.e.sem_inc(pair_free[2], 1)

                def gate(m):
                    t.e.wait_ge(z_tanh, t.next(z_tanh))
                    t.e.scalar_tensor_tensor(out=z_t[m], in0=conv_in[:, 3:3 + T], scalar=1.0, in1=z_t[m],
                                             op0=ALU.add, op1=ALU.mult).then_inc(dve_done, 1)
                    t.e.wait_ge(dve_done, t.next(dve_done))

                def output(m):
                    t.e.wait_ge(y_inner, t.next(y_inner))
                    t.e.sem_inc(mix_free[0], 1)
                    t.e.sem_inc(mix_free[1], 1)
                    t.e.scalar_tensor_tensor(out=y_t[m], in0=x_t[m], scalar=skip_d[:, bass.ds(i * 2 + m, 1)],
                                             in1=flat(pair[2]), op0=ALU.mult, op1=ALU.add).then_inc(dve_done, 1)
                    t.e.wait_ge(dve_done, t.next(dve_done))
                    t.e.sem_inc(pair_free[2], 1)
                    t.e.wait_ge(y_outer, t.next(y_outer))
                    t.e.wait_ge(exp_here[m], t.next(exp_here[m], 32))
                    t.e.tensor_tensor(x_t[m][:, P:T], flat(pair[3])[:, P:T], exp_a[m][:, P:T], ALU.mult).then_inc(dve_done, 1)
                    t.e.wait_ge(dve_done, t.next(dve_done))
                    t.e.sem_inc(pair_free[3], 1)
                    t.e.tensor_tensor(y_t[m][:, P:T], y_t[m][:, P:T], x_t[m][:, P:T], ALU.add).then_inc(dve_done, 1)
                    t.e.wait_ge(dve_done, t.next(dve_done))

                def gated(m):
                    t.e.scalar_tensor_tensor(out=y_t[m], in0=z_t[m], scalar=0.5, in1=y_t[m], op0=ALU.mult,
                                             op1=ALU.mult).then_inc(dve_done, 1)
                    t.e.wait_ge(dve_done, t.next(dve_done))
                    t.e.sem_inc(y_gated, 1)

                conv(x_t[0], 0, bass.ds(i * 2, 1))
                t.e.sem_inc(x_ready, 1)
                t.e.wait_ge(cb_done, t.next(cb_done))
                t.e.scalar_tensor_tensor(out=chunks(cb), in0=causal[:, :, :].to_broadcast([P, NC, P]), scalar=0.0,
                                         in1=pair_chunks(3), op0=ALU.is_ge, op1=ALU.mult).then_inc(dve_done, 1)
                t.e.wait_ge(dve_done, t.next(dve_done))
                t.e.sem_inc(pair_free[3], 1)
                times_dt(0)
                conv(x_t[1], 1, bass.ds(i * 2 + 1, 1), (lambda: out_tiles(0, 0, 1)) if out else nothing,
                     (lambda: out_tiles(0, 1, 3)) if out else nothing)
                t.e.sem_inc(x_ready, 1)
                if out:
                    out_tiles(0, 3, 4)
                times_dt(1)
                t.e.tensor_tensor(x_w.rearrange("p c (r e) -> p c r e", r=HPG),
                                  x_dt.rearrange("p c (r e) -> p c r e", r=HPG),
                                  by_head(2, 0, HPG).to_broadcast([P, NC, HPG, SP_]), ALU.mult).then_inc(xw_ready, 1)
                weights(0)
                weights(1)
                if not out:
                    t.e.wait_ge(keep_here, t.next(keep_here, 16))
                scaled(t, z_t[0], 1)
                t.e.sem_inc(z_scaled, 1)
                t.e.wait_ge(state_parts, t.next(state_parts, 2))
                for m in range(2):
                    t.e.tensor_copy(s_all[:, 1, m * P:(m + 1) * P], turned(2 + m, 0)).then_inc(dve_done, 1)
                t.e.wait_ge(dve_done, t.next(dve_done, 2))
                for c in range(1, NC - 1):
                    for r in range(HPG):
                        part = slice(r * SP_, (r + 1) * SP_)
                        t.e.scalar_tensor_tensor(out=s_all[:, c + 1, part], in0=s_all[:, c, part],
                                                 scalar=keep_a[:, bass.ds(i * HPG * NC + r * NC + c, 1)],
                                                 in1=turned(2 + r // 2, c)[:, r % 2 * SP_:(r % 2 + 1) * SP_],
                                                 op0=ALU.mult, op1=ALU.add).then_inc(dve_done, 1)
                    t.e.wait_ge(dve_done, t.next(dve_done, HPG))
                for m in range(2):
                    t.e.sem_inc(pair_free[2 + m], 1)
                t.e.sem_inc(s_ready, 1)
                gate(0)
                t.e.sem_inc(exp_free[0], 1)
                scaled(t, z_t[1], 0)
                output(0)
                t.e.sem_inc(z_scaled, 1)
                if out:
                    out_tiles(1, 0, 2)
                weights(2)
                if out:
                    out_tiles(1, 2, 3)
                weights(3)
                if out:
                    out_tiles(1, 3, 4)
                t.e.wait_ge(mix_ready, t.next(mix_ready, HPG))
                t.e.sem_inc(exp_free[1], 1)
                gated(0)
                gate(1)
                output(1)
                gated(1)
                t.e.wait_ge(sq_done, t.next(sq_done, 2))
                t.e.tensor_tensor(z_t[0], z_t[0], z_t[1], ALU.add).then_inc(y_squares, 1)
                if more:
                    conv(c_t, 0, bass.ds(i + 1 + M_C, 1))
                    t.e.sem_inc(bc_ready, 1)
                t.e.wait_ge(y_rstd, t.next(y_rstd))
                for m in range(2):
                    t.e.tensor_tensor(y_t[m], y_t[m], z_t[1], ALU.mult).then_inc(y_normed, 1)

                def low(m):
                    t.e.wait_ge(y_high, t.next(y_high))
                    t.e.scalar_tensor_tensor(out=y_lo[:, m, :], in0=y_t[m], scalar=snorm[:, bass.ds(i * 2 + m, 1)],
                                             in1=y_hi[:, m, :].bitcast(F32), op0=ALU.mult,
                                             op1=ALU.subtract).then_inc(y_ready, 1)
                if more:
                    conv(b_t, 1, bass.ds(i + 1 + M_B, 1), lambda: low(0), lambda: low(1))
                    t.e.sem_inc(bc_ready, 1)
                else:
                    low(0)
                    low(1)

            group(0, False, True)
            t.loop(G - 2, lambda i: group(i + 1, True, True))
            group(G - 1, True, False)
            dve_ssm_out(t, 0, 0, 4, norm)
            dve_ssm_out(t, 1, 0, 4, norm)

        def act_ssm(t):
            def conv(m):
                act_conv(t, ssm_y, ssm_th, sconv_w, sconv_b, m)

            def decays(i, r):
                m = r % 2
                t.e.wait_ge(mix_here[m], t.next(mix_here[m], 16))
                for c in range(NC):
                    part = slice(c * P, (c + 1) * P)
                    t.e.activation(mix[m][:, part], mix[m][:, part], ACT.Relu, scale=-1.0,
                                   bias=step_cols[:, 1, c, bass.ds(i * HPG + r, 1)]).then_inc(act_done, 1)
                t.e.wait_ge(act_done, t.next(act_done, NC))
                t.e.activation(mix[m], mix[m], ACT.Exp, scale=-1.0).then_inc(decay_exp, 1)

            def group(i, more):
                conv(bass.ds(i * 2, 1))
                t.e.wait_ge(b_turned, t.next(b_turned))
                t.e.activation(b_tok, pair_chunks(2), ACT.Copy).then_inc(act_done, 1)
                t.e.wait_ge(act_done, t.next(act_done))
                t.e.sem_inc(pair_free[2], 1)
                t.e.sem_inc(b_tok_ready, 1)
                decays(i, 0)
                conv(bass.ds(i * 2 + 1, 1))
                decays(i, 1)
                t.e.wait_ge(z_scaled, t.next(z_scaled))
                t.e.activation(conv_in[:, 3:3 + T], z_t[0], ACT.Tanh, scale=0.5).then_inc(z_tanh, 1)
                decays(i, 2)
                t.e.wait_ge(z_scaled, t.next(z_scaled))
                t.e.activation(conv_in[:, 3:3 + T], z_t[1], ACT.Tanh, scale=0.5).then_inc(z_tanh, 1)
                decays(i, 3)
                for m in range(2):
                    t.e.wait_ge(y_gated, t.next(y_gated))
                    t.e.activation(z_t[m], y_t[m], ACT.Square).then_inc(sq_done, 1)
                if more:
                    conv(bass.ds(i + 1 + M_C, 1))
                t.e.wait_ge(y_sum, t.next(y_sum))
                t.e.activation(z_t[1], flat(pair[2]), ACT.Ln, scale=1.0 / GW, bias=eps_col[:, 0:1]).then_inc(act_done, 1)
                t.e.wait_ge(act_done, t.next(act_done))
                t.e.sem_inc(pair_free[2], 1)
                t.e.activation(z_t[1], z_t[1], ACT.Exp, scale=-0.5).then_inc(y_rstd, 1)
                for m in range(2):
                    t.e.wait_ge(y_normed, t.next(y_normed))
                    t.e.activation(y_hi[:, m, :], y_t[m], ACT.Copy, scale=snorm[:, bass.ds(i * 2 + m, 1)]).then_inc(y_high, 1)
                if more:
                    conv(bass.ds(i + 1 + M_B, 1))

            group(0, True)
            t.loop(G - 2, lambda i: group(i + 1, True))
            group(G - 1, False)

        final_row = cut(5)
        y_out = cut(6, 4).rearrange("p (b n) -> p b n", b=4)
        sq_out = cut(10, 2).rearrange("p (b n) -> p b n", b=2)

        def pe_final(t):
            t.e.wait_ge(resid_ready, t.next(resid_ready))
            for c in range(NC):
                b = c % 4
                t.e.wait_ge(pair_free[b], t.next(pair_free[b]))
                for k in range(KD):
                    ins = t.e.transpose(pair[b][:, k // 4, k % 4 * P:(k % 4 + 1) * P],
                                        X[:, k, c * P:(c + 1) * P], ident[:, :])
                ins.then_inc(turned_done[c % 2], 1)

        def act_final(t):
            for c in range(NC):
                b = c % 4
                t.e.wait_ge(turned_done[c % 2], t.next(turned_done[c % 2]))
                t.e.activation(sq_out[:, c % 2, :], pair[b][:, :, :].rearrange("p a n -> p (a n)"), ACT.Square,
                               accum_out=ss[:, c:c + 1]).then_inc(act_done, 1)
                t.e.wait_ge(act_done, t.next(act_done))
                t.e.activation(rstd[:, c:c + 1], ss[:, c:c + 1], ACT.Ln, scale=1.0 / D,
                               bias=eps_col[:, 0:1]).then_inc(act_done, 1)
                t.e.wait_ge(act_done, t.next(act_done))
                t.e.activation(rstd[:, c:c + 1], rstd[:, c:c + 1], ACT.Exp, scale=-0.5).then_inc(rstd_ready, 1)

        def dve_final(t):
            t.e.wait_ge(row_gain, t.next(row_gain, 16))
            for c in range(NC):
                b = c % 4
                t.e.wait_ge(rstd_ready, t.next(rstd_ready))
                if c >= 4:
                    t.e.wait_ge(stored[b], t.next(stored[b], 16))
                t.e.scalar_tensor_tensor(out=y_out[:, b, :], in0=pair[b][:, :, :].rearrange("p a n -> p (a n)"),
                                         scalar=rstd[:, c:c + 1], in1=final_row, op0=ALU.mult,
                                         op1=ALU.mult).then_inc(dve_done, 1)
                t.e.wait_ge(dve_done, t.next(dve_done))
                t.e.sem_inc(pair_free[b], 1)
                t.e.sem_inc(rows_ready, 1)

        def sp_final(t):
            t.e.wait_ge(resid_ready, t.next(resid_ready))
            t.e.dma_start(final_row, final_g.rearrange("(a n) -> a n", a=1).to_broadcast([P, D])).then_inc(row_gain, 16)
            for c in range(NC):
                t.e.wait_ge(rows_ready, t.next(rows_ready))
                t.e.dma_start(out[0, c * P:(c + 1) * P, :], y_out[:, c % 4, :]).then_inc(stored[c % 4], 16)
            for b in range(4):
                t.e.wait_ge(stored[b], t.next(stored[b], NC // 4 * 16))

        block = ctx.enter_context(nc.Block())
        n_phases = len(phases)

        @block.sync
        def _(sp):
            t = Tally(sp)
            sp_x(t)
            for ph in phases:
                if ph == "ab":
                    sp_ab(t)
                if ph == "ssm":
                    sp_ssm_small(t)
                    sp_ssm(t)
                if ph[:3] == "mlp":
                    sp_mlp(t, int(ph[3]))
            t.skip(resid_ready, n_phases - 1 - (max(ssm_at - 1, 0) + 1 if "ssm" in phases else 0))
            sp_final(t)

        @block.gpsimd
        def _(pool):
            t = Tally(pool)
            pool.memset(ones[:, :], 1.0)
            pool.memset(conv_in[:, 0:3], 0.0)
            pool.memset(eps_col[:, :], EPS)
            pool.memset(ident[:, :], 0.0).then_inc(pool_done, 1)
            t.e.wait_ge(pool_done, t.next(pool_done))
            pool.memset(causal[:, :, :], 0.0).then_inc(pool_done, 1)
            t.e.wait_ge(pool_done, t.next(pool_done))
            pool.affine_select(out=causal[:, 0, :], in_=causal[:, 0, :], compare_op=ALU.is_ge, fill=NEG, base=0,
                        pattern=[[1, P]], channel_multiplier=-1).then_inc(pool_done, 1)
            t.e.wait_ge(pool_done, t.next(pool_done))
            pool.affine_select(out=ident[:, :], in_=ident[:, :], compare_op=ALU.not_equal, fill=1.0, base=0,
                               pattern=[[-1, P]], channel_multiplier=1).then_inc(const_ready, 1)
            for s in range(2):
                pool.sem_inc(w_split[s], 1)
                pool.sem_inc(unit_done[s], 1)
                pool.sem_inc(x_read[s], 1)
            for s in range(4):
                pool.sem_inc(pair_free[s], 1)
            pool.sem_inc(sq_used, 2)
            pool.sem_inc(gates_free, 1)
            for s in range(2):
                pool.sem_inc(mix_free[s], 1)
            for ph in phases:
                if ph == "ab":
                    pool_ab(t)
                    pool_ab_units(t)
                if ph == "ssm":
                    pool_ssm_units(t)
                if ph[:3] == "mlp":
                    pool_units(t, N_FB, (0, 1) * 4)

        @block.tensor
        def _(pe):
            t = Tally(pe)
            for s in range(2):
                t.skip(w_split[s])
            pe_x(t)
            for ph in phases:
                pe_first_unit(t)
                if ph == "ab":
                    pe_gates(t)
                    pe_ab(t)
                if ph == "ssm":
                    pe_steps(t)
                    pe_ssm(t)
                if ph[:3] == "mlp":
                    pe_mlp(t)
            t.skip(resid_ready, n_phases)
            pe_final(t)

        @block.scalar
        def _(act):
            t = Tally(act)
            for i, g in enumerate((norm_mix_g, norm_mlp_g)):
                for l in range(2):
                    act.dma_start(gains[:, 2 * i + l, :], g[l].rearrange("(k p) -> p k", p=P),
                                 allow_slow_non_contiguous=True).then_inc(small_loaded, 16)
            if "ab" in phases:
                act_ab_small(t)
            t.e.wait_ge(const_ready, t.next(const_ready))
            act_x(t)
            t.e.wait_ge(small_loaded, t.next(small_loaded, 64))
            for ph in phases:
                w = {"ab": 0, "ssm": 1, "mlp0": 2, "mlp1": 3}[ph]
                act_norm(t, w)
                if ph == "ab":
                    act_gates(t)
                    act_ab(t)
                if ph == "ssm":
                    act_steps(t)
                    act_ssm(t)
                if ph[:3] == "mlp":
                    act_mlp(t)
            act_final(t)

        @block.vector
        def _(dve):
            t = Tally(dve)
            for s in range(2):
                t.skip(unit_done[s])
            t.e.wait_ge(const_ready, t.next(const_ready))
            t.e.wait_ge(small_loaded, t.next(small_loaded, 64))
            which = {"ab": 0, "ssm": 1, "mlp0": 2, "mlp1": 3}
            t.e.wait_ge(resid_ready, t.next(resid_ready))
            t.e.sem_inc(x_tile_ready, KD)
            for k in range(KD):
                norm_tile(t, which[phases[0]], k)
            for n, ph in enumerate(phases):
                norm = which[phases[n + 1]] if n + 1 < n_phases else None
                if ph == "ab":
                    dve_gates(t)
                    t.e.wait_ge(rows_kept, t.next(rows_kept, 32))
                    dve_ab(t, norm)
                if ph == "ssm":
                    dve_steps(t)
                    dve_ssm(t, norm)
                if ph[:3] == "mlp":
                    dve_mlp(t, norm)
                t.e.drain().then_inc(resid_ready, 1)
            dve_final(t)


_INS = ["x", "norm_mix_g", "norm_mlp_g", "ab_w_in", "ab_conv_w", "ab_conv_b", "ab_i_bias", "ab_f_bias",
        "ab_mnorm_g", "ab_lam_q1", "ab_lam_k1", "ab_lam_q2", "ab_lam_k2", "ab_dnorm_g", "ab_w_out", "ssm_w_in",
        "ssm_conv_w", "ssm_conv_b", "ssm_dt_bias", "ssm_a_log", "ssm_d", "ssm_norm_g", "ssm_w_out",
        "mlp_w1", "mlp_w2", "final_g"]


def kernel(**inputs):
    import numpy as _np
    import concourse.bacc as _bacc
    from concourse import mybir as _mybir
    from concourse.bass_utils import run_bass_kernel_spmd as _run

    nc = _bacc.Bacc("TRN2", target_bir_lowering=False, num_devices=1)
    arrays, args = {}, []
    for name in _INS:
        a = _np.ascontiguousarray(inputs[name])
        arrays[f"in_{name}_dram"] = a
        args.append(nc.dram_tensor(f"in_{name}_dram", a.shape, _mybir.dt.from_np(a.dtype), kind="ExternalInput").ap())
    args.append(nc.dram_tensor("out_0_dram", (1, T, D), _mybir.dt.float32, kind="ExternalOutput").ap())
    trunk(nc, *args)
    r = _run(nc, [arrays], core_ids=[0])
    return r.results[0]["out_0_dram"]
```
